# Optimizing a Trainium2 kernel written in Bass

```python
import jax, jax.numpy as jnp
from jax import lax
import numpy as np

D_MODEL = 1024
BATCH = 1
SEQ = 512
DEPTH = 2

P_DIM = 256
N_EVEN = (DEPTH + 1) // 2
N_ODD = DEPTH // 2
EPS = 1e-6

A_HEADS = 8
A_HEAD_DIM = 128
A_WIDTH = A_HEADS * A_HEAD_DIM
A_CHUNK = 64
B_HEADS = 16
B_HEAD_DIM = 64
B_WIDTH = B_HEADS * B_HEAD_DIM
B_RANK_W = 64
B_RANK_A = 64
B_LN_EPS = 64e-5
RW_SLAB = 3 * B_WIDTH + B_RANK_W + B_RANK_A
EV_WIDTH = A_WIDTH + B_WIDTH
EV_IN = 3 * A_WIDTH + RW_SLAB + EV_WIDTH
C_HEADS = 8
C_HEAD_DIM = 64
C_WIDTH = C_HEADS * C_HEAD_DIM
C_BLOCK = 256
C_TOPK = 3
C_QCHUNK = 16
D_BLOCKS = 8
D_BLOCK_DIM = 128
D_WIDTH = D_BLOCKS * D_BLOCK_DIM
D_CONV = 4
LRU_C = 8.0
OD_WIDTH = C_WIDTH + D_WIDTH
OD_IN = 3 * C_WIDTH + D_WIDTH + OD_WIDTH

kernel_name = 'hybrid_hgrn2_rwkv7_moba_rglru_trunk'

def _rmsnorm(x, g):
    xf = x.astype(jnp.float32)
    y = xf * lax.rsqrt(jnp.mean(jnp.square(xf), axis=-1, keepdims=True) + EPS)
    return (y * g.astype(jnp.float32)).astype(x.dtype)

def _shift(z):
    return jnp.pad(z, ((0, 0), (1, 0), (0, 0)))[:, :-1]

def _hgrn2(q, f_logit, i, lb):
    bsz, seq, _ = q.shape
    log_f = jnp.logaddexp(jnp.log(lb), jnp.log1p(-lb) + jax.nn.log_sigmoid(f_logit))
    k = -jnp.expm1(log_f)
    q = jax.nn.silu(q)
    nc = seq // A_CHUNK

    def chunks(z):
        return z.reshape(bsz, nc, A_CHUNK, A_HEADS, A_HEAD_DIM).transpose(1, 0, 3, 2, 4)

    causal = jnp.tril(jnp.ones((A_CHUNK, A_CHUNK), dtype=bool))

    def step(state, inp):
        qc, gc, kc, vc = inp
        G = jnp.cumsum(gc, axis=2)
        diff = jnp.where(causal[:, :, None], G[:, :, :, None, :] - G[:, :, None, :, :], -jnp.inf)
        attn = jnp.einsum('bhtk,bhsk,bhtsk->bhts', qc, kc, jnp.exp(diff))
        o = jnp.einsum('bhts,bhsv->bhtv', attn, vc) + jnp.einsum('bhtk,bhkv->bhtv', qc * jnp.exp(G), state)
        g_last = G[:, :, -1:, :]
        state = jnp.exp(g_last[:, :, 0, :, None]) * state + jnp.einsum('bhsk,bhsv->bhkv', kc * jnp.exp(g_last - G), vc)
        return state, o

    s0 = jnp.zeros((bsz, A_HEADS, A_HEAD_DIM, A_HEAD_DIM), q.dtype)
    _, o = lax.scan(step, s0, (chunks(q), chunks(log_f), chunks(k), chunks(i)))
    return o.transpose(1, 0, 3, 2, 4).reshape(bsz, seq, A_HEADS, A_HEAD_DIM)

def _rwkv7(r, k, v, w_lr, a_lr, w0, w2, a0, a2, k_k, k_a, r_k, ln_g, ln_b):
    bsz, seq, _ = r.shape
    hs = (B_HEADS, B_HEAD_DIM)
    heads = lambda z: z.reshape(bsz, seq, B_HEADS, B_HEAD_DIM)
    w = -jax.nn.softplus(-(w0 + jnp.tanh(w_lr) @ w2)) - 0.5
    decay = jnp.exp(-jnp.exp(w))
    a = jax.nn.sigmoid(a0 + a_lr @ a2)
    r, k, v, a, decay = heads(r), heads(k), heads(v), heads(a), heads(decay)
    kk = k * k_k.reshape(hs)
    kk = kk / jnp.maximum(jnp.linalg.norm(kk, axis=-1, keepdims=True), 1e-12)
    k = k * (1.0 + (a - 1.0) * k_a.reshape(hs))

    def step(state, inp):
        rt, wt, kt, vt, kkt, at = inp
        sa = jnp.einsum('bhvk,bhk->bhv', state, -kkt)
        state = state * wt[:, :, None, :] + sa[..., None] * (kkt * at)[:, :, None, :] + vt[..., None] * kt[:, :, None, :]
        return state, jnp.einsum('bhvk,bhk->bhv', state, rt)

    tm = lambda z: jnp.moveaxis(z, 1, 0)
    s0 = jnp.zeros((bsz, B_HEADS, B_HEAD_DIM, B_HEAD_DIM), r.dtype)
    _, y = lax.scan(step, s0, (tm(r), tm(decay), tm(k), tm(v), tm(kk), tm(a)))
    y = jnp.moveaxis(y, 0, 1)
    mu = jnp.mean(y, axis=-1, keepdims=True)
    var = jnp.mean(jnp.square(y - mu), axis=-1, keepdims=True)
    y = (y - mu) * lax.rsqrt(var + B_LN_EPS) * ln_g.reshape(hs) + ln_b.reshape(hs)
    y = y + jnp.sum(r * k * r_k.reshape(hs), axis=-1, keepdims=True) * v
    return y.reshape(bsz, seq, B_WIDTH)

def _moba(q, k, v):
    bsz, seq, _ = q.shape
    nb = -(-seq // C_BLOCK)
    sp = nb * C_BLOCK
    nq = sp // C_QCHUNK
    topk = min(C_TOPK, nb)
    scale = C_HEAD_DIM ** -0.5

    def heads(z):
        z = jnp.pad(z, ((0, 0), (0, sp - seq), (0, 0)))
        return z.reshape(bsz, sp, C_HEADS, C_HEAD_DIM).transpose(0, 2, 1, 3)

    qh, kh, vh = heads(q), heads(k), heads(v)
    kb = kh.reshape(bsz, C_HEADS, nb, C_BLOCK, C_HEAD_DIM)
    vb = vh.reshape(bsz, C_HEADS, nb, C_BLOCK, C_HEAD_DIM)
    qblk = jnp.arange(sp) // C_BLOCK
    gate = jnp.einsum('bhtd,bhnd->bhtn', qh, jnp.mean(kb, axis=3)).astype(jnp.float32)
    gate = jnp.where(jnp.arange(nb)[None, :] < qblk[:, None], gate, -jnp.inf)
    _, idx = lax.top_k(gate, topk)
    valid = idx < qblk[:, None]

    to_chunks = lambda z: jnp.moveaxis(z.reshape(bsz, C_HEADS, nq, C_QCHUNK, z.shape[-1]), 2, 0)
    bi = jnp.arange(bsz)[:, None, None, None]
    hi = jnp.arange(C_HEADS)[None, :, None, None]
    key_off = jnp.arange(C_BLOCK)
    q_off = jnp.arange(C_QCHUNK)

    def attend(args):
        qc, ic, vc_, start = args
        k_sel = kb[bi, hi, ic]
        v_sel = vb[bi, hi, ic]
        blk = start // C_BLOCK
        k_own = lax.dynamic_index_in_dim(kb, blk, axis=2, keepdims=False)
        v_own = lax.dynamic_index_in_dim(vb, blk, axis=2, keepdims=False)
        s_sel = jnp.einsum('bhqd,bhqjkd->bhqjk', qc, k_sel).astype(jnp.float32) * scale
        s_sel = jnp.where(vc_[..., None], s_sel, -jnp.inf).reshape(bsz, C_HEADS, C_QCHUNK, topk * C_BLOCK)
        s_own = jnp.einsum('bhqd,bhkd->bhqk', qc, k_own).astype(jnp.float32) * scale
        causal = (blk * C_BLOCK + key_off)[None, :] <= (start + q_off)[:, None]
        s_own = jnp.where(causal, s_own, -jnp.inf)
        prob = jax.nn.softmax(jnp.concatenate([s_sel, s_own], axis=-1), axis=-1).astype(v.dtype)
        p_sel = prob[..., :topk * C_BLOCK].reshape(bsz, C_HEADS, C_QCHUNK, topk, C_BLOCK)
        p_own = prob[..., topk * C_BLOCK:]
        return jnp.einsum('bhqjk,bhqjkd->bhqd', p_sel, v_sel) + jnp.einsum('bhqk,bhkd->bhqd', p_own, v_own)

    starts = jnp.arange(nq, dtype=jnp.int32) * C_QCHUNK
    o = lax.map(attend, (to_chunks(qh), to_chunks(idx), to_chunks(valid), starts))
    o = o.transpose(1, 2, 0, 3, 4).reshape(bsz, C_HEADS, sp, C_HEAD_DIM)[:, :, :seq]
    return o.transpose(0, 2, 1, 3).reshape(bsz, seq, C_WIDTH)

def _rglru(xr, conv_w, conv_b, wa, ba, wx, bx, lam):
    bsz, seq, _ = xr.shape
    xf = xr.astype(jnp.float32)
    xc = lax.conv_general_dilated(xf, conv_w.astype(jnp.float32)[:, None, :], window_strides=(1,),
                                  padding=[(D_CONV - 1, 0)], dimension_numbers=('NWC', 'WIO', 'NWC'),
                                  feature_group_count=D_WIDTH) + conv_b
    blocks = xc.reshape(bsz, seq, D_BLOCKS, D_BLOCK_DIM)
    r = jax.nn.sigmoid(jnp.einsum('bsnd,nde->bsne', blocks, wa).reshape(bsz, seq, D_WIDTH) + ba)
    i = jax.nn.sigmoid(jnp.einsum('bsnd,nde->bsne', blocks, wx).reshape(bsz, seq, D_WIDTH) + bx)
    log_a = -LRU_C * r * jax.nn.softplus(-lam)
    a = jnp.exp(log_a)
    b = jnp.sqrt(-jnp.expm1(2.0 * log_a)) * (i * xc)

    def combine(lhs, rhs):
        return lhs[0] * rhs[0], rhs[0] * lhs[1] + rhs[1]

    _, h = lax.associative_scan(combine, (a, b), axis=1)
    return h

def _even_layer(x, norm_g, w_in, w_out, lb, hg_norm, mu, w0, w2, a0, a2, k_k, k_a, r_k, ln_g, ln_b):
    bsz, seq, _ = x.shape
    h = _rmsnorm(x, norm_g)
    z = (h @ w_in).astype(jnp.float32)
    za, zb, gate = jnp.split(z, [3 * A_WIDTH, 3 * A_WIDTH + RW_SLAB], axis=-1)
    qa, fa, ia = jnp.split(za, 3, axis=-1)
    zb = zb + (_shift(zb) - zb) * mu
    rb, kb, vb, wlr, alr = jnp.split(zb, [B_WIDTH, 2 * B_WIDTH, 3 * B_WIDTH, 3 * B_WIDTH + B_RANK_W], axis=-1)
    oa = _rmsnorm(_hgrn2(qa, fa, ia, lb), hg_norm.reshape(A_HEADS, A_HEAD_DIM)).reshape(bsz, seq, A_WIDTH)
    ob = _rwkv7(rb, kb, vb, wlr, alr, w0, w2, a0, a2, k_k, k_a, r_k, ln_g, ln_b)
    y = jnp.concatenate([oa, ob], axis=-1) * jax.nn.silu(gate)
    return y.astype(x.dtype) @ w_out

def _odd_layer(x, norm_g, w_in, w_out, conv_w, conv_b, wa, ba, wx, bx, lam):
    h = _rmsnorm(x, norm_g)
    z = h @ w_in
    qc, kc, vc, xd, gate = jnp.split(z, [C_WIDTH, 2 * C_WIDTH, 3 * C_WIDTH, 3 * C_WIDTH + D_WIDTH], axis=-1)
    oc = _moba(qc, kc, vc).astype(jnp.float32)
    od = _rglru(xd, conv_w, conv_b, wa, ba, wx, bx, lam)
    y = jnp.concatenate([oc, od], axis=-1) * jax.nn.silu(gate.astype(jnp.float32))
    return y.astype(x.dtype) @ w_out

def setup_inputs(seed: int = 0) -> dict:
    key = jax.random.key(seed)
    ks = iter(jax.random.split(key, 40))
    nrm = lambda shape, scale: scale * jax.random.normal(next(ks), shape, jnp.float32)
    gain = lambda shape: 1.0 + 0.1 * jax.random.normal(next(ks), shape, jnp.float32)
    uni = lambda shape, lo, hi: jax.random.uniform(next(ks), shape, jnp.float32, lo, hi)
    a8 = uni((N_ODD, D_WIDTH), 0.9, 0.999)
    sig = a8 ** (1.0 / LRU_C)
    lam = jnp.log(sig) - jnp.log1p(-sig)
    return {
        'x': nrm((BATCH, SEQ, D_MODEL), 1.0),
        'p': nrm((DEPTH, BATCH, SEQ, P_DIM), 1.0),
        'ev_norm': gain((N_EVEN, D_MODEL)),
        'ev_w_in': nrm((N_EVEN, D_MODEL, EV_IN), D_MODEL ** -0.5),
        'ev_w_out': nrm((N_EVEN, EV_WIDTH, D_MODEL), EV_WIDTH ** -0.5),
        'hg_lb_logits': 1.0 + nrm((N_EVEN, A_WIDTH), 0.5),
        'hg_norm': gain((N_EVEN, A_WIDTH)),
        'rw_mu': uni((N_EVEN, RW_SLAB), 0.0, 1.0),
        'rw_w0': uni((N_EVEN, B_WIDTH), -6.5, -1.5),
        'rw_w2': nrm((N_EVEN, B_RANK_W, B_WIDTH), 0.5 * B_RANK_W ** -0.5),
        'rw_a0': nrm((N_EVEN, B_WIDTH), 0.1),
        'rw_a2': nrm((N_EVEN, B_RANK_A, B_WIDTH), B_RANK_A ** -0.5),
        'rw_k_k': 0.85 + nrm((N_EVEN, B_WIDTH), 0.05),
        'rw_k_a': 1.0 + nrm((N_EVEN, B_WIDTH), 0.05),
        'rw_r_k': nrm((N_EVEN, B_WIDTH), 0.1),
        'rw_ln_g': gain((N_EVEN, B_WIDTH)),
        'rw_ln_b': nrm((N_EVEN, B_WIDTH), 0.01),
        'od_norm': gain((N_ODD, D_MODEL)),
        'od_w_in': nrm((N_ODD, D_MODEL, OD_IN), D_MODEL ** -0.5),
        'od_w_out': nrm((N_ODD, OD_WIDTH, D_MODEL), OD_WIDTH ** -0.5),
        'lru_conv_w': nrm((N_ODD, D_CONV, D_WIDTH), D_CONV ** -0.5),
        'lru_conv_b': nrm((N_ODD, D_WIDTH), 0.01),
        'lru_wa': nrm((N_ODD, D_BLOCKS, D_BLOCK_DIM, D_BLOCK_DIM), D_BLOCK_DIM ** -0.5),
        'lru_ba': nrm((N_ODD, D_WIDTH), 0.01),
        'lru_wx': nrm((N_ODD, D_BLOCKS, D_BLOCK_DIM, D_BLOCK_DIM), D_BLOCK_DIM ** -0.5),
        'lru_bx': nrm((N_ODD, D_WIDTH), 0.01),
        'lru_lambda': lam,
        'ple_proj': nrm((DEPTH, P_DIM, D_MODEL), P_DIM ** -0.5),
        'ple_gate': nrm((DEPTH, D_MODEL, D_MODEL), D_MODEL ** -0.5),
        'ple_norm': gain((DEPTH, D_MODEL)),
        'final_norm': gain((D_MODEL,)),
    }

def reference(x, p, ev_norm, ev_w_in, ev_w_out, hg_lb_logits, hg_norm, rw_mu, rw_w0, rw_w2, rw_a0, rw_a2,
              rw_k_k, rw_k_a, rw_r_k, rw_ln_g, rw_ln_b, od_norm, od_w_in, od_w_out, lru_conv_w, lru_conv_b,
              lru_wa, lru_ba, lru_wx, lru_bx, lru_lambda, ple_proj, ple_gate, ple_norm, final_norm):
    s = jax.nn.softmax(hg_lb_logits.astype(jnp.float32), axis=0)
    lower_bounds = jnp.maximum(jnp.cumsum(s, axis=0) - s[0], 0.0)
    for i in range(DEPTH):
        j = i // 2
        if i % 2 == 0:
            x = x + _even_layer(x, ev_norm[j], ev_w_in[j], ev_w_out[j], lower_bounds[j], hg_norm[j], rw_mu[j],
                                rw_w0[j], rw_w2[j], rw_a0[j], rw_a2[j], rw_k_k[j], rw_k_a[j], rw_r_k[j],
                                rw_ln_g[j], rw_ln_b[j])
        else:
            x = x + _odd_layer(x, od_norm[j], od_w_in[j], od_w_out[j], lru_conv_w[j], lru_conv_b[j],
                               lru_wa[j], lru_ba[j], lru_wx[j], lru_bx[j], lru_lambda[j])
        x = x + (p[i] @ ple_proj[i]) * jax.nn.sigmoid(_rmsnorm(x, ple_norm[i]) @ ple_gate[i])
    return _rmsnorm(x, final_norm)


_drawn_inputs = setup_inputs


def setup_inputs(seed=0):
    import zlib

    import numpy as np

    out = dict(_drawn_inputs(seed))
    spreads = {}
    factors = {'rw_w2': 8.0,
     'rw_a0': 4.62,
     'rw_k_k': 17.207,
     'rw_k_a': 3.231,
     'rw_ln_b': 8.0,
     'lru_conv_b': 3.638,
     'lru_ba': 64.0,
     'lru_bx': 64.0}
    for name, (base, spread) in spreads.items():
        noise = np.random.default_rng([zlib.crc32(name.encode()), seed]).standard_normal(out[name].shape)
        drawn = base * np.exp(spread * noise) if base else spread * noise
        out[name] = __import__('jax').numpy.asarray(drawn.astype(out[name].dtype))
    for name, factor in factors.items():
        out[name] = (out[name] * factor).astype(out[name].dtype)
    return out
```

```python
from contextlib import ExitStack

import numpy as np
import concourse.bass as bass
from concourse import mybir

F32 = mybir.dt.float32
F32R = mybir.dt.float32r
U8 = mybir.dt.uint8
ALU = mybir.AluOpType
ACT = mybir.ActivationFunctionType

T = 512
D = 1024
P = 128
KC = D // P
CH = 4
L = T // CH
EPS = 1e-6
LN_EPS = 64e-5
KAPPA = float(np.exp(-0.5))
LN2 = float(np.log(2.0))
EV_ROUNDS = 8
OD_ROUNDS = 4
TILES = 8
LEVELS = 7
N_MASK = LEVELS * 2 * P + T + 4 * P + (LEVELS - 1) * P

EV_UNITS = 2 * (TILES * EV_ROUNDS + 1)
U_OUT0 = EV_UNITS
U_PRJ0 = U_OUT0 + 32
U_GAT0 = U_PRJ0 + 4
U_ODD = U_GAT0 + 16
U_OUT1 = U_ODD + 2 * TILES * OD_ROUNDS
U_PRJ1 = U_OUT1 + 24
U_GAT1 = U_PRJ1 + 4
N_UNITS = U_GAT1 + 16
SLOTS = 4

(MU_R, MU_K, MU_V, W0, A0, K_K, K_A, R_K, LN_G, LN_B, LB_LOGIT, HG_G,
 OMU_R, OMU_K, OMU_V, LB, OLB) = range(17)
N_EV, N_EVP = 12, 17
CW0, CW1, CW2, CW3, CONV_B, BA, BX, LAM, CNEG, CPOS = range(10)
N_OD, N_ODP = 8, 10


PER_ROUND = dict(
    w_hi=1, w_ready=1, units_done=1,
    x_added=8, sq_ready=8, sq_used=8, ln_done=1, rstd=1, hn_ready=8, hi_ready=8, h_ready=8,
    p_hi=2, p_ready=2, prj_evac=4, gate_sig=8, gate_mul=8, y_hi=1, y_split=1,
    par_dve=19, par_exp=1, par_lam=4, zeroed=1, masks_set=1, bias_set=4,
    free0=4, free1=4, cur_e=1, cur_r=1, lr_shift=1, lr_ready=1, sig_gb=1, sig_q=1, sig_f=1, fk=2, sig_ga=1, shifted=3,
    hg_lvl=8, hg_even=14, hg_qk=8, hg_masked=8, hg_vt=1, hg_vtok=1, hg_kt=1, hg_ktok=1, hg_kv=1,
    hg_state=3, hg_o=1, hg_sq=1, hg_ssq=1, hg_ln=1, hg_rstd=1, hg_n=1, hg_y=1,
    rw_wx=1, rw_ax=1, rw_sw=1, rw_av=1, rw_ksq=1, rw_ssq=1, rw_prep=5, rw_center=1, rw_rk=1, rw_m1=1, rw_ln=1, rw_rn=1,
    rw_bon=1, rw_bonus=1, rw_exp=3, rw_kk=2, rw_ops=4, rw_rho=1, rw_tr=3, rw_tok=3, rw_reset=1,
    rw_qk=8, rw_nat=2, rw_masked=8, rw_init=2, rw_p=24, rw_pev=24, rw_n=24, rw_x=24,
    rw_rhs=4, rw_rhse=4, rw_u=4, rw_ue=4, rw_st=3, rw_sadd=3, rw_s=3, rw_yc=4,
    rw_ysb=1, rw_mean=1, rw_d=1, rw_dsq=1, rw_var=1, rw_lnv=1, rw_rstd=1, rw_norm=2, rw_y=1,
    ofree0=4, ofree1=4, cur_o=1, o_sig=3, mo_vt=1, mo_vtok=1, mo_s=8, mo_max=8, mo_neg=8, mo_exp=8, mo_inv=8, mo_p=8,
    mo_tr=8, mo_pt=8, mo_pv=8, mo_y=1,
    conv_pad=1, ru_conv=8, ru_r_mm=2, ru_i_mm=2, ru_r=2, ru_i=2, ru_th=2, ru_clamp=2, ru_a=2, ru_u1=2, ru_u2=2, ru_d=2, ru_e=2,
    ru_ix=2, ru_b=2, ru_h=2, ru_y=2,
)


def count(name, r, j=0):
    value = r * PER_ROUND[name] + j + 1
    assert not isinstance(value, int) or value > 0, (name, r, j)
    return value


def trunk(nc, xT, pT, wall, par_e, par_o, gains, w2a2, lru_w, masks, out):
    ctx = ExitStack()
    with ctx:
        def sb(name, shape, dt=F32):
            return ctx.enter_context(nc.sbuf_tensor(name, shape, dt))

        sem = {n: ctx.enter_context(nc.semaphore(n)) for n in PER_ROUND}
        raw_loaded = [ctx.enter_context(nc.semaphore(f"raw_loaded{i}")) for i in range(SLOTS)]
        x_loaded = ctx.enter_context(nc.semaphore("x_loaded"))
        x_again = ctx.enter_context(nc.semaphore("x_again"))
        const_loaded = ctx.enter_context(nc.semaphore("const_loaded"))
        w2_loaded = ctx.enter_context(nc.semaphore("w2_loaded"))
        lru_loaded = ctx.enter_context(nc.semaphore("lru_loaded"))
        p_loaded = ctx.enter_context(nc.semaphore("p_loaded"))
        stored = ctx.enter_context(nc.semaphore("stored"))
        vector_copies = ctx.enter_context(nc.semaphore("vector_copies"))
        splits = ctx.enter_context(nc.semaphore("splits"))

        w_raw = sb("w_raw", [P, SLOTS, 4 * P])
        w_hi = sb("w_hi", [P, SLOTS, 4, P], F32R)
        w_lo = sb("w_lo", [P, SLOTS, 4, P], F32R)
        h_split = sb("h_split", [P, 2 * KC, T], F32R)
        y = sb("y", [P, 2 * KC, T])
        mix = sb("mix", [P, 28800])
        ev = sb("ev", [P, N_EVP, 8])
        od = sb("od", [P, N_ODP, 8])
        gain = sb("gain", [P, 5, KC])
        par_t = sb("par_t", [P, 3, 8])
        mu_lr = sb("mu_lr", [P, 3])
        bias = sb("bias", [P, 5])
        mask8 = sb("mask8", [P, N_MASK], U8)
        fconst = sb("fconst", [P, 4, P])
        ident, ones, bones, causal = (fconst[:, n, :] for n in range(4))
        psum = ctx.enter_context(nc.psum_tensor("psum", [P, 8, T], F32))
        bank = [psum[:, n, :] for n in range(8)]
        H0, H1, R0, R1, R2, R3 = bank[2:8]

        used = [0]

        def place(width):
            at = used[0]
            used[0] += width
            assert used[0] <= 28800, used[0]
            return mix[:, at:at + width]

        x_at = place(KC * T)
        x = x_at.rearrange("p (c t) -> p c t", c=KC)
        rw_m = x_at.rearrange("p (c e s t) -> p c e s t", c=CH, e=2, s=4)
        start = used[0]
        hq, hk, hf, hv, sig_a, sig_b, g_a = (place(T) for _ in range(7))
        qp = place(4 * T).rearrange("p (r t) -> p r t", r=4)
        kr = place(4 * T).rearrange("p (r t) -> p r t", r=4)
        tot = [hf] + [place(T >> (n + 1)) for n in range(7)]
        attn = place(T)
        h_vtok, h_ktok = place(T), place(T)
        h_state = place(3 * P)
        wr, wk, wv, g_b = (place(T) for _ in range(4))
        shift = place(T + 8)
        t1, t2, w_a = (place(T) for _ in range(3))
        cum = place(CH * (L + 1)).rearrange("p (c t) -> p c t", c=CH)
        e_pos = place(CH * (L + 1)).rearrange("p (c t) -> p c t", c=CH)
        e_neg = place(T)
        ar = place(2 * T).rearrange("p (c s t) -> p c s t", c=CH, s=2)
        b_t, k_t, w_bonus = (place(T) for _ in range(3))
        b_tok, k_tok, v_tok = (place(T) for _ in range(3))
        inv = place(CH * T).rearrange("p (c s t) -> p c s t", c=CH, s=4)
        p_full = place(4 * P).rearrange("p (r e t) -> p r e t", r=2, e=2)
        rhs_s = place(2 * P).rearrange("p (r t) -> p r t", r=2)
        u_s = place(2 * P).rearrange("p (r t) -> p r t", r=2)
        w_state = place(2 * 64).rearrange("p (r t) -> p r t", r=2)
        s_sum = place(64)
        e_mid, rho = place(CH), place(CH)
        lr = place(T)
        w2_slot = place(P)
        cur_e, cur_r = place(N_EVP), place(N_EVP)
        used[0] = start
        sq = place(2 * T).rearrange("p (r t) -> p r t", r=2)
        hn = place(2 * T).rearrange("p (r t) -> p r t", r=2)
        rstd_s = place(T)
        sg = place(2 * T).rearrange("p (r t) -> p r t", r=2)
        prj = place(KC * T).rearrange("p (c t) -> p c t", c=KC)
        masks_in = prj.rearrange("p c t -> p (c t)")[:, 0:N_MASK]
        p_raw = place(2 * T).rearrange("p (c t) -> p c t", c=2)
        mq, mk, mv, m_vtok = (place(T) for _ in range(4))
        prob = place(2 * T).rearrange("p (r t) -> p r t", r=2)
        prob_t = place(2 * T).rearrange("p (r t) -> p r t", r=2)
        m_stat = place(3 * 8).rearrange("p (k t) -> p k t", k=3)
        m_sum = place(8)
        og = place(3 * T).rearrange("p (r t) -> p r t", r=3)
        osig = place(T)
        xd = place(2 * (T + 8)).rearrange("p (r t) -> p r t", r=2)
        xc = place(2 * T).rearrange("p (r t) -> p r t", r=2)
        u_r, u_i, u_th, u_1, u_2 = ((place(T), place(T)) for _ in range(5))
        lru_slot = place(4 * P).rearrange("p (k t) -> p k t", k=4)
        cur_o = place(2 * N_ODP).rearrange("p (k b) -> p k b", b=2)

        hg_mask = mask8[:, 0:7 * 256].rearrange("p (l t) -> p l t", l=7)
        diag_mask = mask8[:, 1792:2304]
        m4_mask = mask8[:, 2304:2816].rearrange("p (s t) -> p s t", s=4)
        nat_mask = mask8[:, 2816:3584].rearrange("p (l t) -> p l t", l=6)

        def halves(ap, m):
            v = ap.rearrange("p (b two m) -> p b two m", two=2, m=m)
            return v[:, :, 0, :], v[:, :, 1, :]

        block = ctx.enter_context(nc.Block())

        @block.sync
        def _(sp):
            sp.dma_start(x[:, 0:4, :], xT[:, 0:4, :]).then_inc(x_loaded, 16)
            sp.dma_start(x[:, 4:8, :], xT[:, 4:8, :]).then_inc(x_loaded, 16)
            sp.dma_start(ev[:, 0:N_EV, :], par_e[:, 0:N_EV, :]).then_inc(const_loaded, 16)
            sp.dma_start(od[:, 0:N_OD, :], par_o).then_inc(const_loaded, 16)
            sp.dma_start(gain[:, :, :], gains).then_inc(const_loaded, 16)
            sp.dma_start(mu_lr[:, 0:2], par_e[:, N_EV, 0:2]).then_inc(const_loaded, 16)
            sp.dma_start(masks_in, masks[0]).then_inc(const_loaded, 16)
            sp.dma_start(fconst[:, :, :], masks[1]).then_inc(const_loaded, 16)

            def load_unit(g, slot):
                sp.dma_start(w_raw[:, slot, :], wall[bass.ds(g * SLOTS + slot, 1), :, :]).then_inc(raw_loaded[slot], 16)

            for slot in range(SLOTS):
                load_unit(0, slot)
            with sp.Fori(1, N_UNITS // SLOTS) as g:
                for slot in range(SLOTS):
                    sp.wait_ge(sem["w_ready"], count("w_ready", g * SLOTS + slot - SLOTS))
                    load_unit(g, slot)
            for slot in range(N_UNITS % SLOTS):
                g = N_UNITS // SLOTS
                sp.wait_ge(sem["w_ready"], count("w_ready", (g - 1) * SLOTS + slot))
                load_unit(g, slot)
            for c in range(KC):
                sp.wait_ge(sem["hn_ready"], count("hn_ready", 4, c))
                sp.dma_start(out[:, c, :], prj[:, c, :]).then_inc(stored, 16)
            sp.wait_ge(stored, 16 * KC)

        @block.gpsimd
        def _(pool):
            def split_unit(g, slot, first=False):
                u = g * SLOTS + slot
                pool.wait_ge(raw_loaded[slot], 16 * (g + 1))
                if not first:
                    pool.wait_ge(sem["units_done"], count("units_done", u - SLOTS))
                pool.sem_inc(splits, 1)
                pool.tensor_scalar(w_hi[:, slot, :, :], w_raw[:, slot, :], 1.0, 0.0, ALU.mult, ALU.add).then_inc(sem["w_hi"], 1)
                pool.wait_ge(sem["w_hi"], count("w_hi", u))
                pool.tensor_tensor(w_lo[:, slot, :, :], w_raw[:, slot, :],
                                          w_hi[:, slot, :, :].bitcast(F32).rearrange("p k n -> p (k n)"), ALU.subtract).then_inc(sem["w_ready"], 1)

            for slot in range(SLOTS):
                split_unit(0, slot, first=True)
            with pool.Fori(1, N_UNITS // SLOTS) as g:
                for slot in range(SLOTS):
                    split_unit(g, slot)
            for slot in range(N_UNITS % SLOTS):
                split_unit(N_UNITS // SLOTS, slot)

        @block.tensor
        def _(pe):
            def mm(o, lhsT, rhs, start=True, stop=True):
                return pe.matmul(o, lhsT, rhs, start=start, stop=stop, skip_group_check=True)

            def split_products(o, slot, j, hi, lo, start, stop):
                mm(o, w_hi[:, slot, j, :], hi, start, False)
                mm(o, w_hi[:, slot, j, :], lo, False, False)
                return mm(o, w_lo[:, slot, j, :], hi, False, stop)

            def tile(r, j, unit0, free, first_free):
                o = bank[j % 2][:, :]
                if not first_free:
                    pe.wait_ge(sem[f"{free}{j % 2}"], count(f"{free}{j % 2}", r, j // 2 - 1))
                for half in range(2):
                    slot = (unit0 + 2 * j + half) % SLOTS
                    pe.wait_ge(sem["w_ready"], (r * 2 * TILES) + unit0 + 2 * j + half + 1)
                    for k in range(4):
                        c = 4 * half + k
                        last = split_products(o, slot, k, h_split[:, c, :], h_split[:, KC + c, :], c == 0, c == KC - 1)
                    last.then_inc(sem["units_done"], 1)

            def sumsq(stage, o, c):
                pe.wait_ge(sem["sq_ready"], count("sq_ready", stage, c))
                last = mm(o, ones, sq[:, c % 2, :], c == 0, c == KC - 1)
                last.then_inc(sem["sq_used"], 1)

            pe.wait_ge(const_loaded, 96)
            for c in range(KC):
                sumsq(0, R3[:, :], c)
            pe.wait_ge(sem["h_ready"], count("h_ready", 0, 7))

            def low_rank(r):
                pe.wait_ge(w2_loaded, (r + 1) * 16)
                if isinstance(r, int) and r == 0:
                    pe.wait_ge(sem["lr_ready"], count("lr_ready", 0))
                    pe.wait_ge(sem["zeroed"], count("zeroed", 0))
                else:
                    pe.wait_ge(sem["rw_d"], count("rw_d", r - 1))
                    pe.wait_ge(sem["rw_lnv"], count("rw_lnv", r - 1))
                mm(R0[:, :], w2_slot[0:64, :], lr[0:64, :]).then_inc(sem["rw_wx"], 1)
                mm(R1[:, :], w2_slot[64:128, :], lr[64:128, :]).then_inc(sem["rw_ax"], 1)

            def key_norm(r):
                pe.wait_ge(sem["rw_ksq"], count("rw_ksq", r))
                if not (isinstance(r, int) and r == 0):
                    pe.wait_ge(sem["rw_ysb"], count("rw_ysb", r - 1))
                mm(R2[:, :], bones, t1).then_inc(sem["rw_ssq"], 1)

            def bonus(r):
                pe.wait_ge(sem["rw_rk"], count("rw_rk", r))
                mm(R3[:, :], bones, t2).then_inc(sem["rw_bon"], 1)

            def transposes(r):
                pe.wait_ge(sem["rw_av"], count("rw_av", r))
                for n, (src, o) in enumerate(((b_t, R0), (k_t, R1), (wv, R2))):
                    if n < 2:
                        pe.wait_ge(sem["rw_ops"], count("rw_ops", r, 2 + n))
                    else:
                        pe.wait_ge(sem["rw_m1"], count("rw_m1", r))
                        pe.wait_ge(sem["rw_bonus"], count("rw_bonus", r))
                    for c in range(CH):
                        last = pe.transpose(o[:, c * L:(c + 1) * L], src[:, c * L:(c + 1) * L], ident)
                    last.then_inc(sem["rw_tr"], 1)

            def products(r):
                for e in range(2):
                    rows = slice(64 * e, 64 * e + 64)
                    if e == 0:
                        pe.wait_ge(sem["rw_tok"], count("rw_tok", r, 2))
                    for c in range(CH):
                        last = mm(bank[6 + e][:, c * P:(c + 1) * P], ar[rows, c, 0, :], b_t[rows, c * L:(c + 1) * L])
                    last.then_inc(sem["rw_nat"], 1)
                for c in range(CH):
                    for e in range(2):
                        n = 2 * c + e
                        rows = slice(64 * e, 64 * e + 64)
                        o = bank[4 + n % 2]
                        if n < 2:
                            pe.wait_ge(sem["rw_tok"], count("rw_tok", r, n))
                        else:
                            pe.wait_ge(sem["rw_masked"], count("rw_masked", r, n - 2))
                        both = ar[rows, c, :, :]
                        mm(o[:, 0:256], b_t[rows, c * L:(c + 1) * L], both)
                        mm(o[:, 256:512], k_t[rows, c * L:(c + 1) * L], both).then_inc(sem["rw_qk"], 1)

            def inverse_p(r, lvl, c):
                n, m = (lvl - 1) * CH + c, 1 << lvl
                if lvl == 1:
                    pe.wait_ge(sem["rw_masked"], count("rw_masked", r, 2 * c + 1))
                    pe.wait_ge(sem["rw_init"], count("rw_init", r, 1))
                    pe.wait_ge(sem["rw_masked"], count("rw_masked", r, 7))
                else:
                    pe.wait_ge(sem["rw_x"], count("rw_x", r, n - CH))
                if n >= 2:
                    pe.wait_ge(sem["rw_pev"], count("rw_pev", r, n - 2))
                for e in range(2):
                    even, _ = halves(inv[:, c, e, :], m)
                    last = mm(bank[4 + c % 2][:, e * 64:e * 64 + 64], rw_m[:, c, e, 0, :], even)
                last.then_inc(sem["rw_p"], 1)

            def inverse_n(r, lvl, c):
                n, m = (lvl - 1) * CH + c, 1 << lvl
                pe.wait_ge(sem["rw_pev"], count("rw_pev", r, n))
                if n >= 2:
                    pe.wait_ge(sem["rw_x"], count("rw_x", r, n - 2))
                else:
                    pe.wait_ge(sem["rw_init"], count("rw_init", r, 1))
                o = bank[6 + c % 2]
                for e in range(2):
                    even, _ = halves(p_full[:, c % 2, e, :], m)
                    _, odd = halves(inv[:, c, 2 + e, :], m)
                    if lvl < 6:
                        mm(o[:, e * 64:e * 64 + 64], inv[:, c, 2 + e, :], even)
                        last = mm(o[:, P + e * 64:P + e * 64 + 64], p_full[:, c % 2, e, :], odd)
                    else:
                        last = mm(o[0:64, e * 64:e * 64 + 64], p_full[:, c % 2, e, 0:64], odd)
                last.then_inc(sem["rw_n"], 1)

            def inverse(r, lvl):
                for step in ((inverse_p, 0), (inverse_p, 1), (inverse_n, 0), (inverse_p, 2),
                             (inverse_n, 1), (inverse_p, 3), (inverse_n, 2), (inverse_n, 3)):
                    step[0](r, lvl, step[1])

            def chain(r, c):
                if c == 0:
                    pe.wait_ge(sem["rw_pev"], count("rw_pev", r, 23))
                    pe.wait_ge(sem["rw_x"], count("rw_x", r, 23))
                else:
                    pe.wait_ge(sem["rw_ue"], count("rw_ue", r, c - 1))
                heads = [(e, slice(64 * e, 64 * e + 64)) for e in range(2)]
                if c:
                    pe.wait_ge(sem["rw_s"], count("rw_s", r, c - 1))
                for e, rows in heads:
                    at = slice(c * L + 64 * e, c * L + 64 * e + 64)
                    o = bank[4 + e][:, 0:64]
                    last = mm(o, rw_m[:, c, e, 2, :], v_tok[:, at], True, c == 0)
                    if c:
                        last = mm(o, ar[rows, c, 0, :], w_state[rows, c % 2, :], False, True)
                last.then_inc(sem["rw_rhs"], 1)
                pe.wait_ge(sem["rw_rhse"], count("rw_rhse", r, c))
                for e, rows in heads:
                    last = mm(R0[:, 64 + 64 * e:128 + 64 * e], inv[:, c, 2 + e, :], rhs_s[:, c % 2, rows])
                last.then_inc(sem["rw_u"], 1)
                pe.wait_ge(sem["rw_ue"], count("rw_ue", r, c))
                if c < CH - 1:
                    if c:
                        pe.wait_ge(sem["rw_s"], count("rw_s", r, c - 1))
                    for e, rows in heads:
                        at = slice(c * L + 64 * e, c * L + 64 * e + 64)
                        mm(R3[rows, 0:64], k_tok[:, at], v_tok[:, at], True, False)
                        last = mm(R3[rows, 0:64], b_tok[:, at], u_s[:, c % 2, rows], False, True)
                    last.then_inc(sem["rw_st"], 1)
                for e, rows in heads:
                    at = slice(c * L + 64 * e, c * L + 64 * e + 64)
                    o = R2[rows, c * L:(c + 1) * L]
                    mm(o, v_tok[:, at], rw_m[:, c, e, 3, :], True, False)
                    last = mm(o, u_s[:, c % 2, rows], rw_m[:, c, e, 1, :], False, c == 0)
                    if c:
                        last = mm(o, w_state[rows, c % 2, :], ar[rows, c, 1, :], False, True)
                last.then_inc(sem["rw_yc"], 1)

            def head_norm(r):
                pe.wait_ge(sem["rw_ysb"], count("rw_ysb", r))
                mm(R0[:, :], bones, b_t).then_inc(sem["rw_mean"], 1)
                pe.wait_ge(sem["rw_dsq"], count("rw_dsq", r))
                mm(R1[:, :], bones, k_t).then_inc(sem["rw_var"], 1)

            def hg_values(r):
                pe.wait_ge(sem["free0"], count("free0", r, 2))
                if not (isinstance(r, int) and r == 0):
                    pe.wait_ge(sem["hg_ln"], count("hg_ln", r - 1))
                for c in range(CH):
                    last = pe.transpose(H0[:, c * L:(c + 1) * L], hv[:, c * L:(c + 1) * L], ident)
                last.then_inc(sem["hg_vt"], 1)

            def hg_level(r, lvl):
                o = bank[2 + lvl % 2]
                pe.wait_ge(sem["hg_lvl"], count("hg_lvl", r, lvl))
                if lvl:
                    pe.wait_ge(sem["hg_even"], count("hg_even", r, 2 * lvl - 1))
                if lvl == 0:
                    pe.wait_ge(sem["hg_vtok"], count("hg_vtok", r))
                elif lvl == 1:
                    if not (isinstance(r, int) and r == 0):
                        pe.wait_ge(sem["hg_n"], count("hg_n", r - 1))
                else:
                    pe.wait_ge(sem["hg_masked"], count("hg_masked", r, lvl - 2))
                keys = hk if lvl == 0 else kr[:, lvl % 4, :]
                for c in range(CH):
                    _, odd = halves(qp[:, lvl % 4, c * L:(c + 1) * L], 1 << lvl)
                    last = mm(o[:, c * 64:c * 64 + 64], keys[:, c * L:(c + 1) * L], odd)
                last.then_inc(sem["hg_qk"], 1)

            def hg_diagonal(r):
                pe.wait_ge(sem["hg_masked"], count("hg_masked", r, 5))
                for c in range(CH):
                    last = mm(H1[:, c * L:(c + 1) * L], hk[:, c * L:(c + 1) * L], hq[:, c * L:(c + 1) * L])
                last.then_inc(sem["hg_qk"], 1)

            def hg_states(r):
                pe.wait_ge(sem["hg_lvl"], count("hg_lvl", r, 7))
                pe.wait_ge(sem["hg_even"], count("hg_even", r, 13))
                pe.wait_ge(sem["hg_masked"], count("hg_masked", r, 6))
                for c in range(CH - 1):
                    last = pe.transpose(H0[:, c * L:(c + 1) * L], kr[:, 3, c * L:(c + 1) * L], ident)
                last.then_inc(sem["hg_kt"], 1)
                pe.wait_ge(sem["hg_ktok"], count("hg_ktok", r))
                for c in range(CH - 1):
                    last = mm(H0[:, c * L:(c + 1) * L], h_ktok[:, c * L:(c + 1) * L], h_vtok[:, c * L:(c + 1) * L])
                last.then_inc(sem["hg_kv"], 1)

            def hg_outputs(r):
                pe.wait_ge(sem["hg_masked"], count("hg_masked", r, 7))
                for c in range(CH):
                    at = slice(c * L, (c + 1) * L)
                    if c == 0 and not (isinstance(r, int) and r == 0):
                        pe.wait_ge(sem["hg_n"], count("hg_n", r - 1))
                    last = mm(H1[:, at], h_vtok[:, at], attn[:, at], True, c == 0)
                    if c:
                        pe.wait_ge(sem["hg_state"], count("hg_state", r, c - 1))
                        last = mm(H1[:, at], h_state[:, (c - 1) * P:c * P], qp[:, 3, at], False, True)
                last.then_inc(sem["hg_o"], 1)

            def hg_norm(r):
                pe.wait_ge(sem["hg_sq"], count("hg_sq", r))
                mm(H0[:, :], ones, hk).then_inc(sem["hg_ssq"], 1)

            def even_round(i, head=True, pair=True):
                r = i - 1
                first = isinstance(i, int) and i == 0

                def t(j):
                    tile(i, j, 0, "free", first and j < 2)

                t(0)
                if pair:
                    low_rank(r)
                if head:
                    t(1)
                if pair:
                    key_norm(r)
                    bonus(r)
                if head:
                    t(2)
                    t(3)
                    t(4)
                if pair:
                    transposes(r)
                    products(r)
                    for lvl in range(1, 7):
                        inverse(r, lvl)
                    chain(r, 0)
                if head:
                    t(5)
                    hg_values(i)
                    hg_level(i, 0)
                    hg_level(i, 1)
                if pair:
                    chain(r, 1)
                if head:
                    t(6)
                    hg_level(i, 2)
                    hg_level(i, 3)
                if pair:
                    chain(r, 2)
                if head:
                    t(7)
                    hg_level(i, 4)
                    hg_level(i, 5)
                if pair:
                    chain(r, 3)
                if head:
                    hg_level(i, 6)
                    hg_diagonal(i)
                    hg_states(i)
                if pair:
                    head_norm(r)
                if head:
                    hg_outputs(i)
                    hg_norm(i)

            even_round(0, pair=False)
            even_round(1)
            with pe.Fori(2, EV_ROUNDS) as i:
                even_round(i)
            even_round(EV_ROUNDS, head=False)

            def out_projection(unit0, n_chunks, y_from):
                for c in range(n_chunks):
                    ring = c % 6
                    pe.wait_ge(sem["y_split"], count("y_split", 0, y_from + c))
                    for half in range(2):
                        u = unit0 + 2 * c + half
                        pe.wait_ge(sem["w_ready"], count("w_ready", u))
                        for k in range(4):
                            last = split_products(bank[4 * half + k][:, :], u % SLOTS, k, h_split[:, ring, :],
                                                  h_split[:, KC + ring, :], c == 0, c == n_chunks - 1)
                        last.then_inc(sem["units_done"], 1)

            def ple(stage, unit_p, unit_g):
                layer = stage // 2
                pe.wait_ge(sem["p_ready"], count("p_ready", layer, 1))
                pe.wait_ge(sem["x_added"], count("x_added", stage - 1, 0))
                for n in range(KC):
                    sumsq(stage, bank[0][:, :], n)
                    pe.wait_ge(sem["x_added"], count("x_added", stage - 1, 1 + n % 7))
                    if n == 7:
                        pe.wait_ge(sem["prj_evac"], count("prj_evac", layer, 0))
                    u = unit_p + n // 2
                    pe.wait_ge(sem["w_ready"], count("w_ready", u))
                    for c in range(2):
                        last = split_products(bank[1 + n % 7][:, :], u % SLOTS, 2 * (n % 2) + c, h_split[:, 6 + c, :],
                                              h_split[:, KC + 6 + c, :], c == 0, c == 1)
                    if n % 2:
                        last.then_inc(sem["units_done"], 1)
                pe.wait_ge(sem["prj_evac"], count("prj_evac", layer, 3))
                for c in range(KC):
                    pe.wait_ge(sem["h_ready"], count("h_ready", stage, c))
                    for half in range(2):
                        u = unit_g + 2 * c + half
                        pe.wait_ge(sem["w_ready"], count("w_ready", u))
                        for k in range(4):
                            last = split_products(bank[4 * half + k][:, :], u % SLOTS, k, h_split[:, c, :],
                                                  h_split[:, KC + c, :], c == 0, c == KC - 1)
                        last.then_inc(sem["units_done"], 1)

            pe.wait_ge(sem["free0"], count("free0", EV_ROUNDS, 0))
            pe.wait_ge(sem["free1"], count("free1", EV_ROUNDS - 1, 3))
            pe.wait_ge(sem["hg_n"], count("hg_n", EV_ROUNDS - 1))
            pe.wait_ge(sem["rw_d"], count("rw_d", EV_ROUNDS - 1))
            pe.wait_ge(sem["rw_lnv"], count("rw_lnv", EV_ROUNDS - 1))
            out_projection(U_OUT0, 2 * KC, 0)
            ple(1, U_PRJ0, U_GAT0)
            pe.wait_ge(sem["x_added"], count("x_added", 1, 0))
            for c in range(KC):
                sumsq(2, bank[0][:, :], c)
            pe.wait_ge(sem["h_ready"], count("h_ready", 2, 7))

            def mo_values(r):
                pe.wait_ge(sem["ofree0"], count("ofree0", r, 1))
                if not (isinstance(r, int) and r == 0):
                    pe.wait_ge(sem["mo_pt"], count("mo_pt", r - 1, 7))
                for c in range(CH):
                    last = pe.transpose(bank[4][:, c * L:(c + 1) * L], mv[:, c * L:(c + 1) * L], ident)
                last.then_inc(sem["mo_vt"], 1)

            def mo_scores(r, n):
                e, qt = divmod(n, CH)
                rows = slice(64 * e, 64 * e + 64)
                o = bank[2 + n % 2]
                if n >= 2:
                    pe.wait_ge(sem["mo_exp"], count("mo_exp", r, n - 2))
                elif not (isinstance(r, int) and r == 0):
                    pe.wait_ge(sem["mo_exp"], count("mo_exp", r - 1, 6 + n))
                pe.wait_ge(sem["ofree1"], count("ofree1", r, 0))
                mm(o[:, 0:(qt + 1) * L], mq[rows, qt * L:(qt + 1) * L], mk[rows, 0:(qt + 1) * L], True, False)
                mm(o[:, qt * L:(qt + 1) * L], ident, causal, False, True).then_inc(sem["mo_s"], 1)

            def mo_transposes(r, n):
                qt = n % CH
                pe.wait_ge(sem["mo_p"], count("mo_p", r, n))
                if n:
                    pe.wait_ge(sem["mo_pt"], count("mo_pt", r, n - 1))
                else:
                    pe.wait_ge(sem["mo_vtok"], count("mo_vtok", r))
                for j in range(qt + 1):
                    last = pe.transpose(bank[4][:, j * L:(j + 1) * L], prob[:, n % 2, j * L:(j + 1) * L], ident)
                last.then_inc(sem["mo_tr"], 1)

            def mo_output(r, n):
                e, qt = divmod(n, CH)
                rows = slice(64 * e, 64 * e + 64)
                pe.wait_ge(sem["mo_pt"], count("mo_pt", r, n))
                if n == 0 and not (isinstance(r, int) and r == 0):
                    pe.wait_ge(sem["mo_y"], count("mo_y", r - 1))
                for j in range(qt + 1):
                    last = mm(bank[5][rows, qt * L:(qt + 1) * L], m_vtok[:, j * L + 64 * e:j * L + 64 * e + 64],
                              prob_t[:, n % 2, j * L:(j + 1) * L], j == 0, j == qt)
                last.then_inc(sem["mo_pv"], 1)

            def ru_gates(r, b):
                pe.wait_ge(sem["ru_conv"], count("ru_conv", r, 4 * b + 3))
                if b == 0:
                    pe.wait_ge(lru_loaded, (r + 1) * 16)
                    if not (isinstance(r, int) and r == 0):
                        pe.wait_ge(sem["ru_i"], count("ru_i", r - 1, 1))
                else:
                    pe.wait_ge(sem["ru_i"], count("ru_i", r, 0))
                mm(bank[6][:, :], lru_slot[:, 2 * b, :], xc[:, b, :]).then_inc(sem["ru_r_mm"], 1)
                mm(bank[7][:, :], lru_slot[:, 2 * b + 1, :], xc[:, b, :]).then_inc(sem["ru_i_mm"], 1)

            def odd_round(i):
                first = isinstance(i, int) and i == 0

                def t(j):
                    tile(i, j, U_ODD, "ofree", first and j < 2)

                def attend(n):
                    if n + 1 < 2 * CH:
                        mo_scores(i, n + 1)
                    mo_transposes(i, n)
                    mo_output(i, n)

                t(0)
                t(1)
                t(2)
                mo_scores(i, 0)
                mo_values(i)
                attend(0)
                attend(1)
                t(3)
                attend(2)
                attend(3)
                t(4)
                attend(4)
                t(5)
                attend(5)
                t(6)
                attend(6)
                attend(7)
                ru_gates(i, 0)
                ru_gates(i, 1)
                t(7)

            odd_round(0)
            with pe.Fori(1, OD_ROUNDS) as i:
                odd_round(i)

            pe.wait_ge(sem["ofree1"], count("ofree1", OD_ROUNDS - 1, 3))
            pe.wait_ge(sem["mo_y"], count("mo_y", OD_ROUNDS - 1))
            pe.wait_ge(sem["ru_i"], count("ru_i", OD_ROUNDS - 1, 1))
            out_projection(U_OUT1, 4 + KC, 2 * KC)
            ple(3, U_PRJ1, U_GAT1)
            pe.wait_ge(sem["x_added"], count("x_added", 3, 0))
            for c in range(KC):
                sumsq(4, bank[0][:, :], c)

        @block.scalar
        def _(act):
            def f(o, i, func, bias=0.0, scale=1.0, **kw):
                return act.activation(o, i, func, bias=bias, scale=scale, **kw)

            def tile_done(r, j, unit0=0):
                act.wait_ge(sem["units_done"], r * 2 * TILES + unit0 + 2 * j + 2)

            def is_first(r):
                return isinstance(r, int) and r == 0

            def squares(stage, c):
                if stage:
                    act.wait_ge(sem["x_added"], count("x_added", stage - 1, c))
                if c >= 2:
                    act.wait_ge(sem["sq_used"], count("sq_used", stage, c - 2))
                f(sq[:, c % 2, :], x[:, c, :], ACT.Square).then_inc(sem["sq_ready"], 1)

            def root(stage, o):
                act.wait_ge(sem["sq_used"], count("sq_used", stage, 7))
                f(rstd_s, o, ACT.Ln, bias=bias[:, 0:1], scale=1.0 / D).then_inc(sem["ln_done"], 1)
                act.wait_ge(sem["ln_done"], count("ln_done", stage))
                f(rstd_s, rstd_s, ACT.Exp, scale=-0.5).then_inc(sem["rstd"], 1)

            def high_halves(stage):
                for c in range(KC):
                    act.wait_ge(sem["hn_ready"], count("hn_ready", stage, c))
                    f(h_split[:, c, :], hn[:, c % 2, :], ACT.Copy).then_inc(sem["hi_ready"], 1)

            act.dma_start(w2_slot, w2a2[0]).then_inc(w2_loaded, 16)
            act.wait_ge(x_loaded, 32)
            act.wait_ge(sem["bias_set"], count("bias_set", 0, 3))
            for c in range(KC):
                squares(0, c)
            root(0, R3[:, :])
            high_halves(0)

            act.wait_ge(sem["par_dve"], count("par_dve", 0, 3))
            f(ev[:, LB, :], par_t[:, 0, :], ACT.Exp).then_inc(sem["par_exp"], 1)
            act.wait_ge(sem["par_dve"], count("par_dve", 0, 10))
            f(par_t[:, 2, :], par_t[:, 1, :], ACT.Exp, scale=-1.0).then_inc(sem["par_lam"], 1)
            act.wait_ge(sem["par_lam"], count("par_lam", 0, 0))
            f(par_t[:, 2, :], par_t[:, 2, :], ACT.Ln, bias=bias[:, 3:4]).then_inc(sem["par_lam"], 1)

            def level_copies(r, lvl):
                m = 1 << (lvl - 1)
                act.wait_ge(sem["hg_lvl"], count("hg_lvl", r, lvl - 1))
                if lvl >= 2:
                    act.wait_ge(sem["hg_even"], count("hg_even", r, 2 * lvl - 3))
                if lvl >= 4:
                    act.wait_ge(sem["hg_qk"], count("hg_qk", r, lvl - 4))
                elif lvl == 3 and not is_first(r):
                    act.wait_ge(sem["hg_kt"], count("hg_kt", r - 1))
                keys = hk if lvl == 1 else kr[:, (lvl - 1) % 4, :]
                f(halves(qp[:, lvl % 4, :], m)[0], halves(qp[:, (lvl - 1) % 4, :], m)[0], ACT.Copy).then_inc(sem["hg_even"], 1)
                f(halves(kr[:, lvl % 4, :], m)[1], halves(keys, m)[1], ACT.Copy).then_inc(sem["hg_even"], 1)

            def shifted(i, n, j):
                tile_done(i, j)
                if n == 0:
                    if is_first(i):
                        act.wait_ge(sem["free0"], count("free0", 0, 0))
                    else:
                        act.wait_ge(sem["free1"], count("free1", i - 1, 3))
                    act.wait_ge(sem["cur_e"], count("cur_e", i))
                else:
                    act.wait_ge(sem[f"free{(j - 1) % 2}"], count(f"free{(j - 1) % 2}", i, (j - 1) // 2))
                f(shift[:, 1:T + 1], bank[j % 2][:, :], ACT.Copy, scale=cur_e[:, MU_R + n:MU_R + n + 1]).then_inc(sem["shifted"], 1)

            def inverse(r, lvl):
                for c in range(CH):
                    n = (lvl - 1) * CH + c
                    act.wait_ge(sem["rw_p"], count("rw_p", r, n))
                    if n >= 2:
                        act.wait_ge(sem["rw_n"], count("rw_n", r, n - 2))
                    elif not is_first(r):
                        act.wait_ge(sem["rw_n"], count("rw_n", r - 1, 22 + n))
                    o = bank[4 + c % 2]
                    if lvl < 6:
                        m = 1 << lvl
                        even, _ = halves(p_full[:, c % 2, :, :].rearrange("p e t -> p (e t)"), m)
                        src = o[:, 0:P].rearrange("p (b m) -> p b m", m=m)
                    else:
                        even = p_full[:, c % 2, :, 0:64]
                        src = o[:, 0:P].rearrange("p (e t) -> p e t", e=2)
                    f(even, src, ACT.Copy).then_inc(sem["rw_pev"], 1)

            def chain(r, c):
                act.wait_ge(sem["rw_rhs"], count("rw_rhs", r, c))
                f(rhs_s[:, c % 2, :].rearrange("p (e t) -> p e t", e=2), psum[:, 4:6, 0:64], ACT.Copy).then_inc(sem["rw_rhse"], 1)
                act.wait_ge(sem["rw_u"], count("rw_u", r, c))
                if c < 2 and not is_first(r):
                    act.wait_ge(sem["rw_yc"], count("rw_yc", r - 1, 3))
                elif c >= 2:
                    act.wait_ge(sem["rw_yc"], count("rw_yc", r, c - 2))
                f(u_s[:, c % 2, :], R0[:, 64:192], ACT.Copy).then_inc(sem["rw_ue"], 1)

            def even_round(i, head=True, pair=True):
                r = i - 1
                tile_done(i, 0)
                if is_first(i):
                    act.wait_ge(sem["zeroed"], count("zeroed", 0))
                    f(shift[:, 1:T + 1], bank[0][:, :], ACT.Copy, scale=mu_lr[:, 0:1]).then_inc(sem["lr_shift"], 1)
                    act.wait_ge(sem["free0"], count("free0", 0, 0))
                    f(lr[0:64, :], lr[0:64, :], ACT.Tanh).then_inc(sem["lr_ready"], 1)
                else:
                    act.wait_ge(sem["free1"], count("free1", i - 1, 1))
                    f(sig_a, bank[0][:, :], ACT.Sigmoid).then_inc(sem["sig_gb"], 1)
                if pair:
                    act.wait_ge(sem["cur_r"], count("cur_r", r))
                    act.wait_ge(sem["rw_wx"], count("rw_wx", r))
                    f(e_neg, R0[:, :], ACT.Sigmoid, bias=cur_r[:, W0:W0 + 1]).then_inc(sem["rw_sw"], 1)
                    act.wait_ge(sem["rw_ax"], count("rw_ax", r))
                    f(w_a, R1[:, :], ACT.Sigmoid, bias=cur_r[:, A0:A0 + 1]).then_inc(sem["rw_av"], 1)
                    if head:
                        act.dma_start(w2_slot, w2a2[bass.ds(i, 1), :, :]).then_inc(w2_loaded, 16)
                    f(t1, wk, ACT.Square, scale=cur_r[:, K_K:K_K + 1]).then_inc(sem["rw_ksq"], 1)
                if head:
                    tile_done(i, 1)
                    f(sig_b, bank[1][:, :], ACT.Sigmoid).then_inc(sem["sig_q"], 1)
                    tile_done(i, 2)
                    if is_first(i):
                        act.wait_ge(sem["free1"], count("free1", 0, 0))
                    else:
                        act.wait_ge(sem["free0"], count("free0", i, 0))
                    f(sig_a, bank[0][:, :], ACT.Sigmoid).then_inc(sem["sig_f"], 1)
                    act.wait_ge(sem["free1"], count("free1", i, 0))
                    f(sig_b, bank[0][:, :], ACT.Sigmoid, scale=-1.0).then_inc(sem["free0"], 1)
                    tile_done(i, 3)
                    act.wait_ge(sem["fk"], count("fk", i, 0))
                    f(sig_a, bank[1][:, :], ACT.Sigmoid).then_inc(sem["sig_ga"], 1)
                if pair:
                    act.wait_ge(sem["rw_center"], count("rw_center", r))
                    f(e_pos, cum, ACT.Exp, scale=-KAPPA).then_inc(sem["rw_exp"], 1)
                    f(e_neg, cum[:, :, 1:L + 1], ACT.Exp, scale=KAPPA).then_inc(sem["rw_exp"], 1)
                    f(e_mid, e_mid, ACT.Exp, scale=-KAPPA).then_inc(sem["rw_exp"], 1)
                    act.wait_ge(sem["rw_m1"], count("rw_m1", r))
                    f(t1, t1, ACT.Ln).then_inc(sem["rw_ln"], 1)
                    act.wait_ge(sem["rw_ln"], count("rw_ln", r))
                    f(t1, t1, ACT.Exp, bias=bias[:, 2:3], scale=-0.5).then_inc(sem["rw_rn"], 1)
                if head:
                    tile_done(i, 4)
                    if not is_first(i):
                        act.wait_ge(sem["hg_vt"], count("hg_vt", i - 1))
                    f(hv, bank[0][:, :], ACT.Copy).then_inc(sem["free0"], 1)
                if pair:
                    if not is_first(r):
                        act.wait_ge(sem["rw_u"], count("rw_u", r - 1, 3))
                    f(inv.rearrange("p c s t -> p (c s) t"), fconst[:, 0:1, :].to_broadcast([P, 16, P]), ACT.Copy).then_inc(sem["rw_reset"], 1)
                    for n, (dst, src) in enumerate(((b_tok, R0), (k_tok, R1), (v_tok, R2))):
                        act.wait_ge(sem["rw_tr"], count("rw_tr", r, n))
                        f(dst, src[:, :], ACT.Copy).then_inc(sem["rw_tok"], 1)
                    for lvl in range(1, 7):
                        inverse(r, lvl)
                    chain(r, 0)
                if head:
                    shifted(i, 0, 5)
                    act.wait_ge(sem["hg_vt"], count("hg_vt", i))
                    f(h_vtok, H0[:, :], ACT.Copy).then_inc(sem["hg_vtok"], 1)
                    level_copies(i, 1)
                    level_copies(i, 2)
                if pair:
                    chain(r, 1)
                if head:
                    shifted(i, 1, 6)
                    level_copies(i, 3)
                    level_copies(i, 4)
                if pair:
                    chain(r, 2)
                if head:
                    shifted(i, 2, 7)
                    level_copies(i, 5)
                    level_copies(i, 6)
                if pair:
                    chain(r, 3)
                    if not head:
                        act.wait_ge(sem["rw_yc"], count("rw_yc", r, 3))
                        act.dma_start(x, xT).then_inc(x_again, 16)
                if head:
                    level_copies(i, 7)
                    act.wait_ge(sem["hg_kt"], count("hg_kt", i))
                    f(h_ktok[:, 0:3 * L], H0[:, 0:3 * L], ACT.Copy).then_inc(sem["hg_ktok"], 1)
                if pair:
                    act.wait_ge(sem["rw_yc"], count("rw_yc", r, 3))
                    f(b_t, R2[:, :], ACT.Copy).then_inc(sem["rw_ysb"], 1)
                    act.wait_ge(sem["rw_d"], count("rw_d", r))
                    f(k_t, b_t, ACT.Square).then_inc(sem["rw_dsq"], 1)
                    act.wait_ge(sem["rw_var"], count("rw_var", r))
                    f(t1, R1[:, :], ACT.Ln, bias=bias[:, 1:2], scale=1.0 / 64).then_inc(sem["rw_lnv"], 1)
                    act.wait_ge(sem["rw_lnv"], count("rw_lnv", r))
                    f(t1, t1, ACT.Exp, scale=-0.5).then_inc(sem["rw_rstd"], 1)
                if head:
                    act.wait_ge(sem["hg_o"], count("hg_o", i))
                    f(hk, H1[:, :], ACT.Square).then_inc(sem["hg_sq"], 1)
                    act.wait_ge(sem["hg_ssq"], count("hg_ssq", i))
                    f(sig_b, H0[:, :], ACT.Ln, bias=bias[:, 0:1], scale=1.0 / P).then_inc(sem["hg_ln"], 1)
                    act.wait_ge(sem["hg_ln"], count("hg_ln", i))
                    f(sig_b, sig_b, ACT.Exp, scale=-0.5).then_inc(sem["hg_rstd"], 1)

            even_round(0, pair=False)
            even_round(1)
            with act.Fori(2, EV_ROUNDS) as i:
                even_round(i)
            even_round(EV_ROUNDS, head=False)

            def split_outputs(unit0, n_chunks, y_from, units_before):
                for c in range(n_chunks):
                    act.wait_ge(sem["units_done"], units_before if c < 6 else unit0 + 2 * (c - 5))
                    if y_from == 0 and c == n_chunks - 1:
                        act.wait_ge(sem["rw_y"], count("rw_y", EV_ROUNDS - 1))
                    elif y_from == 0 and c == 0:
                        act.wait_ge(sem["hg_y"], count("hg_y", EV_ROUNDS - 1))
                    elif y_from and c == 0:
                        act.wait_ge(sem["ru_y"], count("ru_y", OD_ROUNDS - 1, 1))
                    f(h_split[:, c % 6, :], y[:, c, :], ACT.Copy).then_inc(sem["y_hi"], 1)

            def split_embedding(layer, units_before):
                act.wait_ge(p_loaded, 16 * (layer + 1))
                act.wait_ge(sem["units_done"], units_before)
                for c in range(2):
                    f(h_split[:, 6 + c, :], p_raw[:, c, :], ACT.Copy).then_inc(sem["p_hi"], 1)

            def ple(stage, unit_p, unit_g):
                layer = stage // 2
                for c in range(KC):
                    squares(stage, c)
                root(stage, bank[0][:, :])
                for m in range(4):
                    act.wait_ge(sem["sq_used"], count("sq_used", stage, 7))
                    act.wait_ge(sem["units_done"], unit_p + m + 1)
                    for n in (2 * m, 2 * m + 1):
                        last = f(prj[:, n, :], bank[1 + n % 7][:, :], ACT.Copy)
                    last.then_inc(sem["prj_evac"], 1)
                high_halves(stage)
                act.wait_ge(sem["units_done"], unit_g + 16)
                for n in range(KC):
                    if n >= 2:
                        act.wait_ge(sem["gate_mul"], count("gate_mul", stage // 2, n - 2))
                    f(sg[:, n % 2, :], bank[n][:, :], ACT.Sigmoid).then_inc(sem["gate_sig"], 1)

            act.dma_start(p_raw, pT[0]).then_inc(p_loaded, 16)
            split_embedding(0, EV_UNITS)
            split_outputs(U_OUT0, 2 * KC, 0, EV_UNITS)
            ple(1, U_PRJ0, U_GAT0)
            for c in range(KC):
                squares(2, c)
            root(2, bank[0][:, :])
            high_halves(2)

            def attend(i, n):
                qt = n % CH
                w = (qt + 1) * L
                act.wait_ge(sem["mo_neg"], count("mo_neg", i, n))
                if n >= 2:
                    act.wait_ge(sem["mo_tr"], count("mo_tr", i, n - 2))
                f(prob[:, n % 2, 0:w], bank[2 + n % 2][:, 0:w], ACT.Exp, bias=m_stat[:, 1, n:n + 1], scale=0.125,
                         accum_out=m_sum[:, n:n + 1]).then_inc(sem["mo_exp"], 1)
                act.wait_ge(sem["mo_tr"], count("mo_tr", i, n))
                if n >= 2:
                    act.wait_ge(sem["mo_pv"], count("mo_pv", i, n - 2))
                f(prob_t[:, n % 2, 0:w], bank[4][:, 0:w], ACT.Copy).then_inc(sem["mo_pt"], 1)

            def odd_round(i):
                act.wait_ge(sem["cur_o"], count("cur_o", i))
                if not is_first(i):
                    act.wait_ge(sem["ru_i_mm"], count("ru_i_mm", i - 1, 1))
                act.dma_start(lru_slot, lru_w[i] if isinstance(i, int) else lru_w[bass.ds(i, 1), :, :, :]).then_inc(lru_loaded, 16)
                for j, dst, free in ((0, mq, "ofree0"), (1, mk, "ofree1"), (2, mv, "ofree0")):
                    tile_done(i, j, U_ODD)
                    f(dst, bank[j % 2][:, :], ACT.Copy).then_inc(sem[free], 1)
                act.wait_ge(sem["mo_vt"], count("mo_vt", i))
                f(m_vtok, bank[4][:, :], ACT.Copy).then_inc(sem["mo_vtok"], 1)
                attend(i, 0)
                attend(i, 1)
                tile_done(i, 3, U_ODD)
                f(xd[:, 0, 3:T + 3], bank[1][:, :], ACT.Copy).then_inc(sem["ofree1"], 1)
                attend(i, 2)
                attend(i, 3)
                tile_done(i, 4, U_ODD)
                f(xd[:, 1, 3:T + 3], bank[0][:, :], ACT.Copy).then_inc(sem["ofree0"], 1)
                for n in range(4, 8):
                    attend(i, n)
                for n, j in ((0, 5), (1, 6)):
                    tile_done(i, j, U_ODD)
                    if n:
                        act.wait_ge(sem["ofree1"], count("ofree1", i, 2))
                    elif not is_first(i):
                        act.wait_ge(sem["ofree1"], count("ofree1", i - 1, 3))
                    f(osig, bank[j % 2][:, :], ACT.Sigmoid).then_inc(sem["o_sig"], 1)
                for b in range(2):
                    act.wait_ge(sem["ru_r_mm"], count("ru_r_mm", i, b))
                    f(u_r[b], bank[6][:, :], ACT.Sigmoid, bias=cur_o[:, BA, b:b + 1]).then_inc(sem["ru_r"], 1)
                    act.wait_ge(sem["ru_i_mm"], count("ru_i_mm", i, b))
                    f(u_i[b], bank[7][:, :], ACT.Sigmoid, bias=cur_o[:, BX, b:b + 1]).then_inc(sem["ru_i"], 1)
                    act.wait_ge(sem["ru_r"], count("ru_r", i, b))
                    f(u_th[b], u_r[b], ACT.Tanh, scale=cur_o[:, CPOS, b:b + 1]).then_inc(sem["ru_th"], 1)
                tile_done(i, 7, U_ODD)
                act.wait_ge(sem["ofree0"], count("ofree0", i, 3))
                f(osig, bank[1][:, :], ACT.Sigmoid).then_inc(sem["o_sig"], 1)
                for b in range(2):
                    act.wait_ge(sem["ru_th"], count("ru_th", i, b))
                    f(u_r[b], u_r[b], ACT.Exp, scale=cur_o[:, CNEG, b:b + 1]).then_inc(sem["ru_a"], 1)
                    f(u_1[b], u_th[b], ACT.Ln, bias=bias[:, 3:4]).then_inc(sem["ru_u1"], 1)
                    act.wait_ge(sem["ru_clamp"], count("ru_clamp", i, b))
                    f(u_2[b], u_2[b], ACT.Ln).then_inc(sem["ru_u2"], 1)
                    act.wait_ge(sem["ru_d"], count("ru_d", i, b))
                    f(u_2[b], u_2[b], ACT.Exp, bias=bias[:, 4:5], scale=0.5).then_inc(sem["ru_e"], 1)

            odd_round(0)
            with act.Fori(1, OD_ROUNDS) as i:
                odd_round(i)
            act.wait_ge(sem["gate_mul"], count("gate_mul", 0, 7))
            act.dma_start(p_raw, pT[1]).then_inc(p_loaded, 16)
            split_embedding(1, U_OUT1)
            split_outputs(U_OUT1, 4 + KC, 2 * KC, U_OUT1)
            ple(3, U_PRJ1, U_GAT1)
            for c in range(KC):
                squares(4, c)
            root(4, bank[0][:, :])

        @block.vector
        def _(dve):
            def is_first(r):
                return isinstance(r, int) and r == 0

            def tile_done(r, j, unit0=0):
                dve.wait_ge(sem["units_done"], r * 2 * TILES + unit0 + 2 * j + 2)

            def stt(o, a, scalar, b, op0, op1):
                return dve.scalar_tensor_tensor(out=o, in0=a, scalar=scalar, in1=b, op0=op0, op1=op1)

            def low_half(stage, c):
                dve.wait_ge(sem["hi_ready"], count("hi_ready", stage, c))
                dve.tensor_tensor(h_split[:, KC + c, :], hn[:, c % 2, :], h_split[:, c, :].bitcast(F32), ALU.subtract).then_inc(sem["h_ready"], 1)

            def normed(stage, g, dst):
                dve.wait_ge(sem["rstd"], count("rstd", stage))
                for c in range(KC):
                    if dst is hn and c >= 2:
                        dve.wait_ge(sem["h_ready"], count("h_ready", stage, c - 2))
                    o = hn[:, c % 2, :] if dst is hn else dst[:, c, :]
                    stt(o, x[:, c, :], gain[:, g, c:c + 1], rstd_s, ALU.mult, ALU.mult).then_inc(sem["hn_ready"], 1)
                    if dst is hn and c >= 1:
                        low_half(stage, c - 1)
                if dst is hn:
                    low_half(stage, KC - 1)

            for n, v in enumerate((EPS, LN_EPS, 20 * LN2, 1.0, -20 * LN2)):
                ins = dve.memset(bias[:, n:n + 1], v)
                if n:
                    ins.then_inc(sem["bias_set"], 1)
            dve.wait_ge(const_loaded, 96)
            dve.wait_ge(x_loaded, 32)
            normed(0, 0, hn)

            dve.tensor_scalar(ev[:, OMU_R:OMU_V + 1, :], ev[:, MU_R:MU_V + 1, :], -1.0, 1.0, ALU.mult, ALU.add).then_inc(sem["par_dve"], 1)
            dve.tensor_scalar(mu_lr[:, 2:3], mu_lr[:, 0:1], -1.0, 1.0, ALU.mult, ALU.add).then_inc(sem["par_dve"], 1)
            dve.memset(par_t[:, 1, :], 0.0).then_inc(sem["par_dve"], 1)
            dve.tensor_tensor(par_t[:, 0, :], ev[:, LB_LOGIT, :], ev[:, LB_LOGIT, :], ALU.subtract).then_inc(sem["par_dve"], 1)
            dve.wait_ge(sem["par_exp"], count("par_exp", 0))
            dve.reciprocal(par_t[:, 0, :], ev[:, LB, :]).then_inc(sem["par_dve"], 1)
            dve.wait_ge(sem["par_dve"], count("par_dve", 0, 4))
            dve.tensor_tensor(par_t[:, 0, :], par_t[:, 0, :], ev[:, LB, :], ALU.mult).then_inc(sem["par_dve"], 1)
            dve.wait_ge(sem["par_dve"], count("par_dve", 0, 5))
            dve.tensor_tensor(par_t[:, 0, :], par_t[:, 0, :], par_t[:, 0, :], ALU.subtract).then_inc(sem["par_dve"], 1)
            dve.wait_ge(sem["par_dve"], count("par_dve", 0, 6))
            dve.tensor_scalar(ev[:, LB, :], par_t[:, 0, :], 0.0, None, ALU.max).then_inc(sem["par_dve"], 1)
            dve.wait_ge(sem["par_dve"], count("par_dve", 0, 7))
            dve.tensor_scalar(ev[:, OLB, :], ev[:, LB, :], -1.0, 1.0, ALU.mult, ALU.add).then_inc(sem["par_dve"], 1)
            dve.tensor_scalar(par_t[:, 0, :], od[:, LAM, :], -1.0, None, ALU.mult).then_inc(sem["par_dve"], 1)
            dve.wait_ge(sem["par_dve"], count("par_dve", 0, 9))
            dve.tensor_tensor(par_t[:, 1, :], par_t[:, 0, :], od[:, LAM, :], ALU.max).then_inc(sem["par_dve"], 1)
            dve.tensor_scalar(par_t[:, 0, :], par_t[:, 0, :], 0.0, None, ALU.max).then_inc(sem["par_dve"], 1)
            dve.wait_ge(sem["par_lam"], count("par_lam", 0, 1))
            dve.wait_ge(sem["par_dve"], count("par_dve", 0, 11))
            dve.tensor_tensor(par_t[:, 0, :], par_t[:, 0, :], par_t[:, 2, :], ALU.add).then_inc(sem["par_dve"], 1)
            dve.wait_ge(sem["par_dve"], count("par_dve", 0, 12))
            dve.tensor_scalar(od[:, CNEG, :], par_t[:, 0, :], -8.0, None, ALU.mult).then_inc(sem["par_dve"], 1)
            dve.tensor_scalar(od[:, CPOS, :], par_t[:, 0, :], 8.0, None, ALU.mult).then_inc(sem["par_dve"], 1)
            dve.wait_ge(sem["sq_ready"], count("sq_ready", 0, 7))
            dve.memset(attn, 0.0).then_inc(sem["par_dve"], 1)
            dve.memset(p_full, 0.0).then_inc(sem["par_dve"], 1)
            dve.memset(shift[:, 0:1], 0.0).then_inc(sem["par_dve"], 1)
            dve.wait_ge(sem["par_dve"], count("par_dve", 0, 17))
            dve.memset(cum[:, :, 0:1], 0.0).then_inc(sem["par_dve"], 1)
            dve.tensor_copy(mask8[:, :], masks_in).then_inc(sem["masks_set"], 1)
            dve.memset(rw_m, 0.0).then_inc(sem["zeroed"], 1)
            dve.wait_ge(sem["zeroed"], count("zeroed", 0))

            def masked_copy(dst, mask, src):
                dve.sem_inc(vector_copies, 1)
                return dve.copy_predicated(dst, mask, src)

            def gated(i, j, ready, sig, dst):
                dve.wait_ge(sem[ready], count(ready, i - 1 if j == 0 else i))
                dve.tensor_tensor(dst, bank[j % 2][:, :], sig, ALU.mult).then_inc(sem[f"free{j % 2}"], 1)

            def mixed(i, n, j, dst):
                dve.wait_ge(sem["shifted"], count("shifted", i, n))
                if n == 2 and not is_first(i):
                    dve.wait_ge(sem["rw_tr"], count("rw_tr", i - 1, 2))
                stt(dst, bank[j % 2][:, :], cur_e[:, OMU_R + n:OMU_R + n + 1], shift[:, 0:T], ALU.mult, ALU.add).then_inc(sem[f"free{j % 2}"], 1)

            def level(r, lvl):
                if lvl == 0:
                    dve.wait_ge(sem["fk"], count("fk", r, 1))
                    if not is_first(r):
                        dve.wait_ge(sem["hg_sq"], count("hg_sq", r - 1))
                    dve.tensor_tensor(qp[:, 0, :], hq, hf, ALU.mult).then_inc(sem["hg_lvl"], 1)
                    return
                m = 1 << (lvl - 1)
                keys = hk if lvl == 1 else kr[:, (lvl - 1) % 4, :]
                dve.wait_ge(sem["hg_lvl"], count("hg_lvl", r, lvl - 1))
                if lvl >= 2:
                    dve.wait_ge(sem["hg_even"], count("hg_even", r, 2 * lvl - 3))
                if lvl >= 4:
                    dve.wait_ge(sem["hg_qk"], count("hg_qk", r, lvl - 4))
                t_even, t_odd = halves(tot[lvl - 1], 1)
                nb = T // (2 * m)
                q_dst, k_dst = halves(qp[:, lvl % 4, :], m)[1], halves(kr[:, lvl % 4, :], m)[0]
                q_src, k_src = halves(qp[:, (lvl - 1) % 4, :], m)[1], halves(keys, m)[0]
                dve.tensor_tensor(q_dst, q_src, t_even.to_broadcast([P, nb, m]), ALU.mult)
                dve.tensor_tensor(k_dst, k_src, t_odd.to_broadcast([P, nb, m]), ALU.mult)
                dve.tensor_tensor(tot[lvl].rearrange("p (b m) -> p b m", m=1), t_even, t_odd, ALU.mult).then_inc(sem["hg_lvl"], 1)

            def masked(r, lvl):
                dve.wait_ge(sem["hg_qk"], count("hg_qk", r, lvl))
                if lvl:
                    dve.wait_ge(sem["hg_masked"], count("hg_masked", r, lvl - 1))
                if lvl < 7:
                    m = 1 << lvl
                    _, dst = halves(attn, m)
                    mask = hg_mask[:, lvl, :].rearrange("p (b m) -> p b m", m=m)
                    src = bank[2 + lvl % 2][:, 0:256].rearrange("p (b m) -> p b m", m=m)
                    masked_copy(dst, mask, src).then_inc(sem["hg_masked"], 1)
                else:
                    masked_copy(attn, diag_mask, H1[:, :]).then_inc(sem["hg_masked"], 1)

            def states(r):
                dve.wait_ge(sem["hg_kv"], count("hg_kv", r))
                dve.tensor_copy(h_state[:, 0:P], H0[:, 0:P]).then_inc(sem["hg_state"], 1)
                for c in range(1, CH - 1):
                    dve.wait_ge(sem["hg_state"], count("hg_state", r, c - 1))
                    stt(h_state[:, c * P:(c + 1) * P], h_state[:, (c - 1) * P:c * P], tot[7][:, c:c + 1],
                               H0[:, c * P:(c + 1) * P], ALU.mult, ALU.add).then_inc(sem["hg_state"], 1)

            def head_out(r):
                dve.wait_ge(sem["hg_rstd"], count("hg_rstd", r))
                stt(sig_b, H1[:, :], cur_e[:, HG_G:HG_G + 1], sig_b, ALU.mult, ALU.mult).then_inc(sem["hg_n"], 1)
                dve.wait_ge(sem["hg_n"], count("hg_n", r))
                dve.tensor_tensor(y[:, r, :] if isinstance(r, int) else y[:, bass.ds(r, 1), :].rearrange("p a t -> p (a t)"),
                                         sig_b, g_a, ALU.mult).then_inc(sem["hg_y"], 1)

            def decay_sums(r):
                dve.wait_ge(sem["rw_sw"], count("rw_sw", r))
                if not is_first(r):
                    dve.wait_ge(sem["rw_rho"], count("rw_rho", r - 1))
                dve.memset(cum[:, :, 0:1], 0.0).then_inc(sem["rw_prep"], 1)
                for c in range(CH):
                    last = dve.tensor_tensor_scan(out=cum[:, c, 1:L + 1], data0=ones, data1=e_neg[:, c * L:(c + 1) * L],
                                                  initial=0.0, op0=ALU.mult, op1=ALU.add)
                last.then_inc(sem["rw_prep"], 1)
                dve.wait_ge(sem["rw_prep"], count("rw_prep", r, 1))
                dve.tensor_copy(e_mid, cum[:, :, L // 2]).then_inc(sem["rw_prep"], 1)
                dve.wait_ge(sem["rw_prep"], count("rw_prep", r, 2))
                dve.tensor_tensor(cum, cum, e_mid.unsqueeze(2).to_broadcast([P, CH, L + 1]), ALU.subtract).then_inc(sem["rw_center"], 1)
                dve.wait_ge(sem["rw_av"], count("rw_av", r))
                dve.tensor_scalar(t2, w_a, 1.0, cur_r[:, K_A:K_A + 1], ALU.subtract, ALU.mult).then_inc(sem["rw_prep"], 1)
                dve.wait_ge(sem["rw_prep"], count("rw_prep", r, 3))
                stt(k_t, t2, 1.0, wk, ALU.add, ALU.mult).then_inc(sem["rw_prep"], 1)
                dve.wait_ge(sem["rw_prep"], count("rw_prep", r, 4))
                stt(t2, wr, cur_r[:, R_K:R_K + 1], k_t, ALU.mult, ALU.mult).then_inc(sem["rw_rk"], 1)

            def key_norm(r):
                dve.wait_ge(sem["rw_ssq"], count("rw_ssq", r))
                dve.tensor_scalar(t1, R2[:, :], 1e-24, float(2 ** 40), ALU.max, ALU.mult).then_inc(sem["rw_m1"], 1)
                dve.wait_ge(sem["rw_bon"], count("rw_bon", r))
                dve.tensor_tensor(w_bonus, R3[:, :], wv, ALU.mult).then_inc(sem["rw_bonus"], 1)

            def operands(r):
                chunks = lambda ap: ap.rearrange("p (c t) -> p c t", c=CH)
                dve.wait_ge(sem["rw_rn"], count("rw_rn", r))
                stt(t1, wk, cur_r[:, K_K:K_K + 1], t1, ALU.mult, ALU.mult).then_inc(sem["rw_kk"], 1)
                dve.wait_ge(sem["rw_kk"], count("rw_kk", r, 0))
                dve.tensor_tensor(b_t, t1, w_a, ALU.mult).then_inc(sem["rw_kk"], 1)
                dve.wait_ge(sem["rw_kk"], count("rw_kk", r, 1))
                dve.wait_ge(sem["rw_exp"], count("rw_exp", r, 2))
                stt(ar[:, :, 0, :], chunks(t1), -1.0, e_pos[:, :, 0:L], ALU.mult, ALU.mult).then_inc(sem["rw_ops"], 1)
                dve.tensor_tensor(ar[:, :, 1, :], chunks(wr), e_pos[:, :, 1:L + 1], ALU.mult).then_inc(sem["rw_ops"], 1)
                dve.tensor_tensor(b_t, b_t, e_neg, ALU.mult).then_inc(sem["rw_ops"], 1)
                dve.tensor_tensor(k_t, k_t, e_neg, ALU.mult).then_inc(sem["rw_ops"], 1)
                dve.tensor_tensor(rho[:, 0:3], e_pos[:, 0:3, L], e_mid[:, 1:4], ALU.mult).then_inc(sem["rw_rho"], 1)

            def matrices(r):
                dve.wait_ge(sem["rw_reset"], count("rw_reset", r))
                for e in range(2):
                    dve.wait_ge(sem["rw_nat"], count("rw_nat", r, e))
                    even = lambda ap: ap.rearrange("p c (b two) -> p c b two", two=2)[:, :, :, 0]
                    masked_copy(even(inv[:, :, e, :]), nat_mask[:, 0, 0:64].unsqueeze(1).to_broadcast([P, CH, 64]),
                                       even(bank[6 + e].rearrange("p (c t) -> p c t", c=CH))).then_inc(sem["rw_init"], 1)
                for c in range(CH):
                    for e in range(2):
                        n = 2 * c + e
                        o = bank[4 + n % 2]
                        dve.wait_ge(sem["rw_qk"], count("rw_qk", r, n))
                        masked_copy(rw_m[:, c, e, :, :], m4_mask, o[:, :].rearrange("p (s t) -> p s t", s=4))
                        masked_copy(halves(inv[:, c, 2 + e, :], 1)[1],
                                                   hg_mask[:, 0, 0:64].rearrange("p (b m) -> p b m", m=1),
                                                   halves(o[:, 0:P], 1)[1]).then_inc(sem["rw_masked"], 1)

            def inverse(r, lvl):
                m = 1 << lvl
                for c in range(CH):
                    n = (lvl - 1) * CH + c
                    o = bank[6 + c % 2]
                    dve.wait_ge(sem["rw_n"], count("rw_n", r, n))
                    if lvl < 6:
                        blocks = lambda ap: ap.rearrange("p (b m) -> p b m", m=m)
                        masked_copy(halves(inv[:, c, 0:2, :].rearrange("p e t -> p (e t)"), m)[0],
                                            blocks(nat_mask[:, lvl, :]), blocks(o[:, 0:P]))
                        masked_copy(halves(inv[:, c, 2:4, :].rearrange("p e t -> p (e t)"), m)[1],
                                                   blocks(hg_mask[:, lvl, 0:P]), blocks(o[:, P:2 * P])).then_inc(sem["rw_x"], 1)
                    else:
                        dve.tensor_copy(inv[0:64, c, 2:4, 64:P], o[0:64, 0:P].rearrange("p (e t) -> p e t", e=2)).then_inc(sem["rw_x"], 1)

            def state(r, c):
                dve.wait_ge(sem["rw_st"], count("rw_st", r, c))
                if c == 0:
                    if not is_first(r):
                        dve.wait_ge(sem["rw_yc"], count("rw_yc", r - 1, 3))
                    dve.tensor_copy(w_state[:, 0, :], R3[:, 0:64]).then_inc(sem["rw_sadd"], 1)
                else:
                    dve.wait_ge(sem["rw_s"], count("rw_s", r, c - 1))
                    if c == 2:
                        dve.wait_ge(sem["rw_yc"], count("rw_yc", r, 1))
                    dve.tensor_tensor(s_sum, R3[:, 0:64], w_state[:, c % 2, :], ALU.add).then_inc(sem["rw_sadd"], 1)
                dve.wait_ge(sem["rw_sadd"], count("rw_sadd", r, c))
                src = w_state[:, 0, :] if c == 0 else s_sum
                dve.tensor_scalar(w_state[:, (c + 1) % 2, :], src, rho[:, c:c + 1], None, ALU.mult).then_inc(sem["rw_s"], 1)

            def pair_out(r):
                dve.wait_ge(sem["rw_mean"], count("rw_mean", r))
                stt(b_t, R0[:, :], -1.0 / 64, b_t, ALU.mult, ALU.add).then_inc(sem["rw_d"], 1)
                dve.wait_ge(sem["rw_rstd"], count("rw_rstd", r))
                dve.tensor_tensor(b_t, b_t, t1, ALU.mult).then_inc(sem["rw_norm"], 1)
                dve.wait_ge(sem["rw_norm"], count("rw_norm", r, 0))
                stt(b_t, b_t, cur_r[:, LN_G:LN_G + 1], w_bonus, ALU.mult, ALU.add).then_inc(sem["rw_norm"], 1)
                dve.wait_ge(sem["rw_norm"], count("rw_norm", r, 1))
                stt(y[:, KC + r, :] if isinstance(r, int) else y[:, bass.ds(r + KC, 1), :].rearrange("p a t -> p (a t)"),
                           b_t, cur_r[:, LN_B:LN_B + 1], g_b, ALU.add, ALU.mult).then_inc(sem["rw_y"], 1)

            def even_round(i, head=True, pair=True):
                r = i - 1
                if pair:
                    if not is_first(r):
                        dve.wait_ge(sem["rw_y"], count("rw_y", r - 1))
                    dve.tensor_copy(cur_r, ev[:, :, r] if isinstance(r, int) else ev[:, :, bass.ds(r, 1)].rearrange("p k a -> p (k a)")).then_inc(sem["cur_r"], 1)
                if head:
                    if not is_first(i):
                        dve.wait_ge(sem["hg_y"], count("hg_y", i - 1))
                    dve.tensor_copy(cur_e, ev[:, :, i] if isinstance(i, int) else ev[:, :, bass.ds(i, 1)].rearrange("p k a -> p (k a)")).then_inc(sem["cur_e"], 1)
                    dve.wait_ge(sem["cur_e"], count("cur_e", i))
                if is_first(i):
                    dve.wait_ge(sem["lr_shift"], count("lr_shift", 0))
                    stt(lr, bank[0][:, :], mu_lr[:, 2:3], shift[:, 0:T], ALU.mult, ALU.add).then_inc(sem["free0"], 1)
                else:
                    gated(i, 0, "sig_gb", sig_a, g_b)
                if pair:
                    decay_sums(r)
                if head:
                    gated(i, 1, "sig_q", sig_b, hq)
                if pair:
                    key_norm(r)
                if head:
                    dve.wait_ge(sem["free0"], count("free0", i, 1))
                    if not is_first(i):
                        dve.wait_ge(sem["hg_sq"], count("hg_sq", i - 1))
                        dve.wait_ge(sem["hg_ssq"], count("hg_ssq", i - 1))
                    dve.tensor_scalar(hf, sig_a, cur_e[:, OLB:OLB + 1], cur_e[:, LB:LB + 1], ALU.mult, ALU.add).then_inc(sem["fk"], 1)
                    dve.tensor_scalar(hk, sig_b, cur_e[:, OLB:OLB + 1], None, ALU.mult).then_inc(sem["fk"], 1)
                    gated(i, 3, "sig_ga", sig_a, g_a)
                if pair:
                    operands(r)
                if head:
                    level(i, 0)
                    level(i, 1)
                if pair:
                    matrices(r)
                    for lvl in range(1, 7):
                        inverse(r, lvl)
                    state(r, 0)
                if head:
                    mixed(i, 0, 5, wr)
                    masked(i, 0)
                    masked(i, 1)
                    level(i, 2)
                    level(i, 3)
                if pair:
                    state(r, 1)
                if head:
                    mixed(i, 1, 6, wk)
                    masked(i, 2)
                    masked(i, 3)
                    level(i, 4)
                    level(i, 5)
                if pair:
                    state(r, 2)
                if head:
                    mixed(i, 2, 7, wv)
                    masked(i, 4)
                    masked(i, 5)
                    level(i, 6)
                    masked(i, 6)
                    level(i, 7)
                    masked(i, 7)
                    states(i)
                if pair:
                    pair_out(r)
                if head:
                    head_out(i)

            even_round(0, pair=False)
            even_round(1)
            with dve.Fori(2, EV_ROUNDS) as i:
                even_round(i)
            even_round(EV_ROUNDS, head=False)

            def split_outputs(n_chunks, y_from):
                for c in range(n_chunks):
                    dve.wait_ge(sem["y_hi"], count("y_hi", 0, y_from + c))
                    dve.tensor_tensor(h_split[:, KC + c % 6, :], y[:, c, :], h_split[:, c % 6, :].bitcast(F32), ALU.subtract).then_inc(sem["y_split"], 1)

            def split_embedding(layer):
                for c in range(2):
                    dve.wait_ge(sem["p_hi"], count("p_hi", layer, c))
                    dve.tensor_tensor(h_split[:, KC + 6 + c, :], p_raw[:, c, :], h_split[:, 6 + c, :].bitcast(F32),
                                             ALU.subtract).then_inc(sem["p_ready"], 1)

            def add_outputs(stage, unit_end):
                dve.wait_ge(sem["units_done"], unit_end)
                for n in range(KC):
                    dve.tensor_tensor(x[:, n, :], x[:, n, :], bank[n][:, :], ALU.add).then_inc(sem["x_added"], 1)

            def ple(stage, g):
                normed(stage, g, hn)
                for n in range(KC):
                    dve.wait_ge(sem["gate_sig"], count("gate_sig", stage // 2, n))
                    dve.tensor_tensor(prj[:, n, :], prj[:, n, :], sg[:, n % 2, :], ALU.mult).then_inc(sem["gate_mul"], 1)
                    dve.wait_ge(sem["gate_mul"], count("gate_mul", stage // 2, n))
                    dve.tensor_tensor(x[:, n, :], x[:, n, :], prj[:, n, :], ALU.add).then_inc(sem["x_added"], 1)

            split_embedding(0)
            split_outputs(2 * KC, 0)
            dve.wait_ge(x_again, 16)
            add_outputs(0, U_PRJ0)
            ple(1, 1)
            normed(2, 2, hn)
            dve.memset(xd[:, :, 0:3], 0.0).then_inc(sem["conv_pad"], 1)

            def attend(i, n):
                w = (n % CH + 1) * L
                dve.wait_ge(sem["mo_s"], count("mo_s", i, n))
                dve.reduce_max(m_stat[:, 0, n:n + 1], bank[2 + n % 2][:, 0:w], axis=mybir.AxisListType.X).then_inc(sem["mo_max"], 1)
                dve.wait_ge(sem["mo_max"], count("mo_max", i, n))
                dve.tensor_scalar(m_stat[:, 1, n:n + 1], m_stat[:, 0, n:n + 1], -0.125, None, ALU.mult).then_inc(sem["mo_neg"], 1)

            def normalise(i, n):
                w = (n % CH + 1) * L
                dve.wait_ge(sem["mo_exp"], count("mo_exp", i, n))
                dve.reciprocal(m_stat[:, 2, n:n + 1], m_sum[:, n:n + 1]).then_inc(sem["mo_inv"], 1)
                dve.wait_ge(sem["mo_inv"], count("mo_inv", i, n))
                dve.tensor_scalar(prob[:, n % 2, 0:w], prob[:, n % 2, 0:w], m_stat[:, 2, n:n + 1], None, ALU.mult).then_inc(sem["mo_p"], 1)

            def convolve(i, b):
                dve.wait_ge(sem["conv_pad"], count("conv_pad", 0))
                free = ("ofree1", 1) if b == 0 else ("ofree0", 2)
                dve.wait_ge(sem[free[0]], count(free[0], i, free[1]))
                if not is_first(i):
                    dve.wait_ge(sem["ru_ix"], count("ru_ix", i - 1, b))
                dve.tensor_scalar(xc[:, b, :], xd[:, b, 0:T], cur_o[:, CW0, b:b + 1], cur_o[:, CONV_B, b:b + 1], ALU.mult, ALU.add).then_inc(sem["ru_conv"], 1)
                for k in range(1, 4):
                    dve.wait_ge(sem["ru_conv"], count("ru_conv", i, 4 * b + k - 1))
                    stt(xc[:, b, :], xd[:, b, k:k + T], cur_o[:, CW0 + k, b:b + 1], xc[:, b, :], ALU.mult, ALU.add).then_inc(sem["ru_conv"], 1)

            def gate(i, n, j):
                dve.wait_ge(sem["o_sig"], count("o_sig", i, n))
                dve.tensor_tensor(og[:, n, :], bank[j % 2][:, :], osig, ALU.mult).then_inc(sem[f"ofree{j % 2}"], 1)

            def row(base, r, step=1):
                return y[:, base + r * step, :] if isinstance(r, int) else y[:, bass.ds(r * step + base, 1), :].rearrange("p a t -> p (a t)")

            def odd_round(i):
                if not is_first(i):
                    dve.wait_ge(sem["ru_y"], count("ru_y", i - 1, 1))
                dve.tensor_copy(cur_o, od[:, :, bass.ds(i * 2, 2)]).then_inc(sem["cur_o"], 1)
                dve.wait_ge(sem["cur_o"], count("cur_o", i))
                attend(i, 0)
                attend(i, 1)
                normalise(i, 0)
                attend(i, 2)
                normalise(i, 1)
                attend(i, 3)
                convolve(i, 0)
                normalise(i, 2)
                attend(i, 4)
                normalise(i, 3)
                attend(i, 5)
                convolve(i, 1)
                normalise(i, 4)
                attend(i, 6)
                normalise(i, 5)
                attend(i, 7)
                normalise(i, 6)
                normalise(i, 7)
                gate(i, 0, 5)
                gate(i, 1, 6)
                dve.wait_ge(sem["mo_pv"], count("mo_pv", i, 7))
                dve.wait_ge(sem["ofree1"], count("ofree1", i, 2))
                dve.tensor_tensor(row(0, i), bank[5][:, :], og[:, 0, :], ALU.mult).then_inc(sem["mo_y"], 1)
                for b in range(2):
                    dve.wait_ge(sem["ru_i"], count("ru_i", i, b))
                    dve.tensor_tensor(u_i[b], u_i[b], xc[:, b, :], ALU.mult).then_inc(sem["ru_ix"], 1)
                    dve.wait_ge(sem["ru_th"], count("ru_th", i, b))
                    dve.tensor_scalar(u_2[b], u_th[b], float(2.0 ** -103), float(2.0 ** 41), ALU.max, ALU.mult).then_inc(sem["ru_clamp"], 1)
                gate(i, 2, 7)
                for b in range(2):
                    dve.wait_ge(sem["ru_u2"], count("ru_u2", i, b))
                    dve.tensor_tensor(u_2[b], u_2[b], u_1[b], ALU.subtract).then_inc(sem["ru_d"], 1)
                for b in range(2):
                    dve.wait_ge(sem["ru_e"], count("ru_e", i, b))
                    dve.tensor_tensor(u_2[b], u_2[b], u_i[b], ALU.mult).then_inc(sem["ru_b"], 1)
                    dve.wait_ge(sem["ru_b"], count("ru_b", i, b))
                    dve.tensor_tensor_scan(out=u_th[b], data0=u_r[b], data1=u_2[b], initial=0.0, op0=ALU.mult, op1=ALU.add).then_inc(sem["ru_h"], 1)
                    dve.wait_ge(sem["ru_h"], count("ru_h", i, b))
                    dve.wait_ge(sem["ofree0" if b == 0 else "ofree1"], count("ofree0" if b == 0 else "ofree1", i, 3))
                    dve.tensor_tensor(row(4 + b, i, 2), u_th[b], og[:, 1 + b, :], ALU.mult).then_inc(sem["ru_y"], 1)

            odd_round(0)
            with dve.Fori(1, OD_ROUNDS) as i:
                odd_round(i)
            split_embedding(1)
            split_outputs(4 + KC, 2 * KC)
            add_outputs(2, U_PRJ1)
            ple(3, 3)
            normed(4, 4, prj)


def kernel(**inputs):
    import concourse.bacc as bacc
    from concourse.bass_utils import run_bass_kernel_spmd as run

    a = {n: np.asarray(v) for n, v in inputs.items()}

    def units(w):
        k, n = w.shape
        return w.reshape(k // P, P, n // P, P).transpose(0, 2, 1, 3)

    def pack(blocks):
        b = np.stack(blocks)
        return b.reshape(-1, 4, P, P).transpose(0, 2, 1, 3).reshape(-1, P, 4 * P)

    def column_tiles(w, tiles):
        u = units(w)
        return pack([u[k, n] for n in tiles for k in range(KC)])

    w_in = a["ev_w_in"][0]
    za, zr, gates = 0, 24, 49
    order = [zr + 24]
    for i in range(EV_ROUNDS + 1):
        if i:
            order.append(gates + 8 + i - 1)
        if i < EV_ROUNDS:
            order += [za + i, za + 8 + i, gates + i, za + 16 + i, zr + i, zr + 8 + i, zr + 16 + i]
    od_order = []
    for i in range(OD_ROUNDS):
        od_order += [i, 4 + i, 8 + i, 12 + 2 * i, 13 + 2 * i, 20 + i, 24 + 2 * i, 25 + 2 * i]

    def rows(w):
        u = units(w)
        return pack([u[k, n] for k in range(u.shape[0]) for n in range(u.shape[1])])

    def by_output(w):
        u = units(w)
        return pack([u[k, n] for n in range(u.shape[1]) for k in range(u.shape[0])])

    wall = np.concatenate([
        column_tiles(w_in, order), rows(a["ev_w_out"][0]), by_output(a["ple_proj"][0]), rows(a["ple_gate"][0]),
        column_tiles(a["od_w_in"][0], od_order), rows(a["od_w_out"][0]), by_output(a["ple_proj"][1]), rows(a["ple_gate"][1]),
    ])
    assert wall.shape[0] == N_UNITS

    def cols(v):
        return v.reshape(-1, P).T

    mu = a["rw_mu"][0]
    par_e = np.zeros((P, N_EV + 1, 8), np.float32)
    for n, v in enumerate((mu[0:1024], mu[1024:2048], mu[2048:3072], a["rw_w0"][0], a["rw_a0"][0], a["rw_k_k"][0],
                           a["rw_k_a"][0], a["rw_r_k"][0], a["rw_ln_g"][0], a["rw_ln_b"][0], a["hg_lb_logits"][0],
                           a["hg_norm"][0])):
        par_e[:, n, :] = cols(v)
    par_e[:, N_EV, 0] = mu[3072:]
    par_o = np.zeros((P, N_OD, 8), np.float32)
    for n, v in enumerate((*a["lru_conv_w"][0], a["lru_conv_b"][0], a["lru_ba"][0], a["lru_bx"][0], a["lru_lambda"][0])):
        par_o[:, n, :] = cols(v)
    gains = np.stack([cols(v) for v in (a["ev_norm"][0], a["ple_norm"][0], a["od_norm"][0], a["ple_norm"][1],
                                        a["final_norm"])], axis=1)
    w2a2 = np.concatenate([a["rw_w2"][0], a["rw_a2"][0]]).reshape(P, 8, P).transpose(1, 0, 2)
    lru_w = np.stack([a["lru_wa"][0], a["lru_wx"][0]], axis=1).reshape(OD_ROUNDS, 4, P, P).transpose(0, 2, 1, 3)

    t = np.arange(P)
    m8 = np.zeros((P, N_MASK), np.float32)
    for lvl in range(LEVELS):
        m = 1 << lvl
        blocks = t.reshape(-1, 2, m)
        even, odd = blocks[:, 0].ravel(), blocks[:, 1].ravel()
        pairs = (t[:, None] // (2 * m) == odd[None] // (2 * m)) & (t[:, None] % (2 * m) < m)
        m8[:, lvl * 256:(lvl + 1) * 256] = np.tile(pairs, (1, 4))
        if lvl < 6:
            pairs = (t[:, None] // (2 * m) == even[None] // (2 * m)) & (t[:, None] % (2 * m) >= m)
            m8[:, 2816 + lvl * P:2816 + (lvl + 1) * P] = np.tile(pairs, (1, 2))
    m8[:, 1792:2304] = np.tile(np.eye(P), (1, 4))
    before, upto = t[:, None] < t[None], t[:, None] <= t[None]
    m8[:, 2304:2816] = np.concatenate([before, upto, before, upto], axis=1)
    fc = np.zeros((P, 4, P), np.float32)
    fc[:, 0] = np.eye(P)
    fc[:, 1] = 1.0
    fc[:, 2] = t[:, None] // 64 == t[None] // 64
    fc[:, 3] = np.where(t[:, None] < t[None], -1e30, 0.0)

    arrays = {
        "xT": a["x"][0].T.reshape(KC, P, T).transpose(1, 0, 2),
        "pT": a["p"][:, 0].transpose(0, 2, 1).reshape(2, 2, P, T).transpose(0, 2, 1, 3),
        "wall": wall, "par_e": par_e, "par_o": par_o, "gains": gains, "w2a2": w2a2, "lru_w": lru_w,
        "mask_f32": m8, "const_f32": fc,
    }
    arrays = {n: np.ascontiguousarray(v) for n, v in arrays.items()}
    nc = bacc.Bacc("TRN2", target_bir_lowering=False, num_devices=1)
    d = {n: nc.dram_tensor(n, v.shape, mybir.dt.from_np(v.dtype), kind="ExternalInput").ap() for n, v in arrays.items()}
    out = nc.dram_tensor("out", (P, KC, T), F32, kind="ExternalOutput").ap()
    trunk(nc, d["xT"], d["pT"], d["wall"], d["par_e"], d["par_o"], d["gains"], d["w2a2"], d["lru_w"],
          (d["mask_f32"], d["const_f32"]), out)
    r = run(nc, [arrays], core_ids=[0])
    return r.results[0]["out"].transpose(1, 0, 2).reshape(D, T).T.reshape(1, T, D)
```

```python
from contextlib import ExitStack

import numpy as np
import concourse.bass as bass
from concourse import mybir

F32 = mybir.dt.float32
F32R = mybir.dt.float32r
U8 = mybir.dt.uint8
ALU = mybir.AluOpType
ACT = mybir.ActivationFunctionType

T = 512
D = 1024
P = 128
KC = D // P
CH = 4
L = T // CH
EPS = 1e-6
LN_EPS = 64e-5
KAPPA = float(np.exp(-0.5))
LN2 = float(np.log(2.0))
EV_ROUNDS = 8
OD_ROUNDS = 4
TILES = 8
LEVELS = 7
N_MASK = LEVELS * 2 * P + T + 4 * P + (LEVELS - 1) * P

EV_UNITS = 2 * (TILES * EV_ROUNDS + 1)
U_OUT0 = EV_UNITS
U_PRJ0 = U_OUT0 + 32
U_GAT0 = U_PRJ0 + 4
U_ODD = U_GAT0 + 16
U_OUT1 = U_ODD + 2 * TILES * OD_ROUNDS
U_PRJ1 = U_OUT1 + 24
U_GAT1 = U_PRJ1 + 4
N_UNITS = U_GAT1 + 16
SLOTS = 4

(MU_R, MU_K, MU_V, W0, A0, K_K, K_A, R_K, LN_G, LN_B, LB_LOGIT, HG_G,
 OMU_R, OMU_K, OMU_V, LB, OLB) = range(17)
N_EV, N_EVP = 12, 17
CW0, CW1, CW2, CW3, CONV_B, BA, BX, LAM, CNEG, CPOS = range(10)
N_OD, N_ODP = 8, 10


PER_ROUND = dict(
    w_hi=1, w_ready=1, units_done=1,
    x_added=8, sq_ready=8, sq_used=8, ln_done=1, rstd=1, hn_ready=8, hi_ready=8, h_ready=8,
    p_hi=2, p_ready=2, prj_evac=4, gate_sig=8, gate_mul=8, y_hi=1, y_split=1,
    par_dve=19, par_exp=1, par_lam=4, zeroed=1, masks_set=1, bias_set=4,
    free0=4, free1=4, cur_e=1, cur_r=1, lr_shift=1, lr_ready=1, sig_gb=1, sig_q=1, sig_f=1, fk=2, sig_ga=1, shifted=3,
    hg_lvl=8, hg_even=14, hg_qk=8, hg_masked=8, hg_vt=1, hg_vtok=1, hg_kt=1, hg_ktok=1, hg_kv=1,
    hg_state=3, hg_o=1, hg_sq=1, hg_ssq=1, hg_ln=1, hg_rstd=1, hg_n=1, hg_y=1,
    rw_wx=1, rw_ax=1, rw_sw=1, rw_av=1, rw_ksq=1, rw_ssq=1, rw_prep=5, rw_center=1, rw_rk=1, rw_m1=1, rw_ln=1, rw_rn=1,
    rw_bon=1, rw_bonus=1, rw_exp=3, rw_kk=2, rw_ops=4, rw_rho=1, rw_tr=3, rw_tok=3, rw_reset=1,
    rw_qk=8, rw_nat=2, rw_masked=8, rw_init=2, rw_p=24, rw_pev=24, rw_n=24, rw_x=24, rw_t=20, rw_xt=20,
    rw_rhs=4, rw_rhse=4, rw_u=4, rw_ue=4, rw_st=3, rw_sadd=3, rw_s=3, rw_yc=4,
    rw_ysb=1, rw_mean=1, rw_d=1, rw_dsq=1, rw_var=1, rw_lnv=1, rw_rstd=1, rw_norm=2, rw_y=1,
    ofree0=4, ofree1=4, cur_o=1, o_sig=3, o_gate=3, mo_vt=1, mo_vtok=1, mo_s=8, mo_max=8, mo_neg=8, mo_exp=8, mo_inv=8, mo_p=8,
    mo_tr=8, mo_pt=8, mo_pv=8, mo_y=1,
    conv_pad=1, ru_conv=8, ru_r_mm=2, ru_i_mm=2, ru_r=2, ru_i=2, ru_th=2, ru_clamp=2, ru_a=2, ru_u1=2, ru_u2=2, ru_d=2, ru_e=2,
    ru_ix=2, ru_b=2, ru_h=2, ru_y=2,
)


def count(name, r, j=0):
    value = r * PER_ROUND[name] + j + 1
    assert not isinstance(value, int) or value > 0, (name, r, j)
    return value


def trunk(nc, xT, pT, wall, par_e, par_o, gains, w2a2, lru_w, masks, out):
    ctx = ExitStack()
    with ctx:
        def sb(name, shape, dt=F32):
            return ctx.enter_context(nc.sbuf_tensor(name, shape, dt))

        sem = {n: ctx.enter_context(nc.semaphore(n)) for n in PER_ROUND}
        raw_loaded = [ctx.enter_context(nc.semaphore(f"raw_loaded{i}")) for i in range(SLOTS)]
        x_loaded = ctx.enter_context(nc.semaphore("x_loaded"))
        x_again = ctx.enter_context(nc.semaphore("x_again"))
        const_loaded = ctx.enter_context(nc.semaphore("const_loaded"))
        w2_loaded = ctx.enter_context(nc.semaphore("w2_loaded"))
        lru_loaded = ctx.enter_context(nc.semaphore("lru_loaded"))
        p_loaded = ctx.enter_context(nc.semaphore("p_loaded"))
        stored = ctx.enter_context(nc.semaphore("stored"))
        vector_copies = ctx.enter_context(nc.semaphore("vector_copies"))
        splits = ctx.enter_context(nc.semaphore("splits"))

        w_raw = sb("w_raw", [P, SLOTS, 4 * P])
        w_hi = sb("w_hi", [P, SLOTS, 4, P], F32R)
        w_lo = sb("w_lo", [P, SLOTS, 4, P], F32R)
        h_split = sb("h_split", [P, 2 * KC, T], F32R)
        y = sb("y", [P, 2 * KC, T])
        mix = sb("mix", [P, 28800])
        ev = sb("ev", [P, N_EVP, 8])
        od = sb("od", [P, N_ODP, 8])
        gain = sb("gain", [P, 5, KC])
        par_t = sb("par_t", [P, 3, 8])
        mu_lr = sb("mu_lr", [P, 3])
        bias = sb("bias", [P, 5])
        mask8 = sb("mask8", [P, N_MASK], U8)
        fconst = sb("fconst", [P, 4, P])
        ident, ones, bones, causal = (fconst[:, n, :] for n in range(4))
        psum = ctx.enter_context(nc.psum_tensor("psum", [P, 8, T], F32))
        bank = [psum[:, n, :] for n in range(8)]
        H0, H1, R0, R1, R2, R3 = bank[2:8]

        used = [0]

        def place(width):
            at = used[0]
            used[0] += width
            assert used[0] <= 28800, used[0]
            return mix[:, at:at + width]

        x_at = place(KC * T)
        x = x_at.rearrange("p (c t) -> p c t", c=KC)
        rw_m = x_at.rearrange("p (c e s t) -> p c e s t", c=CH, e=2, s=4)
        start = used[0]
        hq, hk, hf, hv, sig_a, sig_b, g_a = (place(T) for _ in range(7))
        qp = place(4 * T).rearrange("p (r t) -> p r t", r=4)
        kr = place(4 * T).rearrange("p (r t) -> p r t", r=4)
        tot = [hf] + [place(T >> (n + 1)) for n in range(7)]
        attn = place(T)
        h_vtok = place(T)
        h_ktok = hf
        h_state = place(3 * P)
        wr, wk, wv, g_b = (place(T) for _ in range(4))
        shift = place(T + 8)
        t1, t2, w_a = (place(T) for _ in range(3))
        cum = place(CH * (L + 1)).rearrange("p (c t) -> p c t", c=CH)
        e_pos = cum
        e_neg = place(T)
        ar = place(4 * T).rearrange("p (c e s t) -> p c e s t", c=CH, e=2, s=2)
        b_t, k_t, w_bonus = (place(T) for _ in range(3))
        b_tok, k_tok, v_tok = (place(T) for _ in range(3))
        inv = place(CH * T).rearrange("p (c s t) -> p c s t", c=CH, s=4)
        p_full = place(4 * P).rearrange("p (r e t) -> p r e t", r=2, e=2)
        rhs_s = place(2 * P).rearrange("p (r t) -> p r t", r=2)
        u_s = place(2 * P).rearrange("p (r t) -> p r t", r=2)
        w_state = place(2 * 64).rearrange("p (r t) -> p r t", r=2)
        s_sum = place(64)
        e_mid, rho = place(CH), place(CH)
        lr = place(T)
        w2_slot = place(2 * P).rearrange("p (k t) -> p k t", k=2)
        cur_e, cur_r = place(N_EVP), place(N_EVP)
        used[0] = start
        sq = place(2 * T).rearrange("p (r t) -> p r t", r=2)
        hn = place(2 * T).rearrange("p (r t) -> p r t", r=2)
        rstd_s = place(T)
        sg = place(2 * T).rearrange("p (r t) -> p r t", r=2)
        prj = place(KC * T).rearrange("p (c t) -> p c t", c=KC)
        masks_in = prj.rearrange("p c t -> p (c t)")[:, 0:N_MASK]
        p_raw = place(2 * T).rearrange("p (c t) -> p c t", c=2)
        mq = place(2 * T).rearrange("p (e t) -> p e t", e=2)
        mk, mv, m_vtok = (place(T) for _ in range(3))
        prob = place(2 * T).rearrange("p (r t) -> p r t", r=2)
        prob_t = place(2 * T).rearrange("p (r t) -> p r t", r=2)
        m_stat = place(3 * 8).rearrange("p (k t) -> p k t", k=3)
        m_sum = place(8)
        og = place(3 * T).rearrange("p (r t) -> p r t", r=3)
        osig = place(3 * T).rearrange("p (r t) -> p r t", r=3)
        xd = place(2 * (T + 8)).rearrange("p (r t) -> p r t", r=2)
        xc = place(2 * T).rearrange("p (r t) -> p r t", r=2)
        u_r, u_i, u_th, u_1, u_2 = ((place(T), place(T)) for _ in range(5))
        lru_slot = place(4 * P).rearrange("p (k t) -> p k t", k=4)
        cur_o = place(2 * N_ODP).rearrange("p (k b) -> p k b", b=2)

        hg_mask = mask8[:, 0:7 * 256].rearrange("p (l t) -> p l t", l=7)
        diag_mask = mask8[:, 1792:2304]
        m4_mask = mask8[:, 2304:2816].rearrange("p (e s t) -> p e s t", e=2, s=2)
        nat_mask = mask8[:, 2816:3584].rearrange("p (l t) -> p l t", l=6)

        def halves(ap, m):
            v = ap.rearrange("p (b two m) -> p b two m", two=2, m=m)
            return v[:, :, 0, :], v[:, :, 1, :]

        block = ctx.enter_context(nc.Block())

        @block.sync
        def _(sp):
            sp.dma_start(x[:, 0:4, :], xT[:, 0:4, :]).then_inc(x_loaded, 16)
            sp.dma_start(x[:, 4:8, :], xT[:, 4:8, :]).then_inc(x_loaded, 16)
            sp.dma_start(ev[:, 0:N_EV, :], par_e[:, 0:N_EV, :]).then_inc(const_loaded, 16)
            sp.dma_start(od[:, 0:N_OD, :], par_o).then_inc(const_loaded, 16)
            sp.dma_start(gain[:, :, :], gains).then_inc(const_loaded, 16)
            sp.dma_start(mu_lr[:, 0:2], par_e[:, N_EV, 0:2]).then_inc(const_loaded, 16)
            sp.dma_start(masks_in, masks[0]).then_inc(const_loaded, 16)
            sp.dma_start(fconst[:, :, :], masks[1]).then_inc(const_loaded, 16)

            def load_unit(g, slot):
                sp.dma_start(w_raw[:, slot, :], wall[bass.ds(g * SLOTS + slot, 1), :, :]).then_inc(raw_loaded[slot], 16)

            for slot in range(SLOTS):
                load_unit(0, slot)
            with sp.Fori(1, N_UNITS // SLOTS) as g:
                for slot in range(SLOTS):
                    sp.wait_ge(sem["w_ready"], count("w_ready", g * SLOTS + slot - SLOTS))
                    load_unit(g, slot)
            for slot in range(N_UNITS % SLOTS):
                g = N_UNITS // SLOTS
                sp.wait_ge(sem["w_ready"], count("w_ready", (g - 1) * SLOTS + slot))
                load_unit(g, slot)
            for c in range(KC):
                sp.wait_ge(sem["hn_ready"], count("hn_ready", 4, c))
                sp.dma_start(out[:, c, :], prj[:, c, :]).then_inc(stored, 16)
            sp.wait_ge(stored, 16 * KC)

        @block.gpsimd
        def _(pool):
            def split_unit(g, slot, first=False):
                u = g * SLOTS + slot
                pool.wait_ge(raw_loaded[slot], 16 * (g + 1))
                if not first:
                    pool.wait_ge(sem["units_done"], count("units_done", u - SLOTS))
                pool.sem_inc(splits, 1)
                pool.tensor_scalar(w_hi[:, slot, :, :], w_raw[:, slot, :], 1.0, 0.0, ALU.mult, ALU.add).then_inc(sem["w_hi"], 1)
                pool.wait_ge(sem["w_hi"], count("w_hi", u))
                pool.tensor_tensor(w_lo[:, slot, :, :], w_raw[:, slot, :],
                                          w_hi[:, slot, :, :].bitcast(F32).rearrange("p k n -> p (k n)"), ALU.subtract).then_inc(sem["w_ready"], 1)

            for slot in range(SLOTS):
                split_unit(0, slot, first=True)
            with pool.Fori(1, N_UNITS // SLOTS) as g:
                for slot in range(SLOTS):
                    split_unit(g, slot)
            for slot in range(N_UNITS % SLOTS):
                split_unit(N_UNITS // SLOTS, slot)

        @block.tensor
        def _(pe):
            def mm(o, lhsT, rhs, start=True, stop=True):
                return pe.matmul(o, lhsT, rhs, start=start, stop=stop, skip_group_check=True)

            def split_products(o, slot, j, hi, lo, start, stop):
                mm(o, w_hi[:, slot, j, :], hi, start, False)
                mm(o, w_hi[:, slot, j, :], lo, False, False)
                return mm(o, w_lo[:, slot, j, :], hi, False, stop)

            def half_tile(r, j, half, unit0, free, first_free, stage=None):
                o = bank[j % 2][:, :]
                if half == 0 and not first_free:
                    pe.wait_ge(sem[f"{free}{j % 2}"], count(f"{free}{j % 2}", r, j // 2 - 1))
                slot = (unit0 + 2 * j + half) % SLOTS
                pe.wait_ge(sem["w_ready"], r * 2 * TILES + unit0 + 2 * j + half + 1)
                for k in range(4):
                    c = 4 * half + k
                    if stage is not None:
                        pe.wait_ge(sem["h_ready"], count("h_ready", stage, c))
                    last = split_products(o, slot, k, h_split[:, c, :], h_split[:, KC + c, :], c == 0, c == KC - 1)
                last.then_inc(sem["units_done"], 1)

            def tile(r, j, unit0, free, first_free, stage=None):
                half_tile(r, j, 0, unit0, free, first_free, stage)
                half_tile(r, j, 1, unit0, free, first_free, stage)

            def sumsq(stage, o, c):
                pe.wait_ge(sem["sq_ready"], count("sq_ready", stage, c))
                last = mm(o, ones, sq[:, c % 2, :], c == 0, c == KC - 1)
                last.then_inc(sem["sq_used"], 1)

            pe.wait_ge(const_loaded, 96)
            for c in range(KC):
                sumsq(0, R3[:, :], c)

            def low_rank(r):
                pe.wait_ge(w2_loaded, (r + 1) * 32)
                if isinstance(r, int) and r == 0:
                    pe.wait_ge(sem["lr_ready"], count("lr_ready", 0))
                    pe.wait_ge(sem["zeroed"], count("zeroed", 0))
                else:
                    pe.wait_ge(sem["rw_d"], count("rw_d", r - 1))
                    pe.wait_ge(sem["rw_lnv"], count("rw_lnv", r - 1))
                mm(R0[:, :], w2_slot[:, 0, :], lr).then_inc(sem["rw_wx"], 1)
                mm(R1[:, :], w2_slot[:, 1, :], lr).then_inc(sem["rw_ax"], 1)

            def key_norm(r):
                pe.wait_ge(sem["rw_ksq"], count("rw_ksq", r))
                if not (isinstance(r, int) and r == 0):
                    pe.wait_ge(sem["rw_ysb"], count("rw_ysb", r - 1))
                mm(R2[:, :], bones, t1).then_inc(sem["rw_ssq"], 1)

            def bonus(r):
                pe.wait_ge(sem["rw_rk"], count("rw_rk", r))
                mm(R3[:, :], bones, t2).then_inc(sem["rw_bon"], 1)

            def transposes(r):
                pe.wait_ge(sem["rw_av"], count("rw_av", r))
                for n, (src, o) in enumerate(((b_t, R0), (k_t, R1), (wv, R2))):
                    if n < 2:
                        pe.wait_ge(sem["rw_ops"], count("rw_ops", r, 2 + n))
                    else:
                        pe.wait_ge(sem["rw_m1"], count("rw_m1", r))
                        pe.wait_ge(sem["rw_bonus"], count("rw_bonus", r))
                    for c in range(CH):
                        last = pe.transpose(o[:, c * L:(c + 1) * L], src[:, c * L:(c + 1) * L], ident)
                    last.then_inc(sem["rw_tr"], 1)

            def products(r):
                for e in range(2):
                    if e == 0:
                        pe.wait_ge(sem["rw_tok"], count("rw_tok", r, 2))
                    for c in range(CH):
                        last = mm(bank[6 + e][:, c * P:(c + 1) * P], ar[:, c, e, 0, :], b_t[:, c * L:(c + 1) * L])
                    last.then_inc(sem["rw_nat"], 1)
                for c in range(CH):
                    for k, keys in enumerate((b_t, k_t)):
                        n = 2 * c + k
                        if n < 2:
                            pe.wait_ge(sem["rw_tok"], count("rw_tok", r, n))
                        else:
                            pe.wait_ge(sem["rw_masked"], count("rw_masked", r, n - 2))
                        mm(bank[4 + k], keys[:, c * L:(c + 1) * L], ar[:, c, :, :, :]).then_inc(sem["rw_qk"], 1)

            def inverse_p(r, lvl, c):
                n, m = (lvl - 1) * CH + c, 1 << lvl
                if lvl == 1:
                    pe.wait_ge(sem["rw_masked"], count("rw_masked", r, 2 * c + 1))
                    pe.wait_ge(sem["rw_init"], count("rw_init", r, 1))
                    pe.wait_ge(sem["rw_masked"], count("rw_masked", r, 7))
                else:
                    pe.wait_ge(sem["rw_x"], count("rw_x", r, n - CH))
                if n >= 2:
                    pe.wait_ge(sem["rw_pev"], count("rw_pev", r, n - 2))
                for e in range(2):
                    last = mm(bank[4 + c % 2][:, e * P:(e + 1) * P], rw_m[:, c, e, 0, :], inv[:, c, e, :])
                last.then_inc(sem["rw_p"], 1)

            def inverse_n(r, lvl, c):
                n = (lvl - 1) * CH + c
                pe.wait_ge(sem["rw_pev"], count("rw_pev", r, n))
                if n >= 2:
                    pe.wait_ge(sem["rw_x"], count("rw_x", r, n - 2))
                else:
                    pe.wait_ge(sem["rw_init"], count("rw_init", r, 1))
                if lvl >= 2:
                    pe.wait_ge(sem["rw_xt"], count("rw_xt", r, n - CH))
                o = bank[6 + c % 2]
                for e in range(2):
                    if lvl < 6:
                        last = mm(o[:, e * P:(e + 1) * P], inv[:, c, 2 + e, :], p_full[:, c % 2, e, :])
                    else:
                        last = mm(o[0:64, e * 64:e * 64 + 64], p_full[:, c % 2, e, 0:64], inv[:, c, 2 + e, 64:P])
                last.then_inc(sem["rw_n"], 1)

            def inverse_t(r, lvl, c):
                n = (lvl - 1) * CH + c
                pe.wait_ge(sem["rw_x"], count("rw_x", r, n))
                if n >= 2:
                    pe.wait_ge(sem["rw_xt"], count("rw_xt", r, n - 2))
                elif n == 0:
                    pe.wait_ge(sem["hg_ln"], count("hg_ln", r))
                else:
                    pe.wait_ge(sem["hg_n"], count("hg_n", r))
                for e in range(2):
                    last = pe.transpose(bank[2 + c % 2][:, e * P:(e + 1) * P], inv[:, c, e, :], ident)
                last.then_inc(sem["rw_t"], 1)

            def inverse(r, lvl):
                inverse_p(r, lvl, 0)
                if lvl > 1:
                    inverse_t(r, lvl - 1, 2)
                inverse_p(r, lvl, 1)
                if lvl > 1:
                    inverse_t(r, lvl - 1, 3)
                inverse_n(r, lvl, 0)
                inverse_p(r, lvl, 2)
                inverse_n(r, lvl, 1)
                if lvl < 6:
                    inverse_t(r, lvl, 0)
                inverse_p(r, lvl, 3)
                inverse_n(r, lvl, 2)
                if lvl < 6:
                    inverse_t(r, lvl, 1)
                inverse_n(r, lvl, 3)

            def chain(r, c):
                if c == 0:
                    pe.wait_ge(sem["rw_pev"], count("rw_pev", r, 23))
                    pe.wait_ge(sem["rw_x"], count("rw_x", r, 23))
                else:
                    pe.wait_ge(sem["rw_ue"], count("rw_ue", r, c - 1))
                heads = [(e, slice(64 * e, 64 * e + 64)) for e in range(2)]
                if c:
                    pe.wait_ge(sem["rw_s"], count("rw_s", r, c - 1))
                for e, rows in heads:
                    at = slice(c * L + 64 * e, c * L + 64 * e + 64)
                    o = bank[4 + e][:, 0:64]
                    last = mm(o, rw_m[:, c, e, 2, :], v_tok[:, at], True, c == 0)
                    if c:
                        last = mm(o, ar[:, c, e, 0, :], w_state[:, c % 2, :], False, True)
                last.then_inc(sem["rw_rhs"], 1)
                pe.wait_ge(sem["rw_rhse"], count("rw_rhse", r, c))
                for e, rows in heads:
                    last = mm(R0[:, 64 + 64 * e:128 + 64 * e], inv[:, c, 2 + e, :], rhs_s[:, c % 2, rows])
                last.then_inc(sem["rw_u"], 1)
                pe.wait_ge(sem["rw_ue"], count("rw_ue", r, c))
                if c < CH - 1:
                    if c:
                        pe.wait_ge(sem["rw_s"], count("rw_s", r, c - 1))
                    for e, rows in heads:
                        at = slice(c * L + 64 * e, c * L + 64 * e + 64)
                        mm(R3[rows, 0:64], k_tok[:, at], v_tok[:, at], True, False)
                        last = mm(R3[rows, 0:64], b_tok[:, at], u_s[:, c % 2, rows], False, True)
                    last.then_inc(sem["rw_st"], 1)
                for e, rows in heads:
                    at = slice(c * L + 64 * e, c * L + 64 * e + 64)
                    o = R2[rows, c * L:(c + 1) * L]
                    mm(o, v_tok[:, at], rw_m[:, c, e, 3, :], True, False)
                    last = mm(o, u_s[:, c % 2, rows], rw_m[:, c, e, 1, :], False, c == 0)
                    if c:
                        last = mm(o, w_state[:, c % 2, :], ar[:, c, e, 1, :], False, True)
                last.then_inc(sem["rw_yc"], 1)

            def head_norm(r):
                pe.wait_ge(sem["rw_ysb"], count("rw_ysb", r))
                mm(R0[:, :], bones, b_t).then_inc(sem["rw_mean"], 1)
                pe.wait_ge(sem["rw_dsq"], count("rw_dsq", r))
                mm(R1[:, :], bones, k_t).then_inc(sem["rw_var"], 1)

            def hg_values(r):
                pe.wait_ge(sem["free0"], count("free0", r, 2))
                if not (isinstance(r, int) and r == 0):
                    pe.wait_ge(sem["hg_ln"], count("hg_ln", r - 1))
                for c in range(CH):
                    last = pe.transpose(H0[:, c * L:(c + 1) * L], hv[:, c * L:(c + 1) * L], ident)
                last.then_inc(sem["hg_vt"], 1)

            def hg_level(r, lvl):
                o = bank[2 + lvl % 2]
                pe.wait_ge(sem["hg_lvl"], count("hg_lvl", r, lvl))
                if lvl:
                    pe.wait_ge(sem["hg_even"], count("hg_even", r, 2 * lvl - 1))
                if lvl == 0:
                    pe.wait_ge(sem["hg_vtok"], count("hg_vtok", r))
                elif lvl == 1:
                    if not (isinstance(r, int) and r == 0):
                        pe.wait_ge(sem["hg_n"], count("hg_n", r - 1))
                else:
                    pe.wait_ge(sem["hg_masked"], count("hg_masked", r, lvl - 2))
                keys = hk if lvl == 0 else kr[:, lvl % 4, :]
                for c in range(CH):
                    at = slice(c * L, (c + 1) * L)
                    last = mm(o[:, at], keys[:, at], qp[:, lvl % 4, at])
                last.then_inc(sem["hg_qk"], 1)

            def hg_diagonal(r):
                pe.wait_ge(sem["hg_masked"], count("hg_masked", r, 5))
                for c in range(CH):
                    last = mm(H1[:, c * L:(c + 1) * L], hk[:, c * L:(c + 1) * L], hq[:, c * L:(c + 1) * L])
                last.then_inc(sem["hg_qk"], 1)

            def hg_states(r):
                pe.wait_ge(sem["hg_lvl"], count("hg_lvl", r, 7))
                pe.wait_ge(sem["hg_even"], count("hg_even", r, 13))
                pe.wait_ge(sem["hg_masked"], count("hg_masked", r, 6))
                for c in range(CH - 1):
                    last = pe.transpose(H0[:, c * L:(c + 1) * L], kr[:, 3, c * L:(c + 1) * L], ident)
                last.then_inc(sem["hg_kt"], 1)
                pe.wait_ge(sem["hg_ktok"], count("hg_ktok", r))
                for c in range(CH - 1):
                    last = mm(H0[:, c * L:(c + 1) * L], h_ktok[:, c * L:(c + 1) * L], h_vtok[:, c * L:(c + 1) * L])
                last.then_inc(sem["hg_kv"], 1)

            def hg_outputs(r):
                pe.wait_ge(sem["hg_masked"], count("hg_masked", r, 7))
                for c in range(CH):
                    at = slice(c * L, (c + 1) * L)
                    if c == 0 and not (isinstance(r, int) and r == 0):
                        pe.wait_ge(sem["hg_n"], count("hg_n", r - 1))
                    last = mm(H1[:, at], h_vtok[:, at], attn[:, at], True, c == 0)
                    if c:
                        pe.wait_ge(sem["hg_state"], count("hg_state", r, c - 1))
                        last = mm(H1[:, at], h_state[:, (c - 1) * P:c * P], qp[:, 3, at], False, True)
                last.then_inc(sem["hg_o"], 1)

            def hg_norm(r):
                pe.wait_ge(sem["hg_sq"], count("hg_sq", r))
                mm(H0[:, :], ones, hk).then_inc(sem["hg_ssq"], 1)

            def even_round(i, head=True, pair=True):
                r = i - 1
                first = isinstance(i, int) and i == 0

                def t(j):
                    tile(i, j, 0, "free", first and j < 2, 0 if first and j == 0 else None)

                t(0)
                if pair:
                    low_rank(r)
                if head:
                    t(1)
                if pair:
                    key_norm(r)
                    bonus(r)
                if head:
                    t(2)
                    t(3)
                    t(4)
                if pair:
                    transposes(r)
                    products(r)
                    for lvl in range(1, 7):
                        inverse(r, lvl)
                    chain(r, 0)
                if head:
                    t(5)
                    hg_values(i)
                    hg_level(i, 0)
                    hg_level(i, 1)
                if pair:
                    chain(r, 1)
                if head:
                    t(6)
                    hg_level(i, 2)
                    hg_level(i, 3)
                if pair:
                    chain(r, 2)
                if head:
                    t(7)
                    hg_level(i, 4)
                    hg_level(i, 5)
                if pair:
                    chain(r, 3)
                if head:
                    hg_level(i, 6)
                    hg_diagonal(i)
                    hg_states(i)
                if pair:
                    head_norm(r)
                if head:
                    hg_outputs(i)
                    hg_norm(i)

            even_round(0, pair=False)
            even_round(1)
            with pe.Fori(2, EV_ROUNDS) as i:
                even_round(i)
            even_round(EV_ROUNDS, head=False)

            def out_projection(unit0, n_chunks, y_from):
                for c in range(n_chunks):
                    ring = c % 6
                    pe.wait_ge(sem["y_split"], count("y_split", 0, y_from + c))
                    for half in range(2):
                        u = unit0 + 2 * c + half
                        pe.wait_ge(sem["w_ready"], count("w_ready", u))
                        for k in range(4):
                            last = split_products(bank[4 * half + k][:, :], u % SLOTS, k, h_split[:, ring, :],
                                                  h_split[:, KC + ring, :], c == 0, c == n_chunks - 1)
                        last.then_inc(sem["units_done"], 1)

            def ple(stage, unit_p, unit_g):
                layer = stage // 2
                pe.wait_ge(sem["p_ready"], count("p_ready", layer, 1))
                pe.wait_ge(sem["x_added"], count("x_added", stage - 1, 0))
                for n in range(KC):
                    sumsq(stage, bank[0][:, :], n)
                    pe.wait_ge(sem["x_added"], count("x_added", stage - 1, 1 + n % 7))
                    if n == 7:
                        pe.wait_ge(sem["prj_evac"], count("prj_evac", layer, 0))
                    u = unit_p + n // 2
                    pe.wait_ge(sem["w_ready"], count("w_ready", u))
                    for c in range(2):
                        last = split_products(bank[1 + n % 7][:, :], u % SLOTS, 2 * (n % 2) + c, h_split[:, 6 + c, :],
                                              h_split[:, KC + 6 + c, :], c == 0, c == 1)
                    if n % 2:
                        last.then_inc(sem["units_done"], 1)
                pe.wait_ge(sem["prj_evac"], count("prj_evac", layer, 3))
                for c in range(KC):
                    pe.wait_ge(sem["h_ready"], count("h_ready", stage, c))
                    for half in range(2):
                        u = unit_g + 2 * c + half
                        pe.wait_ge(sem["w_ready"], count("w_ready", u))
                        for k in range(4):
                            last = split_products(bank[4 * half + k][:, :], u % SLOTS, k, h_split[:, c, :],
                                                  h_split[:, KC + c, :], c == 0, c == KC - 1)
                        last.then_inc(sem["units_done"], 1)

            pe.wait_ge(sem["free0"], count("free0", EV_ROUNDS, 0))
            pe.wait_ge(sem["free1"], count("free1", EV_ROUNDS - 1, 3))
            pe.wait_ge(sem["hg_n"], count("hg_n", EV_ROUNDS - 1))
            pe.wait_ge(sem["rw_d"], count("rw_d", EV_ROUNDS - 1))
            pe.wait_ge(sem["rw_lnv"], count("rw_lnv", EV_ROUNDS - 1))
            out_projection(U_OUT0, 2 * KC, 0)
            ple(1, U_PRJ0, U_GAT0)
            pe.wait_ge(sem["x_added"], count("x_added", 1, 0))
            for c in range(KC):
                sumsq(2, bank[0][:, :], c)

            def mo_values(r):
                pe.wait_ge(sem["ofree1"], count("ofree1", r, 1))
                if not (isinstance(r, int) and r == 0):
                    pe.wait_ge(sem["mo_pt"], count("mo_pt", r - 1, 7))
                for c in range(CH):
                    last = pe.transpose(bank[4][:, c * L:(c + 1) * L], mv[:, c * L:(c + 1) * L], ident)
                last.then_inc(sem["mo_vt"], 1)

            def mo_scores(r, n):
                e, qt = divmod(n, CH)
                o = bank[2 + n % 2]
                if n >= 2:
                    pe.wait_ge(sem["mo_exp"], count("mo_exp", r, n - 2))
                elif not (isinstance(r, int) and r == 0):
                    pe.wait_ge(sem["ru_i"], count("ru_i", r - 1, 1))
                pe.wait_ge(sem["ofree1"], count("ofree1", r, 0))
                pe.wait_ge(sem["ofree0"], count("ofree0", r, 1))
                mm(o[:, 0:(qt + 1) * L], mq[:, e, qt * L:(qt + 1) * L], mk[:, 0:(qt + 1) * L], True, False)
                mm(o[:, qt * L:(qt + 1) * L], ident, causal, False, True).then_inc(sem["mo_s"], 1)

            def mo_transposes(r, n):
                qt = n % CH
                pe.wait_ge(sem["mo_p"], count("mo_p", r, n))
                if n:
                    pe.wait_ge(sem["mo_pt"], count("mo_pt", r, n - 1))
                else:
                    pe.wait_ge(sem["mo_vtok"], count("mo_vtok", r))
                for j in range(qt + 1):
                    last = pe.transpose(bank[4][:, j * L:(j + 1) * L], prob[:, n % 2, j * L:(j + 1) * L], ident)
                last.then_inc(sem["mo_tr"], 1)

            def mo_output(r, n):
                e, qt = divmod(n, CH)
                rows = slice(64 * e, 64 * e + 64)
                pe.wait_ge(sem["mo_pt"], count("mo_pt", r, n))
                if n == 0 and not (isinstance(r, int) and r == 0):
                    pe.wait_ge(sem["mo_y"], count("mo_y", r - 1))
                for j in range(qt + 1):
                    last = mm(bank[5][rows, qt * L:(qt + 1) * L], m_vtok[:, j * L + 64 * e:j * L + 64 * e + 64],
                              prob_t[:, n % 2, j * L:(j + 1) * L], j == 0, j == qt)
                last.then_inc(sem["mo_pv"], 1)

            def ru_gates(r, b):
                pe.wait_ge(sem["ru_conv"], count("ru_conv", r, 4 * b + 3))
                if b == 0:
                    pe.wait_ge(lru_loaded, (r + 1) * 16)
                    if not (isinstance(r, int) and r == 0):
                        pe.wait_ge(sem["ru_i"], count("ru_i", r - 1, 0))
                else:
                    pe.wait_ge(sem["mo_exp"], count("mo_exp", r, 7))
                at = 6 if b == 0 else 2
                mm(bank[at][:, :], lru_slot[:, 2 * b, :], xc[:, b, :]).then_inc(sem["ru_r_mm"], 1)
                mm(bank[at + 1][:, :], lru_slot[:, 2 * b + 1, :], xc[:, b, :]).then_inc(sem["ru_i_mm"], 1)

            def odd_round(i):
                first = isinstance(i, int) and i == 0
                for j in range(4):
                    tile(i, j, U_ODD, "ofree", first and j < 2, 2 if first and j == 0 else None)
                ru_gates(i, 0)
                mo_scores(i, 0)
                mo_scores(i, 1)
                mo_values(i)
                for n in range(2 * CH):
                    half_tile(i, 4 + n // 2, n % 2, U_ODD, "ofree", False)
                    if n:
                        mo_output(i, n - 1)
                    mo_transposes(i, n)
                    if n + 2 < 2 * CH:
                        mo_scores(i, n + 2)
                ru_gates(i, 1)
                mo_output(i, 2 * CH - 1)

            odd_round(0)
            with pe.Fori(1, OD_ROUNDS) as i:
                odd_round(i)

            pe.wait_ge(sem["ofree1"], count("ofree1", OD_ROUNDS - 1, 3))
            pe.wait_ge(sem["mo_y"], count("mo_y", OD_ROUNDS - 1))
            pe.wait_ge(sem["ru_i"], count("ru_i", OD_ROUNDS - 1, 1))
            out_projection(U_OUT1, 4 + KC, 2 * KC)
            ple(3, U_PRJ1, U_GAT1)
            pe.wait_ge(sem["x_added"], count("x_added", 3, 0))
            for c in range(KC):
                sumsq(4, bank[0][:, :], c)

        @block.scalar
        def _(act):
            def f(o, i, func, bias=0.0, scale=1.0, **kw):
                return act.activation(o, i, func, bias=bias, scale=scale, **kw)

            def tile_done(r, j, unit0=0):
                act.wait_ge(sem["units_done"], r * 2 * TILES + unit0 + 2 * j + 2)

            def is_first(r):
                return isinstance(r, int) and r == 0

            def squares(stage, c):
                if stage:
                    act.wait_ge(sem["x_added"], count("x_added", stage - 1, c))
                if c >= 2:
                    act.wait_ge(sem["sq_used"], count("sq_used", stage, c - 2))
                f(sq[:, c % 2, :], x[:, c, :], ACT.Square).then_inc(sem["sq_ready"], 1)

            def root(stage, o):
                act.preload_act_table_set("natural_log_exp_and_others")
                act.wait_ge(sem["sq_used"], count("sq_used", stage, 7))
                f(rstd_s, o, ACT.Ln, bias=bias[:, 0:1], scale=1.0 / D).then_inc(sem["ln_done"], 1)
                act.wait_ge(sem["ln_done"], count("ln_done", stage))
                f(rstd_s, rstd_s, ACT.Exp, scale=-0.5).then_inc(sem["rstd"], 1)

            def high_halves(stage):
                for c in range(KC):
                    act.wait_ge(sem["hn_ready"], count("hn_ready", stage, c))
                    f(h_split[:, c, :], hn[:, c % 2, :], ACT.Copy).then_inc(sem["hi_ready"], 1)

            act.dma_start(w2_slot[0:64, 0, :], w2a2[0, 0:64]).then_inc(w2_loaded, 16)
            act.dma_start(w2_slot[64:P, 1, :], w2a2[0, 64:P]).then_inc(w2_loaded, 16)
            act.wait_ge(x_loaded, 32)
            act.wait_ge(sem["bias_set"], count("bias_set", 0, 3))
            for c in range(KC):
                squares(0, c)
            root(0, R3[:, :])
            high_halves(0)

            act.wait_ge(sem["par_dve"], count("par_dve", 0, 3))
            f(ev[:, LB, :], par_t[:, 0, :], ACT.Exp).then_inc(sem["par_exp"], 1)
            act.wait_ge(sem["par_dve"], count("par_dve", 0, 10))
            f(par_t[:, 2, :], par_t[:, 1, :], ACT.Exp, scale=-1.0).then_inc(sem["par_lam"], 1)
            act.wait_ge(sem["par_lam"], count("par_lam", 0, 0))
            f(par_t[:, 2, :], par_t[:, 2, :], ACT.Ln, bias=bias[:, 3:4]).then_inc(sem["par_lam"], 1)

            def level_copies(r, lvl):
                m = 1 << (lvl - 1)
                act.wait_ge(sem["hg_lvl"], count("hg_lvl", r, lvl - 1))
                if lvl >= 2:
                    act.wait_ge(sem["hg_even"], count("hg_even", r, 2 * lvl - 3))
                if lvl >= 4:
                    act.wait_ge(sem["hg_qk"], count("hg_qk", r, lvl - 4))
                elif lvl == 3 and not is_first(r):
                    act.wait_ge(sem["hg_kt"], count("hg_kt", r - 1))
                keys = hk if lvl == 1 else kr[:, (lvl - 1) % 4, :]
                f(halves(qp[:, lvl % 4, :], m)[0], halves(qp[:, (lvl - 1) % 4, :], m)[0], ACT.Copy).then_inc(sem["hg_even"], 1)
                f(halves(kr[:, lvl % 4, :], m)[1], halves(keys, m)[1], ACT.Copy).then_inc(sem["hg_even"], 1)

            def shifted(i, n, j):
                tile_done(i, j)
                if n == 0:
                    if is_first(i):
                        act.wait_ge(sem["free0"], count("free0", 0, 0))
                    else:
                        act.wait_ge(sem["free1"], count("free1", i - 1, 3))
                    act.wait_ge(sem["cur_e"], count("cur_e", i))
                else:
                    act.wait_ge(sem[f"free{(j - 1) % 2}"], count(f"free{(j - 1) % 2}", i, (j - 1) // 2))
                f(shift[:, 1:T + 1], bank[j % 2][:, :], ACT.Copy, scale=cur_e[:, MU_R + n:MU_R + n + 1]).then_inc(sem["shifted"], 1)

            def inverse_p(r, lvl, c):
                n = (lvl - 1) * CH + c
                act.wait_ge(sem["rw_p"], count("rw_p", r, n))
                if n >= 2:
                    act.wait_ge(sem["rw_n"], count("rw_n", r, n - 2))
                elif not is_first(r):
                    act.wait_ge(sem["rw_n"], count("rw_n", r - 1, 22 + n))
                o = bank[4 + c % 2]
                if lvl < 6:
                    m = 1 << lvl
                    even, _ = halves(p_full[:, c % 2, :, :].rearrange("p e t -> p (e t)"), m)
                    src, _ = halves(o[:, 0:2 * P], m)
                else:
                    even = p_full[:, c % 2, :, 0:64]
                    src = o[:, 0:2 * P].rearrange("p (e t) -> p e t", e=2)[:, :, 0:64]
                f(even, src, ACT.Copy).then_inc(sem["rw_pev"], 1)

            def inverse_t(r, lvl, c):
                act.wait_ge(sem["rw_t"], count("rw_t", r, (lvl - 1) * CH + c))
                f(inv[:, c, 2:4, :].rearrange("p e t -> p (e t)"), bank[2 + c % 2][:, 0:2 * P], ACT.Copy).then_inc(sem["rw_xt"], 1)

            def inverse(r, lvl):
                inverse_p(r, lvl, 0)
                if lvl > 1:
                    inverse_t(r, lvl - 1, 2)
                inverse_p(r, lvl, 1)
                if lvl > 1:
                    inverse_t(r, lvl - 1, 3)
                inverse_p(r, lvl, 2)
                if lvl < 6:
                    inverse_t(r, lvl, 0)
                inverse_p(r, lvl, 3)
                if lvl < 6:
                    inverse_t(r, lvl, 1)

            def chain(r, c):
                act.wait_ge(sem["rw_rhs"], count("rw_rhs", r, c))
                f(rhs_s[:, c % 2, :].rearrange("p (e t) -> p e t", e=2), psum[:, 4:6, 0:64], ACT.Copy).then_inc(sem["rw_rhse"], 1)
                act.wait_ge(sem["rw_u"], count("rw_u", r, c))
                if c < 2 and not is_first(r):
                    act.wait_ge(sem["rw_yc"], count("rw_yc", r - 1, 3))
                elif c >= 2:
                    act.wait_ge(sem["rw_yc"], count("rw_yc", r, c - 2))
                f(u_s[:, c % 2, :], R0[:, 64:192], ACT.Copy).then_inc(sem["rw_ue"], 1)

            def even_round(i, head=True, pair=True):
                r = i - 1
                tile_done(i, 0)
                if is_first(i):
                    act.wait_ge(sem["zeroed"], count("zeroed", 0))
                    f(shift[:, 1:T + 1], bank[0][:, :], ACT.Copy, scale=mu_lr[:, 0:1]).then_inc(sem["lr_shift"], 1)
                    act.wait_ge(sem["free0"], count("free0", 0, 0))
                    f(lr[0:64, :], lr[0:64, :], ACT.Tanh).then_inc(sem["lr_ready"], 1)
                else:
                    act.wait_ge(sem["free1"], count("free1", i - 1, 1))
                    f(sig_a, bank[0][:, :], ACT.Sigmoid).then_inc(sem["sig_gb"], 1)
                if pair:
                    act.wait_ge(sem["cur_r"], count("cur_r", r))
                    act.wait_ge(sem["rw_wx"], count("rw_wx", r))
                    f(e_neg, R0[:, :], ACT.Sigmoid, bias=cur_r[:, W0:W0 + 1]).then_inc(sem["rw_sw"], 1)
                    act.wait_ge(sem["rw_ax"], count("rw_ax", r))
                    f(w_a, R1[:, :], ACT.Sigmoid, bias=cur_r[:, A0:A0 + 1]).then_inc(sem["rw_av"], 1)
                    if head:
                        act.dma_start(w2_slot[0:64, 0, :], w2a2[bass.ds(i, 1), 0:64, :]).then_inc(w2_loaded, 16)
                        act.dma_start(w2_slot[64:P, 1, :], w2a2[bass.ds(i, 1), 64:P, :]).then_inc(w2_loaded, 16)
                    f(t1, wk, ACT.Square, scale=cur_r[:, K_K:K_K + 1]).then_inc(sem["rw_ksq"], 1)
                if head:
                    tile_done(i, 1)
                    f(sig_b, bank[1][:, :], ACT.Sigmoid).then_inc(sem["sig_q"], 1)
                    tile_done(i, 2)
                    if is_first(i):
                        act.wait_ge(sem["free1"], count("free1", 0, 0))
                    else:
                        act.wait_ge(sem["free0"], count("free0", i, 0))
                    f(sig_a, bank[0][:, :], ACT.Sigmoid).then_inc(sem["sig_f"], 1)
                    act.wait_ge(sem["free1"], count("free1", i, 0))
                    f(sig_b, bank[0][:, :], ACT.Sigmoid, scale=-1.0).then_inc(sem["free0"], 1)
                    tile_done(i, 3)
                    act.wait_ge(sem["fk"], count("fk", i, 0))
                    f(sig_a, bank[1][:, :], ACT.Sigmoid).then_inc(sem["sig_ga"], 1)
                act.preload_act_table_set("natural_log_exp_and_others")
                if pair:
                    act.wait_ge(sem["rw_center"], count("rw_center", r))
                    f(e_neg, cum[:, :, 1:L + 1], ACT.Exp, scale=KAPPA).then_inc(sem["rw_exp"], 1)
                    act.wait_ge(sem["rw_exp"], count("rw_exp", r, 0))
                    f(e_pos, cum, ACT.Exp, scale=-KAPPA).then_inc(sem["rw_exp"], 1)
                    f(e_mid, e_mid, ACT.Exp, scale=-KAPPA).then_inc(sem["rw_exp"], 1)
                    act.wait_ge(sem["rw_m1"], count("rw_m1", r))
                    f(t1, t1, ACT.Ln).then_inc(sem["rw_ln"], 1)
                    act.wait_ge(sem["rw_ln"], count("rw_ln", r))
                    f(t1, t1, ACT.Exp, bias=bias[:, 2:3], scale=-0.5).then_inc(sem["rw_rn"], 1)
                if head:
                    tile_done(i, 4)
                    if not is_first(i):
                        act.wait_ge(sem["hg_vt"], count("hg_vt", i - 1))
                    f(hv, bank[0][:, :], ACT.Copy).then_inc(sem["free0"], 1)
                if pair:
                    if not is_first(r):
                        act.wait_ge(sem["rw_u"], count("rw_u", r - 1, 3))
                    f(inv.rearrange("p c s t -> p (c s) t"), fconst[:, 0:1, :].to_broadcast([P, 16, P]), ACT.Copy).then_inc(sem["rw_reset"], 1)
                    for n, (dst, src) in enumerate(((b_tok, R0), (k_tok, R1), (v_tok, R2))):
                        act.wait_ge(sem["rw_tr"], count("rw_tr", r, n))
                        f(dst, src[:, :], ACT.Copy).then_inc(sem["rw_tok"], 1)
                    for lvl in range(1, 7):
                        inverse(r, lvl)
                    chain(r, 0)
                if head:
                    shifted(i, 0, 5)
                    act.wait_ge(sem["hg_vt"], count("hg_vt", i))
                    f(h_vtok, H0[:, :], ACT.Copy).then_inc(sem["hg_vtok"], 1)
                    level_copies(i, 1)
                    level_copies(i, 2)
                if pair:
                    chain(r, 1)
                if head:
                    shifted(i, 1, 6)
                    level_copies(i, 3)
                    level_copies(i, 4)
                if pair:
                    chain(r, 2)
                if head:
                    shifted(i, 2, 7)
                    level_copies(i, 5)
                    level_copies(i, 6)
                if pair:
                    chain(r, 3)
                    if not head:
                        act.wait_ge(sem["rw_yc"], count("rw_yc", r, 3))
                        act.dma_start(x, xT).then_inc(x_again, 16)
                if head:
                    level_copies(i, 7)
                    act.wait_ge(sem["hg_kt"], count("hg_kt", i))
                    f(h_ktok[:, 0:3 * L], H0[:, 0:3 * L], ACT.Copy).then_inc(sem["hg_ktok"], 1)
                if pair:
                    act.wait_ge(sem["rw_yc"], count("rw_yc", r, 3))
                    f(b_t, R2[:, :], ACT.Copy).then_inc(sem["rw_ysb"], 1)
                    act.wait_ge(sem["rw_d"], count("rw_d", r))
                    f(k_t, b_t, ACT.Square).then_inc(sem["rw_dsq"], 1)
                    act.wait_ge(sem["rw_var"], count("rw_var", r))
                    f(t1, R1[:, :], ACT.Ln, bias=bias[:, 1:2], scale=1.0 / 64).then_inc(sem["rw_lnv"], 1)
                    act.wait_ge(sem["rw_lnv"], count("rw_lnv", r))
                    f(t1, t1, ACT.Exp, scale=-0.5).then_inc(sem["rw_rstd"], 1)
                if head:
                    act.wait_ge(sem["hg_o"], count("hg_o", i))
                    f(hk, H1[:, :], ACT.Square).then_inc(sem["hg_sq"], 1)
                    act.wait_ge(sem["hg_ssq"], count("hg_ssq", i))
                    f(sig_b, H0[:, :], ACT.Ln, bias=bias[:, 0:1], scale=1.0 / P).then_inc(sem["hg_ln"], 1)
                    act.wait_ge(sem["hg_ln"], count("hg_ln", i))
                    f(sig_b, sig_b, ACT.Exp, scale=-0.5).then_inc(sem["hg_rstd"], 1)

            even_round(0, pair=False)
            even_round(1)
            with act.Fori(2, EV_ROUNDS) as i:
                even_round(i)
            even_round(EV_ROUNDS, head=False)

            def split_outputs(unit0, n_chunks, y_from, units_before):
                for c in range(n_chunks):
                    act.wait_ge(sem["units_done"], units_before if c < 6 else unit0 + 2 * (c - 5))
                    if y_from == 0 and c == n_chunks - 1:
                        act.wait_ge(sem["rw_y"], count("rw_y", EV_ROUNDS - 1))
                    elif y_from == 0 and c == 0:
                        act.wait_ge(sem["hg_y"], count("hg_y", EV_ROUNDS - 1))
                    elif y_from and c == 0:
                        act.wait_ge(sem["ru_y"], count("ru_y", OD_ROUNDS - 1, 1))
                    f(h_split[:, c % 6, :], y[:, c, :], ACT.Copy).then_inc(sem["y_hi"], 1)

            def split_embedding(layer, units_before):
                act.wait_ge(p_loaded, 16 * (layer + 1))
                act.wait_ge(sem["units_done"], units_before)
                for c in range(2):
                    f(h_split[:, 6 + c, :], p_raw[:, c, :], ACT.Copy).then_inc(sem["p_hi"], 1)

            def ple(stage, unit_p, unit_g):
                layer = stage // 2
                for c in range(KC):
                    squares(stage, c)
                root(stage, bank[0][:, :])
                for m in range(4):
                    act.wait_ge(sem["sq_used"], count("sq_used", stage, 7))
                    act.wait_ge(sem["units_done"], unit_p + m + 1)
                    for n in (2 * m, 2 * m + 1):
                        last = f(prj[:, n, :], bank[1 + n % 7][:, :], ACT.Copy)
                    last.then_inc(sem["prj_evac"], 1)
                high_halves(stage)
                act.wait_ge(sem["units_done"], unit_g + 16)
                for n in range(KC):
                    if n >= 2:
                        act.wait_ge(sem["gate_mul"], count("gate_mul", stage // 2, n - 2))
                    f(sg[:, n % 2, :], bank[n][:, :], ACT.Sigmoid).then_inc(sem["gate_sig"], 1)

            act.dma_start(p_raw, pT[0]).then_inc(p_loaded, 16)
            split_embedding(0, EV_UNITS)
            split_outputs(U_OUT0, 2 * KC, 0, EV_UNITS)
            ple(1, U_PRJ0, U_GAT0)
            for c in range(KC):
                squares(2, c)
            root(2, bank[0][:, :])
            high_halves(2)

            def weights(i, n):
                w = (n % CH + 1) * L
                act.wait_ge(sem["mo_neg"], count("mo_neg", i, n))
                if n >= 2:
                    act.wait_ge(sem["mo_tr"], count("mo_tr", i, n - 2))
                f(prob[:, n % 2, 0:w], bank[2 + n % 2][:, 0:w], ACT.Exp, bias=m_stat[:, 1, n:n + 1], scale=0.125,
                  accum_out=m_sum[:, n:n + 1]).then_inc(sem["mo_exp"], 1)

            def transposed(i, n):
                w = (n % CH + 1) * L
                act.wait_ge(sem["mo_tr"], count("mo_tr", i, n))
                if n >= 2:
                    act.wait_ge(sem["mo_pv"], count("mo_pv", i, n - 2))
                f(prob_t[:, n % 2, 0:w], bank[4][:, 0:w], ACT.Copy).then_inc(sem["mo_pt"], 1)

            def lru_input(i, b):
                if not is_first(i):
                    act.wait_ge(sem["ru_conv"], count("ru_conv", i - 1, 4 * b + 3))
                f(xd[:, b, 3:T + 3], bank[0][:, :], ACT.Copy).then_inc(sem["ofree0"], 1)

            def odd_round(i):
                act.preload_act_table_set("natural_log_exp_and_others")
                act.wait_ge(sem["cur_o"], count("cur_o", i))
                if not is_first(i):
                    act.wait_ge(sem["ru_i_mm"], count("ru_i_mm", i - 1, 1))
                act.dma_start(lru_slot, lru_w[i] if isinstance(i, int) else lru_w[bass.ds(i, 1), :, :, :]).then_inc(lru_loaded, 16)
                tile_done(i, 0, U_ODD)
                lru_input(i, 0)
                tile_done(i, 1, U_ODD)
                act.wait_ge(sem["conv_pad"], count("conv_pad", 0))
                f(mq[0:64, 0, :], bank[1][0:64, :], ACT.Copy)
                f(mq[64:P, 1, :], bank[1][64:P, :], ACT.Copy).then_inc(sem["ofree1"], 1)
                tile_done(i, 3, U_ODD)
                f(mv, bank[1][:, :], ACT.Copy).then_inc(sem["ofree1"], 1)
                weights(i, 0)
                act.wait_ge(sem["mo_vt"], count("mo_vt", i))
                f(m_vtok, bank[4][:, :], ACT.Copy).then_inc(sem["mo_vtok"], 1)
                for n in range(2 * CH):
                    if n + 1 < 2 * CH:
                        weights(i, n + 1)
                    transposed(i, n)
                    if n == 0:
                        tile_done(i, 4, U_ODD)
                        lru_input(i, 1)
                for b in range(2):
                    at = 6 if b == 0 else 2
                    act.wait_ge(sem["ru_r_mm"], count("ru_r_mm", i, b))
                    f(u_r[b], bank[at][:, :], ACT.Sigmoid, bias=cur_o[:, BA, b:b + 1]).then_inc(sem["ru_r"], 1)
                    act.wait_ge(sem["ru_i_mm"], count("ru_i_mm", i, b))
                    f(u_i[b], bank[at + 1][:, :], ACT.Sigmoid, bias=cur_o[:, BX, b:b + 1]).then_inc(sem["ru_i"], 1)
                for b in range(2):
                    act.wait_ge(sem["ru_r"], count("ru_r", i, b))
                    f(u_th[b], u_r[b], ACT.Tanh, scale=cur_o[:, CPOS, b:b + 1]).then_inc(sem["ru_th"], 1)
                for n, free in ((0, ("ofree1", 2)), (1, ("ofree0", 3)), (2, ("ofree1", 3))):
                    act.wait_ge(sem[free[0]], count(free[0], i, free[1]))
                    f(osig[:, n, :], og[:, n, :], ACT.Sigmoid).then_inc(sem["o_sig"], 1)
                act.preload_act_table_set("natural_log_exp_and_others")
                for b in range(2):
                    act.wait_ge(sem["ru_th"], count("ru_th", i, b))
                    f(u_r[b], u_r[b], ACT.Exp, scale=cur_o[:, CNEG, b:b + 1]).then_inc(sem["ru_a"], 1)
                    f(u_1[b], u_th[b], ACT.Ln, bias=bias[:, 3:4]).then_inc(sem["ru_u1"], 1)
                    act.wait_ge(sem["ru_clamp"], count("ru_clamp", i, b))
                    f(u_2[b], u_2[b], ACT.Ln).then_inc(sem["ru_u2"], 1)
                for b in range(2):
                    act.wait_ge(sem["ru_d"], count("ru_d", i, b))
                    f(u_2[b], u_2[b], ACT.Exp, bias=bias[:, 4:5], scale=0.5).then_inc(sem["ru_e"], 1)

            odd_round(0)
            with act.Fori(1, OD_ROUNDS) as i:
                odd_round(i)
            act.wait_ge(sem["gate_mul"], count("gate_mul", 0, 7))
            act.dma_start(p_raw, pT[1]).then_inc(p_loaded, 16)
            split_embedding(1, U_OUT1)
            split_outputs(U_OUT1, 4 + KC, 2 * KC, U_OUT1)
            ple(3, U_PRJ1, U_GAT1)
            for c in range(KC):
                squares(4, c)
            root(4, bank[0][:, :])

        @block.vector
        def _(dve):
            def is_first(r):
                return isinstance(r, int) and r == 0

            def tile_done(r, j, unit0=0):
                dve.wait_ge(sem["units_done"], r * 2 * TILES + unit0 + 2 * j + 2)

            def stt(o, a, scalar, b, op0, op1):
                return dve.scalar_tensor_tensor(out=o, in0=a, scalar=scalar, in1=b, op0=op0, op1=op1)

            def low_half(stage, c):
                dve.wait_ge(sem["hi_ready"], count("hi_ready", stage, c))
                dve.tensor_tensor(h_split[:, KC + c, :], hn[:, c % 2, :], h_split[:, c, :].bitcast(F32), ALU.subtract).then_inc(sem["h_ready"], 1)

            def normed(stage, g, dst):
                dve.wait_ge(sem["rstd"], count("rstd", stage))
                for c in range(KC):
                    if dst is hn and c >= 2:
                        dve.wait_ge(sem["h_ready"], count("h_ready", stage, c - 2))
                    o = hn[:, c % 2, :] if dst is hn else dst[:, c, :]
                    stt(o, x[:, c, :], gain[:, g, c:c + 1], rstd_s, ALU.mult, ALU.mult).then_inc(sem["hn_ready"], 1)
                    if dst is hn and c >= 1:
                        low_half(stage, c - 1)
                if dst is hn:
                    low_half(stage, KC - 1)

            for n, v in enumerate((EPS, LN_EPS, 20 * LN2, 1.0, -20 * LN2)):
                ins = dve.memset(bias[:, n:n + 1], v)
                if n:
                    ins.then_inc(sem["bias_set"], 1)
            dve.wait_ge(const_loaded, 96)
            dve.wait_ge(x_loaded, 32)
            normed(0, 0, hn)

            dve.tensor_scalar(ev[:, OMU_R:OMU_V + 1, :], ev[:, MU_R:MU_V + 1, :], -1.0, 1.0, ALU.mult, ALU.add).then_inc(sem["par_dve"], 1)
            dve.tensor_scalar(mu_lr[:, 2:3], mu_lr[:, 0:1], -1.0, 1.0, ALU.mult, ALU.add).then_inc(sem["par_dve"], 1)
            dve.memset(par_t[:, 1, :], 0.0).then_inc(sem["par_dve"], 1)
            dve.tensor_tensor(par_t[:, 0, :], ev[:, LB_LOGIT, :], ev[:, LB_LOGIT, :], ALU.subtract).then_inc(sem["par_dve"], 1)
            dve.wait_ge(sem["par_exp"], count("par_exp", 0))
            dve.reciprocal(par_t[:, 0, :], ev[:, LB, :]).then_inc(sem["par_dve"], 1)
            dve.wait_ge(sem["par_dve"], count("par_dve", 0, 4))
            dve.tensor_tensor(par_t[:, 0, :], par_t[:, 0, :], ev[:, LB, :], ALU.mult).then_inc(sem["par_dve"], 1)
            dve.wait_ge(sem["par_dve"], count("par_dve", 0, 5))
            dve.tensor_tensor(par_t[:, 0, :], par_t[:, 0, :], par_t[:, 0, :], ALU.subtract).then_inc(sem["par_dve"], 1)
            dve.wait_ge(sem["par_dve"], count("par_dve", 0, 6))
            dve.tensor_scalar(ev[:, LB, :], par_t[:, 0, :], 0.0, None, ALU.max).then_inc(sem["par_dve"], 1)
            dve.wait_ge(sem["par_dve"], count("par_dve", 0, 7))
            dve.tensor_scalar(ev[:, OLB, :], ev[:, LB, :], -1.0, 1.0, ALU.mult, ALU.add).then_inc(sem["par_dve"], 1)
            dve.tensor_scalar(par_t[:, 0, :], od[:, LAM, :], -1.0, None, ALU.mult).then_inc(sem["par_dve"], 1)
            dve.wait_ge(sem["par_dve"], count("par_dve", 0, 9))
            dve.tensor_tensor(par_t[:, 1, :], par_t[:, 0, :], od[:, LAM, :], ALU.max).then_inc(sem["par_dve"], 1)
            dve.tensor_scalar(par_t[:, 0, :], par_t[:, 0, :], 0.0, None, ALU.max).then_inc(sem["par_dve"], 1)
            dve.wait_ge(sem["par_lam"], count("par_lam", 0, 1))
            dve.wait_ge(sem["par_dve"], count("par_dve", 0, 11))
            dve.tensor_tensor(par_t[:, 0, :], par_t[:, 0, :], par_t[:, 2, :], ALU.add).then_inc(sem["par_dve"], 1)
            dve.wait_ge(sem["par_dve"], count("par_dve", 0, 12))
            dve.tensor_scalar(od[:, CNEG, :], par_t[:, 0, :], -8.0, None, ALU.mult).then_inc(sem["par_dve"], 1)
            dve.tensor_scalar(od[:, CPOS, :], par_t[:, 0, :], 8.0, None, ALU.mult).then_inc(sem["par_dve"], 1)
            dve.wait_ge(sem["sq_ready"], count("sq_ready", 0, 7))
            dve.memset(attn, 0.0).then_inc(sem["par_dve"], 1)
            dve.memset(p_full, 0.0).then_inc(sem["par_dve"], 1)
            dve.memset(shift[:, 0:1], 0.0).then_inc(sem["par_dve"], 1)
            dve.wait_ge(sem["par_dve"], count("par_dve", 0, 17))
            dve.memset(cum[:, :, 0:1], 0.0).then_inc(sem["par_dve"], 1)
            dve.tensor_copy(mask8[:, :], masks_in).then_inc(sem["masks_set"], 1)
            dve.memset(w2_slot[64:P, 0, :], 0.0)
            dve.memset(w2_slot[0:64, 1, :], 0.0)
            dve.memset(ar, 0.0)
            dve.memset(rw_m, 0.0).then_inc(sem["zeroed"], 1)
            dve.wait_ge(sem["zeroed"], count("zeroed", 0))

            def masked_copy(dst, mask, src):
                dve.sem_inc(vector_copies, 1)
                return dve.copy_predicated(dst, mask, src)

            def gated(i, j, ready, sig, dst):
                dve.wait_ge(sem[ready], count(ready, i - 1 if j == 0 else i))
                dve.tensor_tensor(dst, bank[j % 2][:, :], sig, ALU.mult).then_inc(sem[f"free{j % 2}"], 1)

            def mixed(i, n, j, dst):
                dve.wait_ge(sem["shifted"], count("shifted", i, n))
                if n == 2 and not is_first(i):
                    dve.wait_ge(sem["rw_tr"], count("rw_tr", i - 1, 2))
                stt(dst, bank[j % 2][:, :], cur_e[:, OMU_R + n:OMU_R + n + 1], shift[:, 0:T], ALU.mult, ALU.add).then_inc(sem[f"free{j % 2}"], 1)

            def level(r, lvl):
                if lvl == 0:
                    dve.wait_ge(sem["fk"], count("fk", r, 1))
                    if not is_first(r):
                        dve.wait_ge(sem["hg_sq"], count("hg_sq", r - 1))
                    dve.tensor_tensor(qp[:, 0, :], hq, hf, ALU.mult).then_inc(sem["hg_lvl"], 1)
                    return
                m = 1 << (lvl - 1)
                keys = hk if lvl == 1 else kr[:, (lvl - 1) % 4, :]
                dve.wait_ge(sem["hg_lvl"], count("hg_lvl", r, lvl - 1))
                if lvl >= 2:
                    dve.wait_ge(sem["hg_even"], count("hg_even", r, 2 * lvl - 3))
                if lvl >= 4:
                    dve.wait_ge(sem["hg_qk"], count("hg_qk", r, lvl - 4))
                t_even, t_odd = halves(tot[lvl - 1], 1)
                nb = T // (2 * m)
                q_dst, k_dst = halves(qp[:, lvl % 4, :], m)[1], halves(kr[:, lvl % 4, :], m)[0]
                q_src, k_src = halves(qp[:, (lvl - 1) % 4, :], m)[1], halves(keys, m)[0]
                dve.tensor_tensor(q_dst, q_src, t_even.to_broadcast([P, nb, m]), ALU.mult)
                dve.tensor_tensor(k_dst, k_src, t_odd.to_broadcast([P, nb, m]), ALU.mult)
                dve.tensor_tensor(tot[lvl].rearrange("p (b m) -> p b m", m=1), t_even, t_odd, ALU.mult).then_inc(sem["hg_lvl"], 1)

            def masked(r, lvl):
                dve.wait_ge(sem["hg_qk"], count("hg_qk", r, lvl))
                if lvl:
                    dve.wait_ge(sem["hg_masked"], count("hg_masked", r, lvl - 1))
                if lvl < 7:
                    m = 1 << lvl
                    _, dst = halves(attn, m)
                    mask = hg_mask[:, lvl, :].rearrange("p (b m) -> p b m", m=m)
                    _, src = halves(bank[2 + lvl % 2], m)
                    masked_copy(dst, mask, src).then_inc(sem["hg_masked"], 1)
                else:
                    masked_copy(attn, diag_mask, H1[:, :]).then_inc(sem["hg_masked"], 1)

            def states(r):
                dve.wait_ge(sem["hg_kv"], count("hg_kv", r))
                dve.tensor_copy(h_state[:, 0:P], H0[:, 0:P]).then_inc(sem["hg_state"], 1)
                for c in range(1, CH - 1):
                    dve.wait_ge(sem["hg_state"], count("hg_state", r, c - 1))
                    stt(h_state[:, c * P:(c + 1) * P], h_state[:, (c - 1) * P:c * P], tot[7][:, c:c + 1],
                               H0[:, c * P:(c + 1) * P], ALU.mult, ALU.add).then_inc(sem["hg_state"], 1)

            def head_out(r):
                dve.wait_ge(sem["hg_rstd"], count("hg_rstd", r))
                stt(sig_b, H1[:, :], cur_e[:, HG_G:HG_G + 1], sig_b, ALU.mult, ALU.mult).then_inc(sem["hg_n"], 1)
                dve.wait_ge(sem["hg_n"], count("hg_n", r))
                dve.tensor_tensor(y[:, r, :] if isinstance(r, int) else y[:, bass.ds(r, 1), :].rearrange("p a t -> p (a t)"),
                                         sig_b, g_a, ALU.mult).then_inc(sem["hg_y"], 1)

            def decay_sums(r):
                dve.wait_ge(sem["rw_sw"], count("rw_sw", r))
                if not is_first(r):
                    dve.wait_ge(sem["rw_rho"], count("rw_rho", r - 1))
                dve.memset(cum[:, :, 0:1], 0.0).then_inc(sem["rw_prep"], 1)
                for c in range(CH):
                    last = dve.tensor_tensor_scan(out=cum[:, c, 1:L + 1], data0=ones, data1=e_neg[:, c * L:(c + 1) * L],
                                                  initial=0.0, op0=ALU.mult, op1=ALU.add)
                last.then_inc(sem["rw_prep"], 1)
                dve.wait_ge(sem["rw_prep"], count("rw_prep", r, 1))
                dve.tensor_copy(e_mid, cum[:, :, L // 2]).then_inc(sem["rw_prep"], 1)
                dve.wait_ge(sem["rw_prep"], count("rw_prep", r, 2))
                dve.tensor_tensor(cum, cum, e_mid.unsqueeze(2).to_broadcast([P, CH, L + 1]), ALU.subtract).then_inc(sem["rw_center"], 1)
                dve.wait_ge(sem["rw_av"], count("rw_av", r))
                dve.tensor_scalar(t2, w_a, 1.0, cur_r[:, K_A:K_A + 1], ALU.subtract, ALU.mult).then_inc(sem["rw_prep"], 1)
                dve.wait_ge(sem["rw_prep"], count("rw_prep", r, 3))
                stt(k_t, t2, 1.0, wk, ALU.add, ALU.mult).then_inc(sem["rw_prep"], 1)
                dve.wait_ge(sem["rw_prep"], count("rw_prep", r, 4))
                stt(t2, wr, cur_r[:, R_K:R_K + 1], k_t, ALU.mult, ALU.mult).then_inc(sem["rw_rk"], 1)

            def key_norm(r):
                dve.wait_ge(sem["rw_ssq"], count("rw_ssq", r))
                dve.tensor_scalar(t1, R2[:, :], 1e-24, float(2 ** 40), ALU.max, ALU.mult).then_inc(sem["rw_m1"], 1)
                dve.wait_ge(sem["rw_bon"], count("rw_bon", r))
                dve.tensor_tensor(w_bonus, R3[:, :], wv, ALU.mult).then_inc(sem["rw_bonus"], 1)

            def operands(r):
                chunks = lambda ap: ap.rearrange("p (c t) -> p c t", c=CH)
                dve.wait_ge(sem["rw_rn"], count("rw_rn", r))
                stt(t1, wk, cur_r[:, K_K:K_K + 1], t1, ALU.mult, ALU.mult).then_inc(sem["rw_kk"], 1)
                dve.wait_ge(sem["rw_kk"], count("rw_kk", r, 0))
                dve.tensor_tensor(b_t, t1, w_a, ALU.mult).then_inc(sem["rw_kk"], 1)
                dve.wait_ge(sem["rw_kk"], count("rw_kk", r, 1))
                dve.wait_ge(sem["rw_exp"], count("rw_exp", r, 2))
                first, second = slice(0, 64), slice(64, P)
                stt(ar[first, :, 0, 0, :], chunks(t1[first]), -1.0, e_pos[first, :, 0:L], ALU.mult, ALU.mult)
                stt(ar[second, :, 1, 0, :], chunks(t1[second]), -1.0, e_pos[second, :, 0:L], ALU.mult, ALU.mult).then_inc(sem["rw_ops"], 1)
                dve.tensor_tensor(ar[first, :, 0, 1, :], chunks(wr[first]), e_pos[first, :, 1:L + 1], ALU.mult)
                dve.tensor_tensor(ar[second, :, 1, 1, :], chunks(wr[second]), e_pos[second, :, 1:L + 1], ALU.mult).then_inc(sem["rw_ops"], 1)
                dve.tensor_tensor(b_t, b_t, e_neg, ALU.mult).then_inc(sem["rw_ops"], 1)
                dve.tensor_tensor(k_t, k_t, e_neg, ALU.mult).then_inc(sem["rw_ops"], 1)
                dve.tensor_tensor(rho[:, 0:3], e_pos[:, 0:3, L], e_mid[:, 1:4], ALU.mult).then_inc(sem["rw_rho"], 1)

            def matrices(r):
                dve.wait_ge(sem["rw_reset"], count("rw_reset", r))
                for e in range(2):
                    dve.wait_ge(sem["rw_nat"], count("rw_nat", r, e))
                    even = lambda ap: ap.rearrange("p c (b two) -> p c b two", two=2)[:, :, :, 0]
                    masked_copy(even(inv[:, :, e, :]), nat_mask[:, 0, 0:64].unsqueeze(1).to_broadcast([P, CH, 64]),
                                       even(bank[6 + e].rearrange("p (c t) -> p c t", c=CH))).then_inc(sem["rw_init"], 1)
                by_head = lambda ap: ap.rearrange("p (e s t) -> p e s t", e=2, s=2)
                odd = lambda ap: ap.rearrange("p e (b two) -> p e b two", two=2)[:, :, :, 1]
                for c in range(CH):
                    for k in range(2):
                        n = 2 * c + k
                        dve.wait_ge(sem["rw_qk"], count("rw_qk", r, n))
                        last = masked_copy(rw_m[:, c, :, 2 * k:2 * k + 2, :], m4_mask, by_head(bank[4 + k]))
                        if k == 0:
                            last = masked_copy(odd(inv[:, c, 2:4, :]), hg_mask[:, 0, 0:64].unsqueeze(1).to_broadcast([P, 2, 64]),
                                               odd(by_head(bank[4])[:, :, 0, :]))
                        last.then_inc(sem["rw_masked"], 1)

            def inverse(r, lvl):
                m = 1 << lvl
                for c in range(CH):
                    n = (lvl - 1) * CH + c
                    o = bank[6 + c % 2]
                    dve.wait_ge(sem["rw_n"], count("rw_n", r, n))
                    if lvl < 6:
                        blocks = lambda ap: ap.rearrange("p (b m) -> p b m", m=m)
                        masked_copy(halves(inv[:, c, 0:2, :].rearrange("p e t -> p (e t)"), m)[0],
                                    blocks(nat_mask[:, lvl, :]), halves(o[:, 0:2 * P], m)[0]).then_inc(sem["rw_x"], 1)
                    else:
                        dve.tensor_copy(inv[0:64, c, 2:4, 64:P], o[0:64, 0:P].rearrange("p (e t) -> p e t", e=2)).then_inc(sem["rw_x"], 1)

            def state(r, c):
                dve.wait_ge(sem["rw_st"], count("rw_st", r, c))
                if c == 0:
                    if not is_first(r):
                        dve.wait_ge(sem["rw_yc"], count("rw_yc", r - 1, 3))
                    dve.tensor_copy(w_state[:, 0, :], R3[:, 0:64]).then_inc(sem["rw_sadd"], 1)
                else:
                    dve.wait_ge(sem["rw_s"], count("rw_s", r, c - 1))
                    if c == 2:
                        dve.wait_ge(sem["rw_yc"], count("rw_yc", r, 1))
                    dve.tensor_tensor(s_sum, R3[:, 0:64], w_state[:, c % 2, :], ALU.add).then_inc(sem["rw_sadd"], 1)
                dve.wait_ge(sem["rw_sadd"], count("rw_sadd", r, c))
                src = w_state[:, 0, :] if c == 0 else s_sum
                dve.tensor_scalar(w_state[:, (c + 1) % 2, :], src, rho[:, c:c + 1], None, ALU.mult).then_inc(sem["rw_s"], 1)

            def pair_out(r):
                dve.wait_ge(sem["rw_mean"], count("rw_mean", r))
                stt(b_t, R0[:, :], -1.0 / 64, b_t, ALU.mult, ALU.add).then_inc(sem["rw_d"], 1)
                dve.wait_ge(sem["rw_rstd"], count("rw_rstd", r))
                dve.tensor_tensor(b_t, b_t, t1, ALU.mult).then_inc(sem["rw_norm"], 1)
                dve.wait_ge(sem["rw_norm"], count("rw_norm", r, 0))
                stt(b_t, b_t, cur_r[:, LN_G:LN_G + 1], w_bonus, ALU.mult, ALU.add).then_inc(sem["rw_norm"], 1)
                dve.wait_ge(sem["rw_norm"], count("rw_norm", r, 1))
                stt(y[:, KC + r, :] if isinstance(r, int) else y[:, bass.ds(r + KC, 1), :].rearrange("p a t -> p (a t)"),
                           b_t, cur_r[:, LN_B:LN_B + 1], g_b, ALU.add, ALU.mult).then_inc(sem["rw_y"], 1)

            def even_round(i, head=True, pair=True):
                r = i - 1
                if pair:
                    if not is_first(r):
                        dve.wait_ge(sem["rw_y"], count("rw_y", r - 1))
                    dve.tensor_copy(cur_r, ev[:, :, r] if isinstance(r, int) else ev[:, :, bass.ds(r, 1)].rearrange("p k a -> p (k a)")).then_inc(sem["cur_r"], 1)
                if head:
                    if not is_first(i):
                        dve.wait_ge(sem["hg_y"], count("hg_y", i - 1))
                    dve.tensor_copy(cur_e, ev[:, :, i] if isinstance(i, int) else ev[:, :, bass.ds(i, 1)].rearrange("p k a -> p (k a)")).then_inc(sem["cur_e"], 1)
                    dve.wait_ge(sem["cur_e"], count("cur_e", i))
                if is_first(i):
                    dve.wait_ge(sem["lr_shift"], count("lr_shift", 0))
                    stt(lr, bank[0][:, :], mu_lr[:, 2:3], shift[:, 0:T], ALU.mult, ALU.add).then_inc(sem["free0"], 1)
                else:
                    gated(i, 0, "sig_gb", sig_a, g_b)
                if pair:
                    decay_sums(r)
                if head:
                    gated(i, 1, "sig_q", sig_b, hq)
                if pair:
                    key_norm(r)
                if head:
                    dve.wait_ge(sem["free0"], count("free0", i, 1))
                    if not is_first(i):
                        dve.wait_ge(sem["hg_sq"], count("hg_sq", i - 1))
                        dve.wait_ge(sem["hg_ssq"], count("hg_ssq", i - 1))
                    dve.tensor_scalar(hf, sig_a, cur_e[:, OLB:OLB + 1], cur_e[:, LB:LB + 1], ALU.mult, ALU.add).then_inc(sem["fk"], 1)
                    dve.tensor_scalar(hk, sig_b, cur_e[:, OLB:OLB + 1], None, ALU.mult).then_inc(sem["fk"], 1)
                    gated(i, 3, "sig_ga", sig_a, g_a)
                if pair:
                    operands(r)
                if head:
                    level(i, 0)
                    level(i, 1)
                if pair:
                    matrices(r)
                    for lvl in range(1, 7):
                        inverse(r, lvl)
                    state(r, 0)
                if head:
                    mixed(i, 0, 5, wr)
                    masked(i, 0)
                    masked(i, 1)
                    level(i, 2)
                    level(i, 3)
                if pair:
                    state(r, 1)
                if head:
                    mixed(i, 1, 6, wk)
                    masked(i, 2)
                    masked(i, 3)
                    level(i, 4)
                    level(i, 5)
                if pair:
                    state(r, 2)
                if head:
                    mixed(i, 2, 7, wv)
                    masked(i, 4)
                    masked(i, 5)
                    level(i, 6)
                    masked(i, 6)
                    level(i, 7)
                    masked(i, 7)
                    states(i)
                if pair:
                    pair_out(r)
                if head:
                    head_out(i)

            even_round(0, pair=False)
            even_round(1)
            with dve.Fori(2, EV_ROUNDS) as i:
                even_round(i)
            even_round(EV_ROUNDS, head=False)

            def split_outputs(n_chunks, y_from):
                for c in range(n_chunks):
                    dve.wait_ge(sem["y_hi"], count("y_hi", 0, y_from + c))
                    dve.tensor_tensor(h_split[:, KC + c % 6, :], y[:, c, :], h_split[:, c % 6, :].bitcast(F32), ALU.subtract).then_inc(sem["y_split"], 1)

            def split_embedding(layer):
                for c in range(2):
                    dve.wait_ge(sem["p_hi"], count("p_hi", layer, c))
                    dve.tensor_tensor(h_split[:, KC + 6 + c, :], p_raw[:, c, :], h_split[:, 6 + c, :].bitcast(F32),
                                             ALU.subtract).then_inc(sem["p_ready"], 1)

            def add_outputs(stage, unit_end):
                dve.wait_ge(sem["units_done"], unit_end)
                for n in range(KC):
                    dve.tensor_tensor(x[:, n, :], x[:, n, :], bank[n][:, :], ALU.add).then_inc(sem["x_added"], 1)

            def ple(stage, g):
                normed(stage, g, hn)
                for n in range(KC):
                    dve.wait_ge(sem["gate_sig"], count("gate_sig", stage // 2, n))
                    dve.tensor_tensor(prj[:, n, :], prj[:, n, :], sg[:, n % 2, :], ALU.mult).then_inc(sem["gate_mul"], 1)
                    dve.wait_ge(sem["gate_mul"], count("gate_mul", stage // 2, n))
                    dve.tensor_tensor(x[:, n, :], x[:, n, :], prj[:, n, :], ALU.add).then_inc(sem["x_added"], 1)

            split_embedding(0)
            split_outputs(2 * KC, 0)
            dve.wait_ge(x_again, 16)
            add_outputs(0, U_PRJ0)
            ple(1, 1)
            normed(2, 2, hn)
            dve.memset(mq[64:P, 0, :], 0.0)
            dve.memset(mq[0:64, 1, :], 0.0)
            dve.memset(xd[:, :, 0:3], 0.0).then_inc(sem["conv_pad"], 1)

            def attend(i, n):
                w = (n % CH + 1) * L
                dve.wait_ge(sem["mo_s"], count("mo_s", i, n))
                dve.reduce_max(m_stat[:, 0, n:n + 1], bank[2 + n % 2][:, 0:w], axis=mybir.AxisListType.X).then_inc(sem["mo_max"], 1)
                dve.wait_ge(sem["mo_max"], count("mo_max", i, n))
                dve.tensor_scalar(m_stat[:, 1, n:n + 1], m_stat[:, 0, n:n + 1], -0.125, None, ALU.mult).then_inc(sem["mo_neg"], 1)

            def normalise(i, n):
                w = (n % CH + 1) * L
                dve.wait_ge(sem["mo_exp"], count("mo_exp", i, n))
                dve.reciprocal(m_stat[:, 2, n:n + 1], m_sum[:, n:n + 1]).then_inc(sem["mo_inv"], 1)
                dve.wait_ge(sem["mo_inv"], count("mo_inv", i, n))
                dve.tensor_scalar(prob[:, n % 2, 0:w], prob[:, n % 2, 0:w], m_stat[:, 2, n:n + 1], None, ALU.mult).then_inc(sem["mo_p"], 1)

            def convolve(i, b, k):
                if k == 0:
                    dve.wait_ge(sem["conv_pad"], count("conv_pad", 0))
                    dve.wait_ge(sem["ofree0"], count("ofree0", i, 2 * b))
                    if not is_first(i):
                        dve.wait_ge(sem["ru_ix"], count("ru_ix", i - 1, b))
                    dve.tensor_scalar(xc[:, b, :], xd[:, b, 0:T], cur_o[:, CW0, b:b + 1], cur_o[:, CONV_B, b:b + 1], ALU.mult,
                                      ALU.add).then_inc(sem["ru_conv"], 1)
                else:
                    dve.wait_ge(sem["ru_conv"], count("ru_conv", i, 4 * b + k - 1))
                    stt(xc[:, b, :], xd[:, b, k:k + T], cur_o[:, CW0 + k, b:b + 1], xc[:, b, :], ALU.mult, ALU.add).then_inc(sem["ru_conv"], 1)

            def gate_tile(i, n, j):
                tile_done(i, j, U_ODD)
                dve.tensor_copy(og[:, n, :], bank[j % 2][:, :]).then_inc(sem[f"ofree{j % 2}"], 1)

            def gate(i, n):
                dve.wait_ge(sem["o_sig"], count("o_sig", i, n))
                dve.tensor_tensor(og[:, n, :], og[:, n, :], osig[:, n, :], ALU.mult).then_inc(sem["o_gate"], 1)

            def row(base, r, step=1):
                return y[:, base + r * step, :] if isinstance(r, int) else y[:, bass.ds(r * step + base, 1), :].rearrange("p a t -> p (a t)")

            def odd_round(i):
                if not is_first(i):
                    dve.wait_ge(sem["ru_y"], count("ru_y", i - 1, 1))
                dve.tensor_copy(cur_o, od[:, :, bass.ds(i * 2, 2)]).then_inc(sem["cur_o"], 1)
                dve.wait_ge(sem["cur_o"], count("cur_o", i))
                for k in range(4):
                    convolve(i, 0, k)
                tile_done(i, 2, U_ODD)
                dve.tensor_copy(mk, bank[0][:, :]).then_inc(sem["ofree0"], 1)
                attend(i, 0)
                attend(i, 1)
                for n in range(2 * CH):
                    normalise(i, n)
                    if n + 2 < 2 * CH:
                        attend(i, n + 2)
                    if 2 <= n < 6:
                        convolve(i, 1, n - 2)
                    if n == 3:
                        gate_tile(i, 0, 5)
                    if n == 5:
                        gate_tile(i, 1, 6)
                gate_tile(i, 2, 7)
                for b in range(2):
                    dve.wait_ge(sem["ru_i"], count("ru_i", i, b))
                    dve.tensor_tensor(u_i[b], u_i[b], xc[:, b, :], ALU.mult).then_inc(sem["ru_ix"], 1)
                for b in range(2):
                    dve.wait_ge(sem["ru_th"], count("ru_th", i, b))
                    dve.tensor_scalar(u_2[b], u_th[b], float(2.0 ** -103), float(2.0 ** 41), ALU.max, ALU.mult).then_inc(sem["ru_clamp"], 1)
                gate(i, 0)
                dve.wait_ge(sem["mo_pv"], count("mo_pv", i, 7))
                dve.wait_ge(sem["o_gate"], count("o_gate", i, 0))
                dve.tensor_tensor(row(0, i), bank[5][:, :], og[:, 0, :], ALU.mult).then_inc(sem["mo_y"], 1)
                gate(i, 1)
                gate(i, 2)
                for b in range(2):
                    dve.wait_ge(sem["ru_u2"], count("ru_u2", i, b))
                    dve.tensor_tensor(u_2[b], u_2[b], u_1[b], ALU.subtract).then_inc(sem["ru_d"], 1)
                for b in range(2):
                    dve.wait_ge(sem["ru_e"], count("ru_e", i, b))
                    dve.tensor_tensor(u_2[b], u_2[b], u_i[b], ALU.mult).then_inc(sem["ru_b"], 1)
                    dve.wait_ge(sem["ru_b"], count("ru_b", i, b))
                    dve.tensor_tensor_scan(out=u_th[b], data0=u_r[b], data1=u_2[b], initial=0.0, op0=ALU.mult,
                                           op1=ALU.add).then_inc(sem["ru_h"], 1)
                    dve.wait_ge(sem["ru_h"], count("ru_h", i, b))
                    dve.wait_ge(sem["o_gate"], count("o_gate", i, 1 + b))
                    dve.tensor_tensor(row(4 + b, i, 2), u_th[b], og[:, 1 + b, :], ALU.mult).then_inc(sem["ru_y"], 1)

            odd_round(0)
            with dve.Fori(1, OD_ROUNDS) as i:
                odd_round(i)
            split_embedding(1)
            split_outputs(4 + KC, 2 * KC)
            add_outputs(2, U_PRJ1)
            ple(3, 3)
            normed(4, 4, prj)


def kernel(**inputs):
    import concourse.bacc as bacc
    from concourse.bass_utils import run_bass_kernel_spmd as run

    a = {n: np.asarray(v) for n, v in inputs.items()}

    def units(w):
        k, n = w.shape
        return w.reshape(k // P, P, n // P, P).transpose(0, 2, 1, 3)

    def pack(blocks):
        b = np.stack(blocks)
        return b.reshape(-1, 4, P, P).transpose(0, 2, 1, 3).reshape(-1, P, 4 * P)

    def column_tiles(w, tiles):
        u = units(w)
        return pack([u[k, n] for n in tiles for k in range(KC)])

    w_in = a["ev_w_in"][0]
    za, zr, gates = 0, 24, 49
    order = [zr + 24]
    for i in range(EV_ROUNDS + 1):
        if i:
            order.append(gates + 8 + i - 1)
        if i < EV_ROUNDS:
            order += [za + i, za + 8 + i, gates + i, za + 16 + i, zr + i, zr + 8 + i, zr + 16 + i]
    od_order = []
    for i in range(OD_ROUNDS):
        od_order += [12 + 2 * i, i, 4 + i, 8 + i, 13 + 2 * i, 20 + i, 24 + 2 * i, 25 + 2 * i]

    def rows(w):
        u = units(w)
        return pack([u[k, n] for k in range(u.shape[0]) for n in range(u.shape[1])])

    def by_output(w):
        u = units(w)
        return pack([u[k, n] for n in range(u.shape[1]) for k in range(u.shape[0])])

    wall = np.concatenate([
        column_tiles(w_in, order), rows(a["ev_w_out"][0]), by_output(a["ple_proj"][0]), rows(a["ple_gate"][0]),
        column_tiles(a["od_w_in"][0], od_order), rows(a["od_w_out"][0]), by_output(a["ple_proj"][1]), rows(a["ple_gate"][1]),
    ])
    assert wall.shape[0] == N_UNITS

    def cols(v):
        return v.reshape(-1, P).T

    mu = a["rw_mu"][0]
    par_e = np.zeros((P, N_EV + 1, 8), np.float32)
    for n, v in enumerate((mu[0:1024], mu[1024:2048], mu[2048:3072], a["rw_w0"][0], a["rw_a0"][0], a["rw_k_k"][0],
                           a["rw_k_a"][0], a["rw_r_k"][0], a["rw_ln_g"][0], a["rw_ln_b"][0], a["hg_lb_logits"][0],
                           a["hg_norm"][0])):
        par_e[:, n, :] = cols(v)
    par_e[:, N_EV, 0] = mu[3072:]
    par_o = np.zeros((P, N_OD, 8), np.float32)
    for n, v in enumerate((*a["lru_conv_w"][0], a["lru_conv_b"][0], a["lru_ba"][0], a["lru_bx"][0], a["lru_lambda"][0])):
        par_o[:, n, :] = cols(v)
    gains = np.stack([cols(v) for v in (a["ev_norm"][0], a["ple_norm"][0], a["od_norm"][0], a["ple_norm"][1],
                                        a["final_norm"])], axis=1)
    w2a2 = np.concatenate([a["rw_w2"][0], a["rw_a2"][0]]).reshape(P, 8, P).transpose(1, 0, 2)
    lru_w = np.stack([a["lru_wa"][0], a["lru_wx"][0]], axis=1).reshape(OD_ROUNDS, 4, P, P).transpose(0, 2, 1, 3)

    t = np.arange(P)
    m8 = np.zeros((P, N_MASK), np.float32)
    for lvl in range(LEVELS):
        m = 1 << lvl
        blocks = t.reshape(-1, 2, m)
        even, odd = blocks[:, 0].ravel(), blocks[:, 1].ravel()
        pairs = (t[:, None] // (2 * m) == odd[None] // (2 * m)) & (t[:, None] % (2 * m) < m)
        m8[:, lvl * 256:(lvl + 1) * 256] = np.tile(pairs, (1, 4))
        if lvl < 6:
            pairs = (t[:, None] // (2 * m) == even[None] // (2 * m)) & (t[:, None] % (2 * m) >= m)
            m8[:, 2816 + lvl * P:2816 + (lvl + 1) * P] = np.tile(pairs, (1, 2))
    m8[:, 1792:2304] = np.tile(np.eye(P), (1, 4))
    before, upto = t[:, None] < t[None], t[:, None] <= t[None]
    m8[:, 2304:2816] = np.concatenate([before, upto, before, upto], axis=1)
    fc = np.zeros((P, 4, P), np.float32)
    fc[:, 0] = np.eye(P)
    fc[:, 1] = 1.0
    fc[:, 2] = t[:, None] // 64 == t[None] // 64
    fc[:, 3] = np.where(t[:, None] < t[None], -1e30, 0.0)

    arrays = {
        "xT": a["x"][0].T.reshape(KC, P, T).transpose(1, 0, 2),
        "pT": a["p"][:, 0].transpose(0, 2, 1).reshape(2, 2, P, T).transpose(0, 2, 1, 3),
        "wall": wall, "par_e": par_e, "par_o": par_o, "gains": gains, "w2a2": w2a2, "lru_w": lru_w,
        "mask_f32": m8, "const_f32": fc,
    }
    arrays = {n: np.ascontiguousarray(v) for n, v in arrays.items()}
    nc = bacc.Bacc("TRN2", target_bir_lowering=False, num_devices=1)
    d = {n: nc.dram_tensor(n, v.shape, mybir.dt.from_np(v.dtype), kind="ExternalInput").ap() for n, v in arrays.items()}
    out = nc.dram_tensor("out", (P, KC, T), F32, kind="ExternalOutput").ap()
    trunk(nc, d["xT"], d["pT"], d["wall"], d["par_e"], d["par_o"], d["gains"], d["w2a2"], d["lru_w"],
          (d["mask_f32"], d["const_f32"]), out)
    r = run(nc, [arrays], core_ids=[0])
    return r.results[0]["out"].transpose(1, 0, 2).reshape(D, T).T.reshape(1, T, D)
```

```python
from contextlib import ExitStack

import numpy as np
import concourse.bass as bass
from concourse import mybir

F32 = mybir.dt.float32
F32R = mybir.dt.float32r
U8 = mybir.dt.uint8
ALU = mybir.AluOpType
ACT = mybir.ActivationFunctionType

T = 512
D = 1024
P = 128
KC = D // P
CH = 4
L = T // CH
EPS = 1e-6
LN_EPS = 64e-5
KAPPA = float(np.exp(-0.5))
LN2 = float(np.log(2.0))
EV_ROUNDS = 8
OD_ROUNDS = 4
TILES = 8
LEVELS = 7
N_MASK = LEVELS * 2 * P + T + 4 * P + (LEVELS - 1) * P

EV_UNITS = 2 * (TILES * EV_ROUNDS + 1)
U_PRJ0 = EV_UNITS
U_OUT0 = U_PRJ0 + 4
U_GAT0 = U_OUT0 + 4 * KC
U_PRJ1 = U_GAT0 + 2 * KC
U_ODD = U_PRJ1 + 4
U_OUT1 = U_ODD + 2 * TILES * OD_ROUNDS
U_GAT1 = U_OUT1 + 3 * KC
N_UNITS = U_GAT1 + 2 * KC
ODD_OUTPUTS = (0, 1, 2, 4, 5, 6, 7, 8, 9, 3, 10, 11)
SLOTS = 4

(MU_R, MU_K, MU_V, W0, A0, K_K, K_A, R_K, LN_G, LN_B, LB_LOGIT, HG_G,
 OMU_R, OMU_K, OMU_V, LB, OLB) = range(17)
N_EV, N_EVP = 12, 17
CW0, CW1, CW2, CW3, CONV_B, BA, BX, LAM, CNEG, CPOS = range(10)
N_OD, N_ODP = 8, 10


PER_ROUND = dict(
    w_hi=1, w_ready=1, units_done=1,
    x_added=8, sq_ready=8, sq_summed=7, sq_used=1, ln_done=1, rstd=1, hn_ready=8, hi_ready=8, h_ready=8,
    p_hi=2, p_ready=2, prj_evac=4, gate_z=8, gate_sig=8, gate_mul=8, y_hi=1, y_split=1,
    par_dve=15, par_exp=1, par_lam=4, zeroed=1, masks_set=1, bias_set=4,
    free0=4, free1=4, cur_e=1, cur_r=1, lr_shift=1, lr_ready=1, sig_gb=1, sig_q=1, sig_f=1, fk=2, sig_ga=1, shifted=3,
    hg_lvl=8, hg_even=14, hg_qk=8, hg_masked=8, hg_vt=1, hg_vtok=1, hg_kt=1, hg_ktok=1, hg_kv=1,
    hg_state=3, hg_o=1, hg_sq=1, hg_ssq=1, hg_ln=1, hg_rstd=1, hg_n=1, hg_y=1,
    rw_wx=1, rw_ax=1, rw_sw=1, rw_av=1, rw_ksq=1, rw_ssq=1, rw_prep=5, rw_center=1, rw_rk=1, rw_m1=1, rw_ln=1, rw_rn=1,
    rw_bon=1, rw_bonus=1, rw_exp=3, rw_kk=2, rw_ops=4, rw_rho=1, rw_tr=3, rw_tok=3, rw_reset=1,
    rw_qk=8, rw_first=4, rw_masked=8, rw_init=4, rw_p=24, rw_pev=24, rw_n=24, rw_x=24, rw_t=20, rw_xt=20,
    rw_rhs=4, rw_rhse=4, rw_u=4, rw_ue=4, rw_st=3, rw_sadd=3, rw_s=3, rw_yc=4,
    rw_ysb=1, rw_mean=1, rw_d=1, rw_dsq=1, rw_var=1, rw_lnv=1, rw_rstd=1, rw_norm=2, rw_y=1,
    ofree0=4, ofree1=4, cur_o=1, o_sig=3, o_gate=3, mo_vt=1, mo_vtok=1, mo_s=8, mo_mask=8, mo_max=8, mo_neg=8, mo_exp=8, mo_inv=8, mo_p=8,
    mo_tr=8, mo_pt=8, mo_pv=8, mo_y=1,
    conv_pad=1, ru_conv=8, cneg_set=1, ru_r_mm=2, ru_i_mm=2, ru_r=2, ru_i=2, ru_th=2, ru_clamp=2, ru_a=2, ru_u1=2, ru_u2=2, ru_d=2, ru_e=2,
    ru_ix=2, ru_b=2, ru_h=2, ru_y=2,
)


def count(name, r, j=0):
    value = r * PER_ROUND[name] + j + 1
    assert not isinstance(value, int) or value > 0, (name, r, j)
    return value


def trunk(nc, xT, pT, wall, par_e, par_o, gains, w2a2, lru_w, masks, out):
    ctx = ExitStack()
    with ctx:
        def sb(name, shape, dt=F32):
            return ctx.enter_context(nc.sbuf_tensor(name, shape, dt))

        sem = {n: ctx.enter_context(nc.semaphore(n)) for n in PER_ROUND}
        raw_loaded = [ctx.enter_context(nc.semaphore(f"raw_loaded{i}")) for i in range(SLOTS)]
        x_loaded = [ctx.enter_context(nc.semaphore(f"x_loaded{i}")) for i in range(4)]
        masks_loaded = ctx.enter_context(nc.semaphore("masks_loaded"))
        x_again = ctx.enter_context(nc.semaphore("x_again"))
        const_loaded = ctx.enter_context(nc.semaphore("const_loaded"))
        w2_loaded = ctx.enter_context(nc.semaphore("w2_loaded"))
        lru_loaded = ctx.enter_context(nc.semaphore("lru_loaded"))
        p_loaded = ctx.enter_context(nc.semaphore("p_loaded"))
        stored = ctx.enter_context(nc.semaphore("stored"))
        vector_copies = ctx.enter_context(nc.semaphore("vector_copies"))
        splits = ctx.enter_context(nc.semaphore("splits"))

        w_raw = sb("w_raw", [P, SLOTS, 4 * P])
        w_hi = sb("w_hi", [P, SLOTS, 4, P], F32R)
        w_lo = sb("w_lo", [P, SLOTS, 4, P], F32R)
        h_split = sb("h_split", [P, 2 * KC, T], F32R)
        y = sb("y", [P, 2 * KC, T])
        mix = sb("mix", [P, 28800])
        ev = sb("ev", [P, N_EVP, 8])
        od = sb("od", [P, N_ODP, 8])
        gain = sb("gain", [P, 5, KC])
        par_t = sb("par_t", [P, 3, 8])
        mu_lr = sb("mu_lr", [P, 3])
        bias = sb("bias", [P, 5])
        mask8 = sb("mask8", [P, N_MASK], U8)
        fconst = sb("fconst", [P, 4, P])
        ident, ones, bones, causal = (fconst[:, n, :] for n in range(4))
        psum = ctx.enter_context(nc.psum_tensor("psum", [P, 8, T], F32))
        bank = [psum[:, n, :] for n in range(8)]
        H0, H1, R0, R1, R2, R3 = bank[2:8]

        used = [0]

        def place(width):
            at = used[0]
            used[0] += width
            assert used[0] <= 28800, used[0]
            return mix[:, at:at + width]

        x_at = place(KC * T)
        x = x_at.rearrange("p (c t) -> p c t", c=KC)
        rw_m = x_at.rearrange("p (c e s t) -> p c e s t", c=CH, e=2, s=4)
        start = used[0]
        hq, hk, hf, hv, sig_a, sig_b, g_a = (place(T) for _ in range(7))
        qp = place(4 * T).rearrange("p (r t) -> p r t", r=4)
        kr = place(4 * T).rearrange("p (r t) -> p r t", r=4)
        tot = [hf] + [place(T >> (n + 1)) for n in range(7)]
        attn = place(T)
        h_vtok = place(T)
        h_ktok = hf
        h_state = place(3 * P)
        wr, wk, wv, g_b = (place(T) for _ in range(4))
        shift = place(T + 8)
        t1, t2, w_a = (place(T) for _ in range(3))
        cum = place(CH * (L + 1)).rearrange("p (c t) -> p c t", c=CH)
        e_pos = cum
        e_neg = place(T)
        ar = place(4 * T).rearrange("p (c e s t) -> p c e s t", c=CH, e=2, s=2)
        b_t, k_t, w_bonus = (place(T) for _ in range(3))
        b_tok, k_tok, v_tok = (place(T) for _ in range(3))
        inv = place(CH * T).rearrange("p (c s t) -> p c s t", c=CH, s=4)
        p_full = place(4 * P).rearrange("p (r e t) -> p r e t", r=2, e=2)
        rhs_s = place(2 * P).rearrange("p (r t) -> p r t", r=2)
        u_s = place(2 * P).rearrange("p (r t) -> p r t", r=2)
        w_state = place(2 * 64).rearrange("p (r t) -> p r t", r=2)
        s_sum = place(64)
        e_mid, rho = place(CH), place(CH)
        lr = place(T)
        w2_slot = place(2 * P).rearrange("p (k t) -> p k t", k=2)
        cur_e, cur_r = place(N_EVP), place(N_EVP)
        used[0] = start
        sq = place(2 * T).rearrange("p (r t) -> p r t", r=2)
        hn = place(2 * T).rearrange("p (r t) -> p r t", r=2)
        sq_sum = place(T)
        rstd_s = place(T)
        sg = place(2 * T).rearrange("p (r t) -> p r t", r=2)
        prj = place(KC * T).rearrange("p (c t) -> p c t", c=KC)
        masks_in = prj.rearrange("p c t -> p (c t)")[:, 0:N_MASK]
        p_raw = place(2 * T).rearrange("p (c t) -> p c t", c=2)
        mq = place(2 * T).rearrange("p (e t) -> p e t", e=2)
        mk, mv, m_vtok = (place(T) for _ in range(3))
        prob = place(2 * T).rearrange("p (r t) -> p r t", r=2)
        prob_t = place(2 * T).rearrange("p (r t) -> p r t", r=2)
        m_stat = place(3 * 8).rearrange("p (k t) -> p k t", k=3)
        m_sum = place(8)
        og = place(3 * T).rearrange("p (r t) -> p r t", r=3)
        osig = place(3 * T).rearrange("p (r t) -> p r t", r=3)
        xd = place(2 * (T + 8)).rearrange("p (r t) -> p r t", r=2)
        xc = place(2 * T).rearrange("p (r t) -> p r t", r=2)
        u_r, u_i, u_th, u_1, u_2 = ((place(T), place(T)) for _ in range(5))
        lru_slot = place(4 * P).rearrange("p (k t) -> p k t", k=4)
        cneg = place(2)
        cur_o = place(2 * N_ODP).rearrange("p (k b) -> p k b", b=2)

        hg_mask = mask8[:, 0:7 * 256].rearrange("p (l t) -> p l t", l=7)
        diag_mask = mask8[:, 1792:2304]
        m4_mask = mask8[:, 2304:2816].rearrange("p (e s t) -> p e s t", e=2, s=2)
        nat_mask = mask8[:, 2816:3584].rearrange("p (l t) -> p l t", l=6)

        def halves(ap, m):
            v = ap.rearrange("p (b two m) -> p b two m", two=2, m=m)
            return v[:, :, 0, :], v[:, :, 1, :]

        p_slot = (6, 2)

        block = ctx.enter_context(nc.Block())

        @block.sync
        def _(sp):
            sp.dma_start(fconst[:, :, :], masks[1]).then_inc(const_loaded, 16)
            sp.dma_start(ev[:, 0:N_EV, :], par_e[:, 0:N_EV, :]).then_inc(const_loaded, 16)
            sp.dma_start(od[:, 0:N_OD, :], par_o).then_inc(const_loaded, 16)
            sp.dma_start(gain[:, :, :], gains).then_inc(const_loaded, 16)
            sp.dma_start(mu_lr[:, 0:2], par_e[:, N_EV, 0:2]).then_inc(const_loaded, 16)
            for n in range(4):
                sp.dma_start(x[:, 2 * n:2 * n + 2, :], xT[:, 2 * n:2 * n + 2, :]).then_inc(x_loaded[n], 16)

            def load_unit(g, slot):
                sp.dma_start(w_raw[:, slot, :], wall[bass.ds(g * SLOTS + slot, 1), :, :]).then_inc(raw_loaded[slot], 16)

            for slot in range(SLOTS):
                load_unit(0, slot)
            sp.dma_start(masks_in, masks[0]).then_inc(masks_loaded, 16)
            with sp.Fori(1, N_UNITS // SLOTS) as g:
                for slot in range(SLOTS):
                    sp.wait_ge(sem["w_ready"], count("w_ready", g * SLOTS + slot - SLOTS))
                    load_unit(g, slot)
            for slot in range(N_UNITS % SLOTS):
                g = N_UNITS // SLOTS
                sp.wait_ge(sem["w_ready"], count("w_ready", (g - 1) * SLOTS + slot))
                load_unit(g, slot)
            for c in range(KC):
                sp.wait_ge(sem["hn_ready"], count("hn_ready", 4, c))
                sp.dma_start(out[:, c, :], prj[:, c, :]).then_inc(stored, 16)
            sp.wait_ge(stored, 16 * KC)

        @block.gpsimd
        def _(pool):
            def split_unit(g, slot, first=False):
                u = g * SLOTS + slot
                pool.wait_ge(raw_loaded[slot], 16 * (g + 1))
                if not first:
                    pool.wait_ge(sem["units_done"], count("units_done", u - SLOTS))
                pool.sem_inc(splits, 1)
                pool.tensor_scalar(w_hi[:, slot, :, :], w_raw[:, slot, :], 1.0, 0.0, ALU.mult, ALU.add).then_inc(sem["w_hi"], 1)
                pool.wait_ge(sem["w_hi"], count("w_hi", u))
                pool.tensor_tensor(w_lo[:, slot, :, :], w_raw[:, slot, :],
                                          w_hi[:, slot, :, :].bitcast(F32).rearrange("p k n -> p (k n)"), ALU.subtract).then_inc(sem["w_ready"], 1)

            for slot in range(SLOTS):
                split_unit(0, slot, first=True)
            with pool.Fori(1, N_UNITS // SLOTS) as g:
                for slot in range(SLOTS):
                    split_unit(g, slot)
            for slot in range(N_UNITS % SLOTS):
                split_unit(N_UNITS // SLOTS, slot)

        @block.tensor
        def _(pe):
            def mm(o, lhsT, rhs, start=True, stop=True):
                return pe.matmul(o, lhsT, rhs, start=start, stop=stop, skip_group_check=True)

            def split_products(o, slot, j, hi, lo, start, stop):
                mm(o, w_hi[:, slot, j, :], hi, start, False)
                mm(o, w_hi[:, slot, j, :], lo, False, False)
                return mm(o, w_lo[:, slot, j, :], hi, False, stop)

            def half_tile(r, j, half, unit0, free, first_free, stage=None):
                o = bank[j % 2][:, :]
                if half == 0 and not first_free:
                    pe.wait_ge(sem[f"{free}{j % 2}"], count(f"{free}{j % 2}", r, j // 2 - 1))
                slot = (unit0 + 2 * j + half) % SLOTS
                pe.wait_ge(sem["w_ready"], r * 2 * TILES + unit0 + 2 * j + half + 1)
                for k in range(4):
                    c = 4 * half + k
                    if stage is not None:
                        pe.wait_ge(sem["h_ready"], count("h_ready", stage, c))
                    last = split_products(o, slot, k, h_split[:, c, :], h_split[:, KC + c, :], c == 0, c == KC - 1)
                last.then_inc(sem["units_done"], 1)

            def tile(r, j, unit0, free, first_free, stage=None):
                half_tile(r, j, 0, unit0, free, first_free, stage)
                half_tile(r, j, 1, unit0, free, first_free, stage)

            def sumsq(stage, o):
                pe.wait_ge(sem["sq_summed"], count("sq_summed", stage, 6))
                mm(o, ones, sq_sum).then_inc(sem["sq_used"], 1)

            pe.wait_ge(const_loaded, 80)
            sumsq(0, R3)

            def embed(layer, m, unit0, banks):
                pe.wait_ge(sem["p_ready"], count("p_ready", layer, 1))
                pe.wait_ge(sem["w_ready"], count("w_ready", unit0 + m))
                for n in range(2):
                    for c in range(2):
                        last = split_products(bank[banks[n]], (unit0 + m) % SLOTS, 2 * n + c, h_split[:, p_slot[layer] + c, :],
                                              h_split[:, KC + p_slot[layer] + c, :], c == 0, c == 1)
                last.then_inc(sem["units_done"], 1)

            def low_rank(r):
                pe.wait_ge(w2_loaded, (r + 1) * 32)
                if isinstance(r, int) and r == 0:
                    pe.wait_ge(sem["lr_ready"], count("lr_ready", 0))
                    pe.wait_ge(sem["zeroed"], count("zeroed", 0))
                else:
                    pe.wait_ge(sem["rw_d"], count("rw_d", r - 1))
                    pe.wait_ge(sem["rw_lnv"], count("rw_lnv", r - 1))
                mm(R0[:, :], w2_slot[:, 0, :], lr).then_inc(sem["rw_wx"], 1)
                mm(R1[:, :], w2_slot[:, 1, :], lr).then_inc(sem["rw_ax"], 1)

            def key_norm(r):
                pe.wait_ge(sem["rw_ksq"], count("rw_ksq", r))
                if not (isinstance(r, int) and r == 0):
                    pe.wait_ge(sem["rw_ysb"], count("rw_ysb", r - 1))
                mm(R2[:, :], bones, t1).then_inc(sem["rw_ssq"], 1)

            def bonus(r):
                pe.wait_ge(sem["rw_rk"], count("rw_rk", r))
                mm(R3[:, :], bones, t2).then_inc(sem["rw_bon"], 1)

            def transposes(r):
                pe.wait_ge(sem["rw_av"], count("rw_av", r))
                for n, (src, o) in enumerate(((b_t, R0), (k_t, R1), (wv, R2))):
                    if n < 2:
                        pe.wait_ge(sem["rw_ops"], count("rw_ops", r, 2 + n))
                    else:
                        pe.wait_ge(sem["rw_m1"], count("rw_m1", r))
                        pe.wait_ge(sem["rw_bonus"], count("rw_bonus", r))
                    for c in range(CH):
                        last = pe.transpose(o[:, c * L:(c + 1) * L], src[:, c * L:(c + 1) * L], ident)
                    last.then_inc(sem["rw_tr"], 1)

            def inverse_start(r, c):
                pe.wait_ge(sem["rw_masked"], count("rw_masked", r, 2 * c))
                if c == 0:
                    pe.wait_ge(sem["hg_ln"], count("hg_ln", r))
                elif c == 1:
                    pe.wait_ge(sem["hg_n"], count("hg_n", r))
                else:
                    pe.wait_ge(sem["rw_init"], count("rw_init", r, c - 2))
                for e in range(2):
                    last = pe.transpose(bank[2 + c % 2][:, e * P:(e + 1) * P], inv[:, c, 2 + e, :], ident)
                last.then_inc(sem["rw_first"], 1)

            def product(r, n):
                c, k = divmod(n, 2)
                if n < 2:
                    pe.wait_ge(sem["rw_tok"], count("rw_tok", r, n))
                else:
                    pe.wait_ge(sem["rw_masked"], count("rw_masked", r, n - 2))
                keys = b_t if k == 0 else k_t
                mm(bank[4 + k], keys[:, c * L:(c + 1) * L], ar[:, c, :, :, :]).then_inc(sem["rw_qk"], 1)

            def inverse_p(r, lvl, c):
                n, m = (lvl - 1) * CH + c, 1 << lvl
                if lvl == 1:
                    pe.wait_ge(sem["rw_masked"], count("rw_masked", r, 2 * c + 1))
                    pe.wait_ge(sem["rw_init"], count("rw_init", r, c))
                    pe.wait_ge(sem["rw_masked"], count("rw_masked", r, 6 + min(c, 1)))
                else:
                    pe.wait_ge(sem["rw_x"], count("rw_x", r, n - CH))
                if n >= 2:
                    pe.wait_ge(sem["rw_pev"], count("rw_pev", r, n - 2))
                for e in range(2):
                    if lvl < 6:
                        last = mm(bank[4 + c % 2][:, e * P:(e + 1) * P], rw_m[:, c, e, 0, :], inv[:, c, e, :])
                    else:
                        last = mm(bank[4 + c % 2][64:P, e * 64:e * 64 + 64], rw_m[:, c, e, 0, 64:P], inv[:, c, e, 0:64])
                last.then_inc(sem["rw_p"], 1)

            def inverse_n(r, lvl, c):
                n = (lvl - 1) * CH + c
                pe.wait_ge(sem["rw_pev"], count("rw_pev", r, n))
                if n >= 2:
                    pe.wait_ge(sem["rw_x"], count("rw_x", r, n - 2))
                elif n == 0:
                    pe.wait_ge(sem["rw_tok"], count("rw_tok", r, 2))
                if lvl >= 2:
                    pe.wait_ge(sem["rw_xt"], count("rw_xt", r, n - CH))
                o = bank[6 + c % 2]
                for e in range(2):
                    if lvl < 6:
                        last = mm(o[:, e * P:(e + 1) * P], inv[:, c, 2 + e, :], p_full[:, c % 2, e, :])
                    else:
                        last = mm(o[0:64, e * 64:e * 64 + 64], p_full[:, c % 2, e, 0:64], inv[:, c, 2 + e, 64:P])
                last.then_inc(sem["rw_n"], 1)

            def inverse_t(r, lvl, c):
                n = (lvl - 1) * CH + c
                pe.wait_ge(sem["rw_x"], count("rw_x", r, n))
                if n >= 2:
                    pe.wait_ge(sem["rw_xt"], count("rw_xt", r, n - 2))
                else:
                    pe.wait_ge(sem["rw_init"], count("rw_init", r, 2 + n))
                for e in range(2):
                    last = pe.transpose(bank[2 + c % 2][:, e * P:(e + 1) * P], inv[:, c, e, :], ident)
                last.then_inc(sem["rw_t"], 1)

            def inverse(r, lvl):
                inverse_p(r, lvl, 0)
                if lvl > 1:
                    inverse_t(r, lvl - 1, 2)
                inverse_p(r, lvl, 1)
                if lvl > 1:
                    inverse_t(r, lvl - 1, 3)
                inverse_n(r, lvl, 0)
                inverse_p(r, lvl, 2)
                inverse_n(r, lvl, 1)
                if lvl < 6:
                    inverse_t(r, lvl, 0)
                inverse_p(r, lvl, 3)
                inverse_n(r, lvl, 2)
                if lvl < 6:
                    inverse_t(r, lvl, 1)
                inverse_n(r, lvl, 3)

            heads = [(e, slice(64 * e, 64 * e + 64)) for e in range(2)]

            def chain_rhs(r, c):
                if c == 0:
                    pe.wait_ge(sem["rw_pev"], count("rw_pev", r, 23))
                    pe.wait_ge(sem["rw_x"], count("rw_x", r, 23))
                else:
                    pe.wait_ge(sem["rw_ue"], count("rw_ue", r, c - 1))
                if c:
                    pe.wait_ge(sem["rw_s"], count("rw_s", r, c - 1))
                for e, rows in heads:
                    at = slice(c * L + 64 * e, c * L + 64 * e + 64)
                    o = bank[4 + e][:, 0:64]
                    last = mm(o, rw_m[:, c, e, 2, :], v_tok[:, at], True, c == 0)
                    if c:
                        last = mm(o, ar[:, c, e, 0, :], w_state[:, c % 2, :], False, True)
                last.then_inc(sem["rw_rhs"], 1)

            def chain_u(r, c):
                pe.wait_ge(sem["rw_rhse"], count("rw_rhse", r, c))
                for e, rows in heads:
                    last = mm(R0[:, 64 + 64 * e:128 + 64 * e], inv[:, c, 2 + e, :], rhs_s[:, c % 2, rows])
                last.then_inc(sem["rw_u"], 1)

            def chain_out(r, c):
                pe.wait_ge(sem["rw_ue"], count("rw_ue", r, c))
                if c < CH - 1:
                    if c:
                        pe.wait_ge(sem["rw_s"], count("rw_s", r, c - 1))
                    for e, rows in heads:
                        at = slice(c * L + 64 * e, c * L + 64 * e + 64)
                        mm(R3[rows, 0:64], k_tok[:, at], v_tok[:, at], True, False)
                        last = mm(R3[rows, 0:64], b_tok[:, at], u_s[:, c % 2, rows], False, True)
                    last.then_inc(sem["rw_st"], 1)
                for e, rows in heads:
                    at = slice(c * L + 64 * e, c * L + 64 * e + 64)
                    o = R2[rows, c * L:(c + 1) * L]
                    mm(o, v_tok[:, at], rw_m[:, c, e, 3, :], True, False)
                    last = mm(o, u_s[:, c % 2, rows], rw_m[:, c, e, 1, :], False, c == 0)
                    if c:
                        last = mm(o, w_state[:, c % 2, :], ar[:, c, e, 1, :], False, True)
                last.then_inc(sem["rw_yc"], 1)

            def head_mean(r):
                pe.wait_ge(sem["rw_ysb"], count("rw_ysb", r))
                mm(R0[:, :], bones, b_t).then_inc(sem["rw_mean"], 1)

            def head_var(r):
                pe.wait_ge(sem["rw_dsq"], count("rw_dsq", r))
                mm(R1[:, :], bones, k_t).then_inc(sem["rw_var"], 1)

            def hg_values(r):
                pe.wait_ge(sem["free0"], count("free0", r, 2))
                if not (isinstance(r, int) and r == 0):
                    pe.wait_ge(sem["hg_ln"], count("hg_ln", r - 1))
                for c in range(CH):
                    last = pe.transpose(H0[:, c * L:(c + 1) * L], hv[:, c * L:(c + 1) * L], ident)
                last.then_inc(sem["hg_vt"], 1)

            def hg_level(r, lvl):
                o = bank[2 + lvl % 2]
                pe.wait_ge(sem["hg_lvl"], count("hg_lvl", r, lvl))
                if lvl:
                    pe.wait_ge(sem["hg_even"], count("hg_even", r, 2 * lvl - 1))
                if lvl == 0:
                    pe.wait_ge(sem["hg_vtok"], count("hg_vtok", r))
                elif lvl == 1:
                    if not (isinstance(r, int) and r == 0):
                        pe.wait_ge(sem["hg_n"], count("hg_n", r - 1))
                else:
                    pe.wait_ge(sem["hg_masked"], count("hg_masked", r, lvl - 2))
                keys = hk if lvl == 0 else kr[:, lvl % 4, :]
                for c in range(CH):
                    at = slice(c * L, (c + 1) * L)
                    if lvl < LEVELS - 1:
                        last = mm(o[:, at], keys[:, at], qp[:, lvl % 4, at])
                    else:
                        even, odd = slice(c * L, c * L + 64), slice(c * L + 64, (c + 1) * L)
                        last = mm(o[0:64, odd], keys[:, even], qp[:, lvl % 4, odd])
                last.then_inc(sem["hg_qk"], 1)

            def hg_diagonal(r):
                pe.wait_ge(sem["hg_masked"], count("hg_masked", r, 5))
                for c in range(CH):
                    last = mm(H1[:, c * L:(c + 1) * L], hk[:, c * L:(c + 1) * L], hq[:, c * L:(c + 1) * L])
                last.then_inc(sem["hg_qk"], 1)

            def hg_keys(r):
                pe.wait_ge(sem["hg_lvl"], count("hg_lvl", r, 7))
                pe.wait_ge(sem["hg_even"], count("hg_even", r, 13))
                pe.wait_ge(sem["hg_masked"], count("hg_masked", r, 6))
                for c in range(CH - 1):
                    last = pe.transpose(H0[:, c * L:(c + 1) * L], kr[:, 3, c * L:(c + 1) * L], ident)
                last.then_inc(sem["hg_kt"], 1)

            def hg_changes(r):
                pe.wait_ge(sem["hg_ktok"], count("hg_ktok", r))
                for c in range(CH - 1):
                    last = mm(H0[:, c * L:(c + 1) * L], h_ktok[:, c * L:(c + 1) * L], h_vtok[:, c * L:(c + 1) * L])
                last.then_inc(sem["hg_kv"], 1)

            def hg_outputs(r):
                pe.wait_ge(sem["hg_masked"], count("hg_masked", r, 7))
                if not (isinstance(r, int) and r == 0):
                    pe.wait_ge(sem["hg_n"], count("hg_n", r - 1))
                for c in range(CH):
                    at = slice(c * L, (c + 1) * L)
                    mm(H1[:, at], h_vtok[:, at], attn[:, at], c == 0, c == 0)
                for c in range(1, CH):
                    at = slice(c * L, (c + 1) * L)
                    pe.wait_ge(sem["hg_state"], count("hg_state", r, c - 1))
                    last = mm(H1[:, at], h_state[:, (c - 1) * P:c * P], qp[:, 3, at], False, True)
                last.then_inc(sem["hg_o"], 1)

            def hg_norm(r):
                pe.wait_ge(sem["hg_sq"], count("hg_sq", r))
                mm(H0[:, :], ones, hk).then_inc(sem["hg_ssq"], 1)

            def even_round(i, head=True, pair=True):
                r = i - 1
                first = isinstance(i, int) and i == 0

                def t(j, halves=(0, 1)):
                    if head or j == 0:
                        for half in halves:
                            half_tile(i, j, half, 0, "free", first and j < 2, 0 if first and j == 0 else None)

                def level(lvl):
                    if head:
                        hg_level(i, lvl)

                def embedding(m):
                    if not head:
                        if m == 0:
                            pe.wait_ge(sem["free0"], count("free0", EV_ROUNDS, 0))
                            pe.wait_ge(sem["free1"], count("free1", EV_ROUNDS - 1, 3))
                        else:
                            pe.wait_ge(sem["prj_evac"], count("prj_evac", 0, m - 1))
                        embed(0, m, U_PRJ0, (0, 1))

                t(0)
                if pair:
                    low_rank(r)
                t(1)
                if pair:
                    key_norm(r)
                    bonus(r)
                embedding(0)
                t(2)
                t(3)
                if pair:
                    transposes(r)
                    t(4, (0,))
                    for n in range(2 * CH):
                        product(r, n)
                        if n >= 3 and n % 2:
                            inverse_start(r, n // 2 - 1)
                    t(4, (1,))
                    inverse_start(r, 3)
                    for lvl in range(1, 7):
                        inverse(r, lvl)
                    chain_rhs(r, 0)
                    t(5, (0,))
                    chain_u(r, 0)
                    t(5, (1,))
                    chain_out(r, 0)
                else:
                    t(4)
                    t(5)
                embedding(1)
                if head:
                    hg_values(i)
                if pair:
                    chain_rhs(r, 1)
                level(0)
                if pair:
                    chain_u(r, 1)
                level(1)
                if pair:
                    chain_out(r, 1)
                embedding(2)
                t(6)
                if pair:
                    chain_rhs(r, 2)
                level(2)
                if pair:
                    chain_u(r, 2)
                level(3)
                if pair:
                    chain_out(r, 2)
                embedding(3)
                t(7)
                if pair:
                    chain_rhs(r, 3)
                level(4)
                if pair:
                    chain_u(r, 3)
                level(5)
                if pair:
                    chain_out(r, 3)
                level(6)
                if head:
                    hg_diagonal(i)
                    hg_keys(i)
                if pair:
                    head_mean(r)
                if head:
                    hg_changes(i)
                    hg_outputs(i)
                if pair:
                    head_var(r)
                if head:
                    hg_norm(i)

            even_round(0, pair=False)
            even_round(1)
            with pe.Fori(2, EV_ROUNDS) as i:
                even_round(i)
            even_round(EV_ROUNDS, head=False)

            def out_projection(stage, unit0, n_chunks, y_from):
                ring = lambda c: (c - n_chunks) % 8
                for c in range(n_chunks - 4):
                    pe.wait_ge(sem["y_split"], count("y_split", 0, y_from + c))
                    for half in range(2):
                        if stage == 2 and c == 0 and half == 1:
                            pe.wait_ge(sem["mo_y"], count("mo_y", OD_ROUNDS - 1))
                        u = unit0 + 2 * c + half
                        pe.wait_ge(sem["w_ready"], count("w_ready", u))
                        for k in range(4):
                            last = split_products(bank[4 * half + k], u % SLOTS, k, h_split[:, ring(c), :],
                                                  h_split[:, KC + ring(c), :], c == 0, False)
                        last.then_inc(sem["units_done"], 1)
                for n in range(KC):
                    u = unit0 + 2 * (n_chunks - 4) + n
                    pe.wait_ge(sem["w_ready"], count("w_ready", u))
                    for k in range(4):
                        c = n_chunks - 4 + k
                        if n == 0:
                            pe.wait_ge(sem["y_split"], count("y_split", 0, y_from + c))
                        last = split_products(bank[n], u % SLOTS, k, h_split[:, ring(c), :], h_split[:, KC + ring(c), :],
                                              False, k == 3)
                    last.then_inc(sem["units_done"], 1)

            def gate_projection(stage, unit0):
                for c in range(4):
                    pe.wait_ge(sem["h_ready"], count("h_ready", stage, c))
                    for half in range(2):
                        u = unit0 + 2 * c + half
                        pe.wait_ge(sem["w_ready"], count("w_ready", u))
                        for k in range(4):
                            n = 4 * half + k
                            if c == 0 and n < 7:
                                pe.wait_ge(sem["x_added"], count("x_added", stage - 1, n + 1))
                            elif c == 0:
                                pe.wait_ge(sem["ln_done"], count("ln_done", stage))
                            last = split_products(bank[(n + 1) % 8], u % SLOTS, k, h_split[:, c, :], h_split[:, KC + c, :],
                                                  c == 0, False)
                        last.then_inc(sem["units_done"], 1)
                        if c == 0 and half == 0:
                            sumsq(stage, bank[0])
                for n in range(KC):
                    u = unit0 + 8 + n
                    pe.wait_ge(sem["w_ready"], count("w_ready", u))
                    for k in range(4):
                        if n == 0:
                            pe.wait_ge(sem["h_ready"], count("h_ready", stage, 4 + k))
                        last = split_products(bank[(n + 1) % 8], u % SLOTS, k, h_split[:, 4 + k, :], h_split[:, KC + 4 + k, :],
                                              False, k == 3)
                    last.then_inc(sem["units_done"], 1)

            pe.wait_ge(sem["prj_evac"], count("prj_evac", 0, 3))
            pe.wait_ge(sem["hg_n"], count("hg_n", EV_ROUNDS - 1))
            pe.wait_ge(sem["rw_d"], count("rw_d", EV_ROUNDS - 1))
            pe.wait_ge(sem["rw_lnv"], count("rw_lnv", EV_ROUNDS - 1))
            out_projection(0, U_OUT0, 2 * KC, 0)
            gate_projection(1, U_GAT0)
            pe.wait_ge(sem["gate_z"], count("gate_z", 0, 2))
            embed(1, 0, U_PRJ1, (2, 3))
            pe.wait_ge(sem["gate_z"], count("gate_z", 0, 4))
            embed(1, 1, U_PRJ1, (4, 5))
            sumsq(2, bank[1])
            pe.wait_ge(sem["gate_z"], count("gate_z", 0, 6))
            embed(1, 2, U_PRJ1, (6, 7))
            pe.wait_ge(sem["prj_evac"], count("prj_evac", 1, 0))
            embed(1, 3, U_PRJ1, (2, 3))

            def mo_values(r):
                pe.wait_ge(sem["ofree1"], count("ofree1", r, 1))
                if not (isinstance(r, int) and r == 0):
                    pe.wait_ge(sem["mo_pt"], count("mo_pt", r - 1, 7))
                for c in range(CH):
                    last = pe.transpose(bank[4][:, c * L:(c + 1) * L], mv[:, c * L:(c + 1) * L], ident)
                last.then_inc(sem["mo_vt"], 1)

            def mo_scores(r, n):
                e, qt = divmod(n, CH)
                o = bank[2 + n % 2]
                if n >= 2:
                    pe.wait_ge(sem["mo_exp"], count("mo_exp", r, n - 2))
                elif not (isinstance(r, int) and r == 0):
                    pe.wait_ge(sem["ru_i"], count("ru_i", r - 1, 1))
                pe.wait_ge(sem["ofree1"], count("ofree1", r, 0))
                pe.wait_ge(sem["ofree0"], count("ofree0", r, 1))
                mm(o[:, 0:(qt + 1) * L], mq[:, e, qt * L:(qt + 1) * L], mk[:, 0:(qt + 1) * L]).then_inc(sem["mo_s"], 1)

            def mo_transposes(r, n):
                qt = n % CH
                pe.wait_ge(sem["mo_p"], count("mo_p", r, n))
                if n:
                    pe.wait_ge(sem["mo_pt"], count("mo_pt", r, n - 1))
                else:
                    pe.wait_ge(sem["mo_vtok"], count("mo_vtok", r))
                for j in range(qt + 1):
                    last = pe.transpose(bank[4][:, j * L:(j + 1) * L], prob[:, n % 2, j * L:(j + 1) * L], ident)
                last.then_inc(sem["mo_tr"], 1)

            def mo_output(r, n):
                e, qt = divmod(n, CH)
                rows = slice(64 * e, 64 * e + 64)
                pe.wait_ge(sem["mo_pt"], count("mo_pt", r, n))
                if n == 0 and not (isinstance(r, int) and r == 0):
                    pe.wait_ge(sem["mo_y"], count("mo_y", r - 1))
                for j in range(qt + 1):
                    last = mm(bank[5][rows, qt * L:(qt + 1) * L], m_vtok[:, j * L + 64 * e:j * L + 64 * e + 64],
                              prob_t[:, n % 2, j * L:(j + 1) * L], j == 0, j == qt)
                last.then_inc(sem["mo_pv"], 1)

            def ru_gates(r, b):
                pe.wait_ge(sem["ru_conv"], count("ru_conv", r, 4 * b + 3))
                if b == 0:
                    pe.wait_ge(lru_loaded, (r + 1) * 16)
                    if not (isinstance(r, int) and r == 0):
                        pe.wait_ge(sem["ru_i"], count("ru_i", r - 1, 0))
                else:
                    pe.wait_ge(sem["mo_exp"], count("mo_exp", r, 7))
                at = 6 if b == 0 else 2
                mm(bank[at][:, :], lru_slot[:, 2 * b, :], xc[:, b, :]).then_inc(sem["ru_r_mm"], 1)
                mm(bank[at + 1][:, :], lru_slot[:, 2 * b + 1, :], xc[:, b, :]).then_inc(sem["ru_i_mm"], 1)

            def odd_round(i):
                first = isinstance(i, int) and i == 0
                for j in range(4):
                    tile(i, j, U_ODD, "ofree", first and j < 2, 2 if first and j == 0 else None)
                ru_gates(i, 0)
                mo_scores(i, 0)
                mo_scores(i, 1)
                mo_values(i)
                for n in range(2 * CH):
                    half_tile(i, 4 + n // 2, n % 2, U_ODD, "ofree", False)
                    if n:
                        mo_output(i, n - 1)
                    mo_transposes(i, n)
                    if n + 2 < 2 * CH:
                        mo_scores(i, n + 2)
                ru_gates(i, 1)
                mo_output(i, 2 * CH - 1)

            odd_round(0)
            with pe.Fori(1, OD_ROUNDS) as i:
                odd_round(i)

            pe.wait_ge(sem["ofree0"], count("ofree0", OD_ROUNDS - 1, 3))
            pe.wait_ge(sem["ofree1"], count("ofree1", OD_ROUNDS - 1, 3))
            pe.wait_ge(sem["ru_i"], count("ru_i", OD_ROUNDS - 1, 1))
            out_projection(2, U_OUT1, 4 + KC, 2 * KC)
            gate_projection(3, U_GAT1)
            sumsq(4, bank[1])

        @block.scalar
        def _(act):
            def f(o, i, func, bias=0.0, scale=1.0, **kw):
                return act.activation(o, i, func, bias=bias, scale=scale, **kw)

            def tile_done(r, j, unit0=0):
                act.wait_ge(sem["units_done"], r * 2 * TILES + unit0 + 2 * j + 2)

            def is_first(r):
                return isinstance(r, int) and r == 0

            def squares(stage, c):
                if stage:
                    act.wait_ge(sem["x_added"], count("x_added", stage - 1, c))
                    if c == 0:
                        act.wait_ge(sem["sq_used"], count("sq_used", stage - 1))
                if c >= 3:
                    act.wait_ge(sem["sq_summed"], count("sq_summed", stage, c - 3))
                f(sq[:, c % 2, :] if c else sq_sum, x[:, c, :], ACT.Square).then_inc(sem["sq_ready"], 1)

            def root(stage, o):
                act.preload_act_table_set("natural_log_exp_and_others")
                act.wait_ge(sem["sq_used"], count("sq_used", stage))
                f(rstd_s, o, ACT.Ln, bias=bias[:, 0:1], scale=1.0 / D).then_inc(sem["ln_done"], 1)
                act.wait_ge(sem["ln_done"], count("ln_done", stage))
                f(rstd_s, rstd_s, ACT.Exp, scale=-0.5).then_inc(sem["rstd"], 1)

            def high_half(stage, c):
                act.wait_ge(sem["hn_ready"], count("hn_ready", stage, c))
                f(h_split[:, c, :], hn[:, c % 2, :], ACT.Copy).then_inc(sem["hi_ready"], 1)

            def split_embedding(layer, units_before):
                act.wait_ge(p_loaded, 16 * (layer + 1))
                act.wait_ge(sem["units_done"], units_before)
                for c in range(2):
                    f(h_split[:, p_slot[layer] + c, :], p_raw[:, c, :], ACT.Copy).then_inc(sem["p_hi"], 1)

            def embedding_tiles(layer, m, unit0, banks):
                act.wait_ge(sem["units_done"], unit0 + m + 1)
                for n in range(2):
                    last = f(prj[:, 2 * m + n, :], bank[banks[n]], ACT.Copy)
                last.then_inc(sem["prj_evac"], 1)

            def output_high(unit0, n_chunks, y_from, rows, c):
                if c == 0:
                    act.wait_ge(sem["units_done"], EV_UNITS if unit0 == U_OUT0 else unit0)
                elif c == 6:
                    act.wait_ge(sem["units_done"], unit0)
                if c >= 8:
                    act.wait_ge(sem["units_done"], unit0 + 2 * (c - 7))
                f(h_split[:, (c - n_chunks) % 8, :], y[:, rows[c], :], ACT.Copy).then_inc(sem["y_hi"], 1)

            act.dma_start(w2_slot[0:64, 0, :], w2a2[0, 0:64]).then_inc(w2_loaded, 16)
            act.dma_start(w2_slot[64:P, 1, :], w2a2[0, 64:P]).then_inc(w2_loaded, 16)
            act.wait_ge(sem["bias_set"], count("bias_set", 0, 3))
            act.preload_act_table_set("natural_log_exp_and_others")
            act.wait_ge(sem["par_dve"], count("par_dve", 0, 3))
            f(ev[:, LB, :], par_t[:, 0, :], ACT.Exp).then_inc(sem["par_exp"], 1)
            act.wait_ge(sem["par_dve"], count("par_dve", 0, 10))
            f(par_t[:, 2, :], par_t[:, 1, :], ACT.Exp, scale=-1.0).then_inc(sem["par_lam"], 1)
            act.wait_ge(sem["par_lam"], count("par_lam", 0, 0))
            f(par_t[:, 2, :], par_t[:, 2, :], ACT.Ln, bias=bias[:, 3:4]).then_inc(sem["par_lam"], 1)

            for c in range(KC):
                act.wait_ge(x_loaded[c // 2], 16)
                squares(0, c)
            root(0, R3[:, :])
            for c in range(KC):
                high_half(0, c)

            def level_copies(r, lvl):
                m = 1 << (lvl - 1)
                act.wait_ge(sem["hg_lvl"], count("hg_lvl", r, lvl - 1))
                if lvl >= 2:
                    act.wait_ge(sem["hg_even"], count("hg_even", r, 2 * lvl - 3))
                if lvl >= 4:
                    act.wait_ge(sem["hg_qk"], count("hg_qk", r, lvl - 4))
                elif lvl == 3 and not is_first(r):
                    act.wait_ge(sem["hg_kt"], count("hg_kt", r - 1))
                keys = hk if lvl == 1 else kr[:, (lvl - 1) % 4, :]
                f(halves(qp[:, lvl % 4, :], m)[0], halves(qp[:, (lvl - 1) % 4, :], m)[0], ACT.Copy).then_inc(sem["hg_even"], 1)
                f(halves(kr[:, lvl % 4, :], m)[1], halves(keys, m)[1], ACT.Copy).then_inc(sem["hg_even"], 1)

            def shifted(i, n, j):
                tile_done(i, j)
                if n == 0:
                    if is_first(i):
                        act.wait_ge(sem["free0"], count("free0", 0, 0))
                    else:
                        act.wait_ge(sem["free1"], count("free1", i - 1, 3))
                    act.wait_ge(sem["cur_e"], count("cur_e", i))
                else:
                    act.wait_ge(sem[f"free{(j - 1) % 2}"], count(f"free{(j - 1) % 2}", i, (j - 1) // 2))
                f(shift[:, 1:T + 1], bank[j % 2][:, :], ACT.Copy, scale=cur_e[:, MU_R + n:MU_R + n + 1]).then_inc(sem["shifted"], 1)

            def inverse_start(r, c):
                act.wait_ge(sem["rw_first"], count("rw_first", r, c))
                f(inv[:, c, 0:2, :].rearrange("p e t -> p (e t)"), bank[2 + c % 2][:, 0:2 * P], ACT.Copy).then_inc(sem["rw_init"], 1)

            def inverse_p(r, lvl, c):
                n = (lvl - 1) * CH + c
                act.wait_ge(sem["rw_p"], count("rw_p", r, n))
                if n >= 2:
                    act.wait_ge(sem["rw_n"], count("rw_n", r, n - 2))
                elif not is_first(r):
                    act.wait_ge(sem["rw_n"], count("rw_n", r - 1, 22 + n))
                o = bank[4 + c % 2]
                if lvl < 6:
                    m = 1 << lvl
                    even, _ = halves(p_full[:, c % 2, :, :].rearrange("p e t -> p (e t)"), m)
                    src, _ = halves(o[:, 0:2 * P], m)
                else:
                    even = p_full[64:P, c % 2, :, 0:64]
                    src = o[64:P, 0:P].rearrange("p (e t) -> p e t", e=2)
                f(even, src, ACT.Copy).then_inc(sem["rw_pev"], 1)

            def inverse_t(r, lvl, c):
                act.wait_ge(sem["rw_t"], count("rw_t", r, (lvl - 1) * CH + c))
                f(inv[:, c, 2:4, :].rearrange("p e t -> p (e t)"), bank[2 + c % 2][:, 0:2 * P], ACT.Copy).then_inc(sem["rw_xt"], 1)

            def inverse(r, lvl):
                inverse_p(r, lvl, 0)
                if lvl > 1:
                    inverse_t(r, lvl - 1, 2)
                inverse_p(r, lvl, 1)
                if lvl > 1:
                    inverse_t(r, lvl - 1, 3)
                inverse_p(r, lvl, 2)
                if lvl < 6:
                    inverse_t(r, lvl, 0)
                inverse_p(r, lvl, 3)
                if lvl < 6:
                    inverse_t(r, lvl, 1)

            def chain(r, c):
                act.wait_ge(sem["rw_rhs"], count("rw_rhs", r, c))
                f(rhs_s[:, c % 2, :].rearrange("p (e t) -> p e t", e=2), psum[:, 4:6, 0:64], ACT.Copy).then_inc(sem["rw_rhse"], 1)
                act.wait_ge(sem["rw_u"], count("rw_u", r, c))
                if c < 2 and not is_first(r):
                    act.wait_ge(sem["rw_yc"], count("rw_yc", r - 1, 3))
                elif c >= 2:
                    act.wait_ge(sem["rw_yc"], count("rw_yc", r, c - 2))
                f(u_s[:, c % 2, :], R0[:, 64:192], ACT.Copy).then_inc(sem["rw_ue"], 1)

            def even_round(i, head=True, pair=True):
                r = i - 1
                tile_done(i, 0)
                if not head:
                    act.wait_ge(sem["hg_y"], count("hg_y", EV_ROUNDS - 1))
                    act.dma_start(p_raw, pT[0]).then_inc(p_loaded, 16)
                if is_first(i):
                    act.wait_ge(sem["zeroed"], count("zeroed", 0))
                    f(shift[:, 1:T + 1], bank[0][:, :], ACT.Copy, scale=mu_lr[:, 0:1]).then_inc(sem["lr_shift"], 1)
                    act.wait_ge(sem["free0"], count("free0", 0, 0))
                    f(lr[0:64, :], lr[0:64, :], ACT.Tanh).then_inc(sem["lr_ready"], 1)
                else:
                    act.wait_ge(sem["free1"], count("free1", i - 1, 1))
                    f(sig_a, bank[0][:, :], ACT.Sigmoid).then_inc(sem["sig_gb"], 1)
                if pair:
                    act.wait_ge(sem["cur_r"], count("cur_r", r))
                    act.wait_ge(sem["rw_wx"], count("rw_wx", r))
                    f(e_neg, R0[:, :], ACT.Sigmoid, bias=cur_r[:, W0:W0 + 1]).then_inc(sem["rw_sw"], 1)
                    act.wait_ge(sem["rw_ax"], count("rw_ax", r))
                    f(w_a, R1[:, :], ACT.Sigmoid, bias=cur_r[:, A0:A0 + 1]).then_inc(sem["rw_av"], 1)
                    if head:
                        act.dma_start(w2_slot[0:64, 0, :], w2a2[bass.ds(i, 1), 0:64, :]).then_inc(w2_loaded, 16)
                        act.dma_start(w2_slot[64:P, 1, :], w2a2[bass.ds(i, 1), 64:P, :]).then_inc(w2_loaded, 16)
                    f(t1, wk, ACT.Square, scale=cur_r[:, K_K:K_K + 1]).then_inc(sem["rw_ksq"], 1)
                if head:
                    tile_done(i, 1)
                    f(sig_b, bank[1][:, :], ACT.Sigmoid).then_inc(sem["sig_q"], 1)
                if not head:
                    split_embedding(0, EV_UNITS)
                if pair:
                    act.preload_act_table_set("natural_log_exp_and_others")
                    act.wait_ge(sem["rw_center"], count("rw_center", r))
                    f(e_neg, cum[:, :, 1:L + 1], ACT.Exp, scale=KAPPA).then_inc(sem["rw_exp"], 1)
                    act.wait_ge(sem["rw_exp"], count("rw_exp", r, 0))
                    f(e_pos, cum, ACT.Exp, scale=-KAPPA).then_inc(sem["rw_exp"], 1)
                    f(e_mid, e_mid, ACT.Exp, scale=-KAPPA).then_inc(sem["rw_exp"], 1)
                    act.wait_ge(sem["rw_m1"], count("rw_m1", r))
                    f(t1, t1, ACT.Ln).then_inc(sem["rw_ln"], 1)
                    act.wait_ge(sem["rw_ln"], count("rw_ln", r))
                    f(t1, t1, ACT.Exp, bias=bias[:, 2:3], scale=-0.5).then_inc(sem["rw_rn"], 1)
                    if not is_first(r):
                        act.wait_ge(sem["rw_u"], count("rw_u", r - 1, 3))
                    for c in range(CH):
                        last = f(inv[:, c, 2:4, :], fconst[:, 0:1, :].to_broadcast([P, 2, P]), ACT.Copy)
                    last.then_inc(sem["rw_reset"], 1)
                if head:
                    tile_done(i, 2)
                    if is_first(i):
                        act.wait_ge(sem["free1"], count("free1", 0, 0))
                    else:
                        act.wait_ge(sem["free0"], count("free0", i, 0))
                    f(sig_a, bank[0][:, :], ACT.Sigmoid).then_inc(sem["sig_f"], 1)
                    act.wait_ge(sem["free1"], count("free1", i, 0))
                    f(sig_b, bank[0][:, :], ACT.Sigmoid, scale=-1.0).then_inc(sem["free0"], 1)
                    tile_done(i, 3)
                    act.wait_ge(sem["fk"], count("fk", i, 0))
                    f(sig_a, bank[1][:, :], ACT.Sigmoid).then_inc(sem["sig_ga"], 1)
                if pair:
                    if not head:
                        embedding_tiles(0, 0, U_PRJ0, (0, 1))
                    for n, (dst, src) in enumerate(((b_tok, R0), (k_tok, R1), (v_tok, R2))):
                        act.wait_ge(sem["rw_tr"], count("rw_tr", r, n))
                        f(dst, src[:, :], ACT.Copy).then_inc(sem["rw_tok"], 1)
                act.preload_act_table_set("natural_log_exp_and_others")
                if pair:
                    for c in range(CH - 1):
                        inverse_start(r, c)
                if head:
                    tile_done(i, 4)
                    if not is_first(i):
                        act.wait_ge(sem["hg_vt"], count("hg_vt", i - 1))
                    f(hv, bank[0][:, :], ACT.Copy).then_inc(sem["free0"], 1)
                if pair:
                    inverse_start(r, CH - 1)
                for lvl in range(1, 7):
                    if pair:
                        inverse(r, lvl)
                    if head and lvl <= 3:
                        level_copies(i, lvl)
                if pair:
                    chain(r, 0)
                if head:
                    shifted(i, 0, 5)
                    act.wait_ge(sem["hg_vt"], count("hg_vt", i))
                    f(h_vtok, H0[:, :], ACT.Copy).then_inc(sem["hg_vtok"], 1)
                if pair:
                    chain(r, 1)
                if not head:
                    embedding_tiles(0, 1, U_PRJ0, (0, 1))
                    output_high(U_OUT0, 2 * KC, 0, range(2 * KC), 0)
                    output_high(U_OUT0, 2 * KC, 0, range(2 * KC), 1)
                if head:
                    level_copies(i, 4)
                    shifted(i, 1, 6)
                if pair:
                    chain(r, 2)
                if not head:
                    embedding_tiles(0, 2, U_PRJ0, (0, 1))
                    output_high(U_OUT0, 2 * KC, 0, range(2 * KC), 2)
                    output_high(U_OUT0, 2 * KC, 0, range(2 * KC), 3)
                if head:
                    level_copies(i, 5)
                    level_copies(i, 6)
                    shifted(i, 2, 7)
                if pair:
                    chain(r, 3)
                if not head:
                    embedding_tiles(0, 3, U_PRJ0, (0, 1))
                    output_high(U_OUT0, 2 * KC, 0, range(2 * KC), 4)
                    output_high(U_OUT0, 2 * KC, 0, range(2 * KC), 5)
                if pair:
                    act.wait_ge(sem["rw_yc"], count("rw_yc", r, 3))
                    if not head:
                        act.dma_start(x, xT).then_inc(x_again, 16)
                    f(b_t, R2[:, :], ACT.Copy).then_inc(sem["rw_ysb"], 1)
                if head:
                    level_copies(i, 7)
                    act.wait_ge(sem["hg_kt"], count("hg_kt", i))
                    f(h_ktok[:, 0:3 * L], H0[:, 0:3 * L], ACT.Copy).then_inc(sem["hg_ktok"], 1)
                if pair:
                    act.wait_ge(sem["rw_d"], count("rw_d", r))
                    f(k_t, b_t, ACT.Square).then_inc(sem["rw_dsq"], 1)
                if head:
                    act.wait_ge(sem["hg_o"], count("hg_o", i))
                    f(hk, H1[:, :], ACT.Square).then_inc(sem["hg_sq"], 1)
                if pair:
                    act.wait_ge(sem["rw_var"], count("rw_var", r))
                    f(t1, R1[:, :], ACT.Ln, bias=bias[:, 1:2], scale=1.0 / 64).then_inc(sem["rw_lnv"], 1)
                    act.wait_ge(sem["rw_lnv"], count("rw_lnv", r))
                    f(t1, t1, ACT.Exp, scale=-0.5).then_inc(sem["rw_rstd"], 1)
                if head:
                    act.wait_ge(sem["hg_ssq"], count("hg_ssq", i))
                    f(sig_b, H0[:, :], ACT.Ln, bias=bias[:, 0:1], scale=1.0 / P).then_inc(sem["hg_ln"], 1)
                    act.wait_ge(sem["hg_ln"], count("hg_ln", i))
                    f(sig_b, sig_b, ACT.Exp, scale=-0.5).then_inc(sem["hg_rstd"], 1)

            even_round(0, pair=False)
            even_round(1)
            with act.Fori(2, EV_ROUNDS) as i:
                even_round(i)
            even_round(EV_ROUNDS, head=False)

            def output_sums(stage, unit_end):
                for n in range(KC):
                    squares(stage + 1, n)
                    if n < 4:
                        high_half(stage + 1, n)
                root(stage + 1, bank[0])
                act.wait_ge(sem["units_done"], unit_end)
                for c in range(4, KC):
                    high_half(stage + 1, c)

            def gates(stage, between=None):
                for n in range(KC):
                    if n == 2 and between:
                        between()
                    act.wait_ge(sem["gate_z"], count("gate_z", stage // 2, n))
                    f(sg[:, n % 2, :], sg[:, n % 2, :], ACT.Sigmoid).then_inc(sem["gate_sig"], 1)
                    if n:
                        squares(stage + 1, n - 1)
                squares(stage + 1, KC - 1)
                if stage == 1:
                    embedding_tiles(1, 0, U_PRJ1, (2, 3))
                    embedding_tiles(1, 1, U_PRJ1, (4, 5))
                root(stage + 1, bank[1])

            for c in range(6, 2 * KC):
                if c == 2 * KC - 1:
                    act.wait_ge(sem["rw_y"], count("rw_y", EV_ROUNDS - 1))
                output_high(U_OUT0, 2 * KC, 0, range(2 * KC), c)
            act.wait_ge(sem["p_ready"], count("p_ready", 0, 1))
            act.dma_start(p_raw, pT[1]).then_inc(p_loaded, 16)
            output_sums(0, U_GAT0)
            gates(1, between=lambda: split_embedding(1, U_GAT0 + 8))
            for c in range(2):
                high_half(2, c)
            embedding_tiles(1, 2, U_PRJ1, (6, 7))
            act.wait_ge(sem["units_done"], U_ODD)
            for c in range(2, 4):
                high_half(2, c)
            embedding_tiles(1, 3, U_PRJ1, (2, 3))
            for c in range(4, KC):
                high_half(2, c)

            def weights(i, n):
                w = (n % CH + 1) * L
                act.wait_ge(sem["mo_neg"], count("mo_neg", i, n))
                if n >= 2:
                    act.wait_ge(sem["mo_tr"], count("mo_tr", i, n - 2))
                f(prob[:, n % 2, 0:w], bank[2 + n % 2][:, 0:w], ACT.Exp, bias=m_stat[:, 1, n:n + 1], scale=0.125,
                  accum_out=m_sum[:, n:n + 1]).then_inc(sem["mo_exp"], 1)

            def transposed(i, n):
                w = (n % CH + 1) * L
                act.wait_ge(sem["mo_tr"], count("mo_tr", i, n))
                if n >= 2:
                    act.wait_ge(sem["mo_pv"], count("mo_pv", i, n - 2))
                f(prob_t[:, n % 2, 0:w], bank[4][:, 0:w], ACT.Copy).then_inc(sem["mo_pt"], 1)

            def lru_input(i, b):
                if not is_first(i):
                    act.wait_ge(sem["ru_conv"], count("ru_conv", i - 1, 4 * b + 3))
                f(xd[:, b, 3:T + 3], bank[0][:, :], ACT.Copy).then_inc(sem["ofree0"], 1)

            def lru_scales(r):
                act.wait_ge(sem["cneg_set"], count("cneg_set", r))
                for b in range(2):
                    act.wait_ge(sem["ru_th"], count("ru_th", r, b))
                    f(u_r[b], u_r[b], ACT.Exp, scale=cneg[:, b:b + 1]).then_inc(sem["ru_a"], 1)
                    f(u_1[b], u_th[b], ACT.Ln, bias=bias[:, 3:4]).then_inc(sem["ru_u1"], 1)
                    act.wait_ge(sem["ru_clamp"], count("ru_clamp", r, b))
                    f(u_2[b], u_2[b], ACT.Ln).then_inc(sem["ru_u2"], 1)

            def lru_roots(r):
                for b in range(2):
                    act.wait_ge(sem["ru_d"], count("ru_d", r, b))
                    f(u_2[b], u_2[b], ACT.Exp, bias=bias[:, 4:5], scale=0.5).then_inc(sem["ru_e"], 1)

            def odd_round(i, last=False):
                act.preload_act_table_set("natural_log_exp_and_others")
                act.wait_ge(sem["cur_o"], count("cur_o", i))
                if not is_first(i):
                    act.wait_ge(sem["ru_i_mm"], count("ru_i_mm", i - 1, 1))
                act.dma_start(lru_slot, lru_w[i] if isinstance(i, int) else lru_w[bass.ds(i, 1), :, :, :]).then_inc(lru_loaded, 16)
                tile_done(i, 0, U_ODD)
                lru_input(i, 0)
                tile_done(i, 1, U_ODD)
                act.wait_ge(sem["conv_pad"], count("conv_pad", 0))
                f(mq[0:64, 0, :], bank[1][0:64, :], ACT.Copy)
                f(mq[64:P, 1, :], bank[1][64:P, :], ACT.Copy).then_inc(sem["ofree1"], 1)
                if not is_first(i):
                    lru_scales(i - 1)
                    lru_roots(i - 1)
                tile_done(i, 3, U_ODD)
                f(mv, bank[1][:, :], ACT.Copy).then_inc(sem["ofree1"], 1)
                weights(i, 0)
                act.wait_ge(sem["mo_vt"], count("mo_vt", i))
                f(m_vtok, bank[4][:, :], ACT.Copy).then_inc(sem["mo_vtok"], 1)
                for n in range(2 * CH):
                    if n + 1 < 2 * CH:
                        weights(i, n + 1)
                    transposed(i, n)
                    if n == 0:
                        tile_done(i, 4, U_ODD)
                        lru_input(i, 1)
                for b in range(2):
                    at = 6 if b == 0 else 2
                    act.wait_ge(sem["ru_r_mm"], count("ru_r_mm", i, b))
                    f(u_r[b], bank[at][:, :], ACT.Sigmoid, bias=cur_o[:, BA, b:b + 1]).then_inc(sem["ru_r"], 1)
                    act.wait_ge(sem["ru_i_mm"], count("ru_i_mm", i, b))
                    f(u_i[b], bank[at + 1][:, :], ACT.Sigmoid, bias=cur_o[:, BX, b:b + 1]).then_inc(sem["ru_i"], 1)
                if last:
                    output_high(U_OUT1, 4 + KC, 2 * KC, ODD_OUTPUTS, 0)
                for b in range(2):
                    act.wait_ge(sem["ru_r"], count("ru_r", i, b))
                    f(u_th[b], u_r[b], ACT.Tanh, scale=cur_o[:, CPOS, b:b + 1]).then_inc(sem["ru_th"], 1)
                for n, free in ((0, ("ofree1", 2)), (1, ("ofree0", 3)), (2, ("ofree1", 3))):
                    act.wait_ge(sem[free[0]], count(free[0], i, free[1]))
                    f(osig[:, n, :], og[:, n, :], ACT.Sigmoid).then_inc(sem["o_sig"], 1)
            odd_round(0)
            with act.Fori(1, OD_ROUNDS - 1) as i:
                odd_round(i)
            odd_round(OD_ROUNDS - 1, last=True)
            for c in range(1, 3):
                output_high(U_OUT1, 4 + KC, 2 * KC, ODD_OUTPUTS, c)
            act.preload_act_table_set("natural_log_exp_and_others")
            lru_scales(OD_ROUNDS - 1)
            lru_roots(OD_ROUNDS - 1)
            for c in range(3, 4 + KC):
                if c == 9:
                    act.wait_ge(sem["ru_y"], count("ru_y", OD_ROUNDS - 1, 1))
                output_high(U_OUT1, 4 + KC, 2 * KC, ODD_OUTPUTS, c)
            output_sums(2, U_GAT1)
            gates(3)

        @block.vector
        def _(dve):
            def is_first(r):
                return isinstance(r, int) and r == 0

            def tile_done(r, j, unit0=0):
                dve.wait_ge(sem["units_done"], r * 2 * TILES + unit0 + 2 * j + 2)

            def stt(o, a, scalar, b, op0, op1):
                return dve.scalar_tensor_tensor(out=o, in0=a, scalar=scalar, in1=b, op0=op0, op1=op1)

            def low_half(stage, c):
                dve.wait_ge(sem["hi_ready"], count("hi_ready", stage, c))
                dve.tensor_tensor(h_split[:, KC + c, :], hn[:, c % 2, :], h_split[:, c, :].bitcast(F32), ALU.subtract).then_inc(sem["h_ready"], 1)

            def normed(stage, g, dst):
                dve.wait_ge(sem["rstd"], count("rstd", stage))
                for c in range(KC):
                    if dst is hn and c >= 2:
                        dve.wait_ge(sem["h_ready"], count("h_ready", stage, c - 2))
                    o = hn[:, c % 2, :] if dst is hn else dst[:, c, :]
                    stt(o, x[:, c, :], gain[:, g, c:c + 1], rstd_s, ALU.mult, ALU.mult).then_inc(sem["hn_ready"], 1)
                    if dst is hn and c >= 1:
                        low_half(stage, c - 1)
                if dst is hn:
                    low_half(stage, KC - 1)

            def sum_squares(stage, c):
                dve.wait_ge(sem["sq_ready"], count("sq_ready", stage, c))
                if c >= 2:
                    dve.wait_ge(sem["sq_summed"], count("sq_summed", stage, c - 2))
                dve.tensor_tensor(sq_sum, sq_sum, sq[:, c % 2, :], ALU.add).then_inc(sem["sq_summed"], 1)

            def split_embedding(layer):
                for c in range(2):
                    dve.wait_ge(sem["p_hi"], count("p_hi", layer, c))
                    dve.tensor_tensor(h_split[:, KC + p_slot[layer] + c, :], p_raw[:, c, :], h_split[:, p_slot[layer] + c, :].bitcast(F32),
                                      ALU.subtract).then_inc(sem["p_ready"], 1)

            def output_low(n_chunks, y_from, rows, c):
                ring = (c - n_chunks) % 8
                dve.wait_ge(sem["y_hi"], count("y_hi", 0, y_from + c))
                dve.tensor_tensor(h_split[:, KC + ring, :], y[:, rows[c], :], h_split[:, ring, :].bitcast(F32),
                                  ALU.subtract).then_inc(sem["y_split"], 1)

            for n, v in enumerate((EPS, LN_EPS, 20 * LN2, 1.0, -20 * LN2)):
                ins = dve.memset(bias[:, n:n + 1], v)
                if n:
                    ins.then_inc(sem["bias_set"], 1)
            dve.memset(attn, 0.0)
            dve.memset(p_full, 0.0)
            dve.memset(shift[:, 0:1], 0.0)
            dve.memset(w2_slot[64:P, 0, :], 0.0)
            dve.memset(w2_slot[0:64, 1, :], 0.0)
            dve.memset(ar, 0.0)
            dve.memset(cum[:, :, 0:1], 0.0).then_inc(sem["zeroed"], 1)
            dve.wait_ge(sem["zeroed"], count("zeroed", 0))

            dve.wait_ge(const_loaded, 80)
            dve.tensor_scalar(ev[:, OMU_R:OMU_V + 1, :], ev[:, MU_R:MU_V + 1, :], -1.0, 1.0, ALU.mult, ALU.add).then_inc(sem["par_dve"], 1)
            dve.tensor_scalar(mu_lr[:, 2:3], mu_lr[:, 0:1], -1.0, 1.0, ALU.mult, ALU.add).then_inc(sem["par_dve"], 1)
            dve.memset(par_t[:, 1, :], 0.0).then_inc(sem["par_dve"], 1)
            dve.tensor_tensor(par_t[:, 0, :], ev[:, LB_LOGIT, :], ev[:, LB_LOGIT, :], ALU.subtract).then_inc(sem["par_dve"], 1)
            dve.wait_ge(sem["par_exp"], count("par_exp", 0))
            dve.reciprocal(par_t[:, 0, :], ev[:, LB, :]).then_inc(sem["par_dve"], 1)
            dve.wait_ge(sem["par_dve"], count("par_dve", 0, 4))
            dve.tensor_tensor(par_t[:, 0, :], par_t[:, 0, :], ev[:, LB, :], ALU.mult).then_inc(sem["par_dve"], 1)
            dve.wait_ge(sem["par_dve"], count("par_dve", 0, 5))
            dve.tensor_tensor(par_t[:, 0, :], par_t[:, 0, :], par_t[:, 0, :], ALU.subtract).then_inc(sem["par_dve"], 1)
            dve.wait_ge(sem["par_dve"], count("par_dve", 0, 6))
            dve.tensor_scalar(ev[:, LB, :], par_t[:, 0, :], 0.0, None, ALU.max).then_inc(sem["par_dve"], 1)
            dve.wait_ge(sem["par_dve"], count("par_dve", 0, 7))
            dve.tensor_scalar(ev[:, OLB, :], ev[:, LB, :], -1.0, 1.0, ALU.mult, ALU.add).then_inc(sem["par_dve"], 1)
            dve.tensor_scalar(par_t[:, 0, :], od[:, LAM, :], -1.0, None, ALU.mult).then_inc(sem["par_dve"], 1)
            dve.wait_ge(sem["par_dve"], count("par_dve", 0, 9))
            dve.tensor_tensor(par_t[:, 1, :], par_t[:, 0, :], od[:, LAM, :], ALU.max).then_inc(sem["par_dve"], 1)
            dve.tensor_scalar(par_t[:, 0, :], par_t[:, 0, :], 0.0, None, ALU.max).then_inc(sem["par_dve"], 1)
            dve.wait_ge(sem["par_lam"], count("par_lam", 0, 1))
            dve.wait_ge(sem["par_dve"], count("par_dve", 0, 11))
            dve.tensor_tensor(par_t[:, 0, :], par_t[:, 0, :], par_t[:, 2, :], ALU.add).then_inc(sem["par_dve"], 1)
            dve.wait_ge(sem["par_dve"], count("par_dve", 0, 12))
            dve.tensor_scalar(od[:, CNEG, :], par_t[:, 0, :], -8.0, None, ALU.mult).then_inc(sem["par_dve"], 1)
            dve.tensor_scalar(od[:, CPOS, :], par_t[:, 0, :], 8.0, None, ALU.mult).then_inc(sem["par_dve"], 1)
            for n in range(4):
                dve.wait_ge(x_loaded[n], 16)
            for c in range(1, KC):
                sum_squares(0, c)
            normed(0, 0, hn)

            def masked_copy(dst, mask, src):
                dve.sem_inc(vector_copies, 1)
                return dve.copy_predicated(dst, mask, src)

            def gated(i, j, ready, sig, dst):
                dve.wait_ge(sem[ready], count(ready, i - 1 if j == 0 else i))
                dve.tensor_tensor(dst, bank[j % 2][:, :], sig, ALU.mult).then_inc(sem[f"free{j % 2}"], 1)

            def mixed(i, n, j, dst):
                dve.wait_ge(sem["shifted"], count("shifted", i, n))
                if n == 2 and not is_first(i):
                    dve.wait_ge(sem["rw_tr"], count("rw_tr", i - 1, 2))
                stt(dst, bank[j % 2][:, :], cur_e[:, OMU_R + n:OMU_R + n + 1], shift[:, 0:T], ALU.mult, ALU.add).then_inc(sem[f"free{j % 2}"], 1)

            def level(r, lvl):
                if lvl == 0:
                    dve.wait_ge(sem["fk"], count("fk", r, 1))
                    if not is_first(r):
                        dve.wait_ge(sem["hg_sq"], count("hg_sq", r - 1))
                    dve.tensor_tensor(qp[:, 0, :], hq, hf, ALU.mult).then_inc(sem["hg_lvl"], 1)
                    return
                m = 1 << (lvl - 1)
                keys = hk if lvl == 1 else kr[:, (lvl - 1) % 4, :]
                dve.wait_ge(sem["hg_lvl"], count("hg_lvl", r, lvl - 1))
                if lvl >= 2:
                    dve.wait_ge(sem["hg_even"], count("hg_even", r, 2 * lvl - 3))
                if lvl >= 4:
                    dve.wait_ge(sem["hg_qk"], count("hg_qk", r, lvl - 4))
                t_even, t_odd = halves(tot[lvl - 1], 1)
                nb = T // (2 * m)
                q_dst, k_dst = halves(qp[:, lvl % 4, :], m)[1], halves(kr[:, lvl % 4, :], m)[0]
                q_src, k_src = halves(qp[:, (lvl - 1) % 4, :], m)[1], halves(keys, m)[0]
                dve.tensor_tensor(q_dst, q_src, t_even.to_broadcast([P, nb, m]), ALU.mult)
                dve.tensor_tensor(k_dst, k_src, t_odd.to_broadcast([P, nb, m]), ALU.mult)
                dve.tensor_tensor(tot[lvl].rearrange("p (b m) -> p b m", m=1), t_even, t_odd, ALU.mult).then_inc(sem["hg_lvl"], 1)

            def masked(r, lvl):
                dve.wait_ge(sem["hg_qk"], count("hg_qk", r, lvl))
                if lvl:
                    dve.wait_ge(sem["hg_masked"], count("hg_masked", r, lvl - 1))
                if lvl == LEVELS - 1:
                    dve.tensor_copy(halves(attn[0:64], 64)[1], halves(bank[2][0:64], 64)[1]).then_inc(sem["hg_masked"], 1)
                elif lvl < LEVELS:
                    m = 1 << lvl
                    _, dst = halves(attn, m)
                    mask = hg_mask[:, lvl, :].rearrange("p (b m) -> p b m", m=m)
                    _, src = halves(bank[2 + lvl % 2], m)
                    masked_copy(dst, mask, src).then_inc(sem["hg_masked"], 1)
                else:
                    masked_copy(attn, diag_mask, H1[:, :]).then_inc(sem["hg_masked"], 1)

            def states(r):
                dve.wait_ge(sem["hg_kv"], count("hg_kv", r))
                dve.tensor_copy(h_state[:, 0:P], H0[:, 0:P]).then_inc(sem["hg_state"], 1)
                for c in range(1, CH - 1):
                    dve.wait_ge(sem["hg_state"], count("hg_state", r, c - 1))
                    stt(h_state[:, c * P:(c + 1) * P], h_state[:, (c - 1) * P:c * P], tot[7][:, c:c + 1],
                               H0[:, c * P:(c + 1) * P], ALU.mult, ALU.add).then_inc(sem["hg_state"], 1)

            def head_out(r):
                dve.wait_ge(sem["hg_rstd"], count("hg_rstd", r))
                stt(sig_b, H1[:, :], cur_e[:, HG_G:HG_G + 1], sig_b, ALU.mult, ALU.mult).then_inc(sem["hg_n"], 1)
                dve.wait_ge(sem["hg_n"], count("hg_n", r))
                dve.tensor_tensor(y[:, r, :] if isinstance(r, int) else y[:, bass.ds(r, 1), :].rearrange("p a t -> p (a t)"),
                                         sig_b, g_a, ALU.mult).then_inc(sem["hg_y"], 1)

            def decay_sums(r):
                dve.wait_ge(sem["rw_sw"], count("rw_sw", r))
                if not is_first(r):
                    dve.wait_ge(sem["rw_rho"], count("rw_rho", r - 1))
                dve.memset(cum[:, :, 0:1], 0.0).then_inc(sem["rw_prep"], 1)
                for c in range(CH):
                    last = dve.tensor_tensor_scan(out=cum[:, c, 1:L + 1], data0=ones, data1=e_neg[:, c * L:(c + 1) * L],
                                                  initial=0.0, op0=ALU.mult, op1=ALU.add)
                last.then_inc(sem["rw_prep"], 1)
                dve.wait_ge(sem["rw_prep"], count("rw_prep", r, 1))
                dve.tensor_copy(e_mid, cum[:, :, L // 2]).then_inc(sem["rw_prep"], 1)
                dve.wait_ge(sem["rw_prep"], count("rw_prep", r, 2))
                dve.tensor_tensor(cum, cum, e_mid.unsqueeze(2).to_broadcast([P, CH, L + 1]), ALU.subtract).then_inc(sem["rw_center"], 1)
                dve.wait_ge(sem["rw_av"], count("rw_av", r))
                dve.tensor_scalar(t2, w_a, 1.0, cur_r[:, K_A:K_A + 1], ALU.subtract, ALU.mult).then_inc(sem["rw_prep"], 1)
                dve.wait_ge(sem["rw_prep"], count("rw_prep", r, 3))
                stt(k_t, t2, 1.0, wk, ALU.add, ALU.mult).then_inc(sem["rw_prep"], 1)
                dve.wait_ge(sem["rw_prep"], count("rw_prep", r, 4))
                stt(t2, wr, cur_r[:, R_K:R_K + 1], k_t, ALU.mult, ALU.mult).then_inc(sem["rw_rk"], 1)

            def key_norm(r):
                dve.wait_ge(sem["rw_ssq"], count("rw_ssq", r))
                dve.tensor_scalar(t1, R2[:, :], 1e-24, float(2 ** 40), ALU.max, ALU.mult).then_inc(sem["rw_m1"], 1)
                dve.wait_ge(sem["rw_bon"], count("rw_bon", r))
                dve.tensor_tensor(w_bonus, R3[:, :], wv, ALU.mult).then_inc(sem["rw_bonus"], 1)

            def operands(r):
                chunks = lambda ap: ap.rearrange("p (c t) -> p c t", c=CH)
                dve.wait_ge(sem["rw_rn"], count("rw_rn", r))
                stt(t1, wk, cur_r[:, K_K:K_K + 1], t1, ALU.mult, ALU.mult).then_inc(sem["rw_kk"], 1)
                dve.wait_ge(sem["rw_kk"], count("rw_kk", r, 0))
                dve.tensor_tensor(b_t, t1, w_a, ALU.mult).then_inc(sem["rw_kk"], 1)
                dve.wait_ge(sem["rw_kk"], count("rw_kk", r, 1))
                dve.wait_ge(sem["rw_exp"], count("rw_exp", r, 2))
                first, second = slice(0, 64), slice(64, P)
                stt(ar[first, :, 0, 0, :], chunks(t1[first]), -1.0, e_pos[first, :, 0:L], ALU.mult, ALU.mult)
                stt(ar[second, :, 1, 0, :], chunks(t1[second]), -1.0, e_pos[second, :, 0:L], ALU.mult, ALU.mult).then_inc(sem["rw_ops"], 1)
                dve.tensor_tensor(ar[first, :, 0, 1, :], chunks(wr[first]), e_pos[first, :, 1:L + 1], ALU.mult)
                dve.tensor_tensor(ar[second, :, 1, 1, :], chunks(wr[second]), e_pos[second, :, 1:L + 1], ALU.mult).then_inc(sem["rw_ops"], 1)
                dve.tensor_tensor(b_t, b_t, e_neg, ALU.mult).then_inc(sem["rw_ops"], 1)
                dve.tensor_tensor(k_t, k_t, e_neg, ALU.mult).then_inc(sem["rw_ops"], 1)
                dve.tensor_tensor(rho[:, 0:3], e_pos[:, 0:3, L], e_mid[:, 1:4], ALU.mult).then_inc(sem["rw_rho"], 1)

            def matrices(r):
                dve.wait_ge(sem["rw_reset"], count("rw_reset", r))
                by_head = lambda ap: ap.rearrange("p (e s t) -> p e s t", e=2, s=2)
                odd = lambda ap: ap.rearrange("p e (b two) -> p e b two", two=2)[:, :, :, 1]
                for c in range(CH):
                    for k in range(2):
                        n = 2 * c + k
                        dve.wait_ge(sem["rw_qk"], count("rw_qk", r, n))
                        last = masked_copy(rw_m[:, c, :, 2 * k:2 * k + 2, :], m4_mask, by_head(bank[4 + k]))
                        if k == 0:
                            last = masked_copy(odd(inv[:, c, 2:4, :]), hg_mask[:, 0, 0:64].unsqueeze(1).to_broadcast([P, 2, 64]),
                                               odd(by_head(bank[4])[:, :, 0, :]))
                        last.then_inc(sem["rw_masked"], 1)

            def inverse(r, lvl):
                m = 1 << lvl
                for c in range(CH):
                    n = (lvl - 1) * CH + c
                    o = bank[6 + c % 2]
                    dve.wait_ge(sem["rw_n"], count("rw_n", r, n))
                    if lvl < 6:
                        blocks = lambda ap: ap.rearrange("p (b m) -> p b m", m=m)
                        masked_copy(halves(inv[:, c, 0:2, :].rearrange("p e t -> p (e t)"), m)[0],
                                    blocks(nat_mask[:, lvl, :]), halves(o[:, 0:2 * P], m)[0]).then_inc(sem["rw_x"], 1)
                    else:
                        dve.tensor_copy(inv[0:64, c, 2:4, 64:P], o[0:64, 0:P].rearrange("p (e t) -> p e t", e=2)).then_inc(sem["rw_x"], 1)

            def state(r, c):
                dve.wait_ge(sem["rw_st"], count("rw_st", r, c))
                if c == 0:
                    if not is_first(r):
                        dve.wait_ge(sem["rw_yc"], count("rw_yc", r - 1, 3))
                    dve.tensor_copy(w_state[:, 0, :], R3[:, 0:64]).then_inc(sem["rw_sadd"], 1)
                else:
                    dve.wait_ge(sem["rw_s"], count("rw_s", r, c - 1))
                    if c == 2:
                        dve.wait_ge(sem["rw_yc"], count("rw_yc", r, 1))
                    dve.tensor_tensor(s_sum, R3[:, 0:64], w_state[:, c % 2, :], ALU.add).then_inc(sem["rw_sadd"], 1)
                dve.wait_ge(sem["rw_sadd"], count("rw_sadd", r, c))
                src = w_state[:, 0, :] if c == 0 else s_sum
                dve.tensor_scalar(w_state[:, (c + 1) % 2, :], src, rho[:, c:c + 1], None, ALU.mult).then_inc(sem["rw_s"], 1)

            def pair_mean(r):
                dve.wait_ge(sem["rw_mean"], count("rw_mean", r))
                stt(b_t, R0[:, :], -1.0 / 64, b_t, ALU.mult, ALU.add).then_inc(sem["rw_d"], 1)

            def pair_out(r):
                dve.wait_ge(sem["rw_rstd"], count("rw_rstd", r))
                dve.tensor_tensor(b_t, b_t, t1, ALU.mult).then_inc(sem["rw_norm"], 1)
                dve.wait_ge(sem["rw_norm"], count("rw_norm", r, 0))
                stt(b_t, b_t, cur_r[:, LN_G:LN_G + 1], w_bonus, ALU.mult, ALU.add).then_inc(sem["rw_norm"], 1)
                dve.wait_ge(sem["rw_norm"], count("rw_norm", r, 1))
                stt(y[:, KC + r, :] if isinstance(r, int) else y[:, bass.ds(r + KC, 1), :].rearrange("p a t -> p (a t)"),
                           b_t, cur_r[:, LN_B:LN_B + 1], g_b, ALU.add, ALU.mult).then_inc(sem["rw_y"], 1)

            def even_round(i, head=True, pair=True):
                r = i - 1
                if pair:
                    if not is_first(r):
                        dve.wait_ge(sem["rw_y"], count("rw_y", r - 1))
                    dve.tensor_copy(cur_r, ev[:, :, r] if isinstance(r, int) else ev[:, :, bass.ds(r, 1)].rearrange("p k a -> p (k a)")).then_inc(sem["cur_r"], 1)
                if head:
                    if not is_first(i):
                        dve.wait_ge(sem["hg_y"], count("hg_y", i - 1))
                    dve.tensor_copy(cur_e, ev[:, :, i] if isinstance(i, int) else ev[:, :, bass.ds(i, 1)].rearrange("p k a -> p (k a)")).then_inc(sem["cur_e"], 1)
                    dve.wait_ge(sem["cur_e"], count("cur_e", i))
                if is_first(i):
                    dve.wait_ge(sem["lr_shift"], count("lr_shift", 0))
                    stt(lr, bank[0][:, :], mu_lr[:, 2:3], shift[:, 0:T], ALU.mult, ALU.add).then_inc(sem["free0"], 1)
                else:
                    gated(i, 0, "sig_gb", sig_a, g_b)
                if pair:
                    decay_sums(r)
                if head:
                    gated(i, 1, "sig_q", sig_b, hq)
                if is_first(i):
                    dve.wait_ge(masks_loaded, 16)
                    dve.tensor_copy(mask8[:, :], masks_in)
                if pair:
                    key_norm(r)
                if not head:
                    split_embedding(0)
                if pair:
                    operands(r)
                if head:
                    dve.wait_ge(sem["free0"], count("free0", i, 1))
                    if not is_first(i):
                        dve.wait_ge(sem["hg_sq"], count("hg_sq", i - 1))
                        dve.wait_ge(sem["hg_ssq"], count("hg_ssq", i - 1))
                    dve.tensor_scalar(hf, sig_a, cur_e[:, OLB:OLB + 1], cur_e[:, LB:LB + 1], ALU.mult, ALU.add).then_inc(sem["fk"], 1)
                    dve.tensor_scalar(hk, sig_b, cur_e[:, OLB:OLB + 1], None, ALU.mult).then_inc(sem["fk"], 1)
                    gated(i, 3, "sig_ga", sig_a, g_a)
                if is_first(i):
                    dve.memset(rw_m, 0.0).then_inc(sem["masks_set"], 1)
                    dve.wait_ge(sem["masks_set"], count("masks_set", 0))
                if pair:
                    matrices(r)
                if head:
                    level(i, 0)
                for lvl in range(1, 7):
                    if pair:
                        inverse(r, lvl)
                    if head and lvl <= 3:
                        level(i, lvl)
                if pair:
                    state(r, 0)
                if head:
                    mixed(i, 0, 5, wr)
                    masked(i, 0)
                    masked(i, 1)
                if pair:
                    state(r, 1)
                if not head:
                    output_low(2 * KC, 0, range(2 * KC), 0)
                    output_low(2 * KC, 0, range(2 * KC), 1)
                if head:
                    level(i, 4)
                    mixed(i, 1, 6, wk)
                    masked(i, 2)
                    level(i, 5)
                    masked(i, 3)
                if pair:
                    state(r, 2)
                if not head:
                    output_low(2 * KC, 0, range(2 * KC), 2)
                    output_low(2 * KC, 0, range(2 * KC), 3)
                if head:
                    mixed(i, 2, 7, wv)
                    level(i, 6)
                    masked(i, 4)
                    masked(i, 5)
                    level(i, 7)
                    masked(i, 6)
                    masked(i, 7)
                if pair:
                    pair_mean(r)
                if head:
                    states(i)
                if pair:
                    pair_out(r)
                if head:
                    head_out(i)

            even_round(0, pair=False)
            even_round(1)
            with dve.Fori(2, EV_ROUNDS) as i:
                even_round(i)
            even_round(EV_ROUNDS, head=False)

            def scaled(stage, c):
                dve.wait_ge(sem["x_added"], count("x_added", stage - 1, c))
                if c >= 2:
                    dve.wait_ge(sem["h_ready"], count("h_ready", stage, c - 2))
                dve.tensor_scalar(hn[:, c % 2, :], x[:, c, :], gain[:, stage, c:c + 1], None, ALU.mult).then_inc(sem["hn_ready"], 1)

            def add_outputs(stage, first_tile):
                for n in range(KC):
                    dve.wait_ge(sem["units_done"], first_tile + n + 1)
                    dve.tensor_tensor(x[:, n, :], x[:, n, :], bank[n], ALU.add).then_inc(sem["x_added"], 1)
                    if n < 4:
                        scaled(stage + 1, n)
                    if 1 <= n <= 4:
                        low_half(stage + 1, n - 1)
                    if n >= 2:
                        sum_squares(stage + 1, n - 1)
                for c in range(4, KC):
                    scaled(stage + 1, c)
                    if c == 4:
                        sum_squares(stage + 1, KC - 1)
                    low_half(stage + 1, c)

            def gates(stage, first_tile):
                def add(n):
                    dve.wait_ge(sem["gate_sig"], count("gate_sig", stage // 2, n))
                    dve.tensor_tensor(prj[:, n, :], prj[:, n, :], sg[:, n % 2, :], ALU.mult).then_inc(sem["gate_mul"], 1)
                    dve.wait_ge(sem["gate_mul"], count("gate_mul", stage // 2, n))
                    dve.tensor_tensor(x[:, n, :], x[:, n, :], prj[:, n, :], ALU.add).then_inc(sem["x_added"], 1)

                dve.wait_ge(sem["rstd"], count("rstd", stage))
                for n in range(KC):
                    if stage == 1 and n == 2:
                        split_embedding(1)
                    dve.wait_ge(sem["units_done"], first_tile + n + 1)
                    if n >= 2:
                        dve.wait_ge(sem["gate_mul"], count("gate_mul", stage // 2, n - 2))
                    dve.tensor_tensor(sg[:, n % 2, :], bank[(n + 1) % 8], rstd_s, ALU.mult).then_inc(sem["gate_z"], 1)
                    if n:
                        add(n - 1)
                    if 3 <= n < KC - 1:
                        sum_squares(stage + 1, n - 2)
                add(KC - 1)
                for c in range(KC - 3, KC):
                    sum_squares(stage + 1, c)

            for c in range(4, 2 * KC):
                output_low(2 * KC, 0, range(2 * KC), c)
            dve.wait_ge(x_again, 16)
            add_outputs(0, U_GAT0 - KC)
            gates(1, U_GAT0 + 8)
            normed(2, 2, hn)
            dve.memset(mq[64:P, 0, :], 0.0)
            dve.memset(mq[0:64, 1, :], 0.0)
            dve.memset(xd[:, :, 0:3], 0.0).then_inc(sem["conv_pad"], 1)

            def attend(i, n):
                w = (n % CH + 1) * L
                qt = n % CH
                dve.wait_ge(sem["mo_s"], count("mo_s", i, n))
                masked_copy(bank[2 + n % 2][:, qt * L:(qt + 1) * L], m4_mask[:, 0, 0, :], causal).then_inc(sem["mo_mask"], 1)
                dve.wait_ge(sem["mo_mask"], count("mo_mask", i, n))
                dve.reduce_max(m_stat[:, 0, n:n + 1], bank[2 + n % 2][:, 0:w], axis=mybir.AxisListType.X).then_inc(sem["mo_max"], 1)
                dve.wait_ge(sem["mo_max"], count("mo_max", i, n))
                dve.tensor_scalar(m_stat[:, 1, n:n + 1], m_stat[:, 0, n:n + 1], -0.125, None, ALU.mult).then_inc(sem["mo_neg"], 1)

            def normalise(i, n):
                w = (n % CH + 1) * L
                dve.wait_ge(sem["mo_exp"], count("mo_exp", i, n))
                dve.reciprocal(m_stat[:, 2, n:n + 1], m_sum[:, n:n + 1]).then_inc(sem["mo_inv"], 1)
                dve.wait_ge(sem["mo_inv"], count("mo_inv", i, n))
                dve.tensor_scalar(prob[:, n % 2, 0:w], prob[:, n % 2, 0:w], m_stat[:, 2, n:n + 1], None, ALU.mult).then_inc(sem["mo_p"], 1)

            def convolve(i, b, k):
                if k == 0:
                    dve.wait_ge(sem["conv_pad"], count("conv_pad", 0))
                    dve.wait_ge(sem["ofree0"], count("ofree0", i, 2 * b))
                    if not is_first(i):
                        dve.wait_ge(sem["ru_ix"], count("ru_ix", i - 1, b))
                    dve.tensor_scalar(xc[:, b, :], xd[:, b, 0:T], cur_o[:, CW0, b:b + 1], cur_o[:, CONV_B, b:b + 1], ALU.mult,
                                      ALU.add).then_inc(sem["ru_conv"], 1)
                else:
                    dve.wait_ge(sem["ru_conv"], count("ru_conv", i, 4 * b + k - 1))
                    stt(xc[:, b, :], xd[:, b, k:k + T], cur_o[:, CW0 + k, b:b + 1], xc[:, b, :], ALU.mult, ALU.add).then_inc(sem["ru_conv"], 1)

            def gate_tile(i, n, j):
                tile_done(i, j, U_ODD)
                dve.tensor_copy(og[:, n, :], bank[j % 2][:, :]).then_inc(sem[f"ofree{j % 2}"], 1)

            def gate(i, n):
                dve.wait_ge(sem["o_sig"], count("o_sig", i, n))
                dve.tensor_tensor(og[:, n, :], og[:, n, :], osig[:, n, :], ALU.mult).then_inc(sem["o_gate"], 1)

            def row(base, r, step=1):
                return y[:, base + r * step, :] if isinstance(r, int) else y[:, bass.ds(r * step + base, 1), :].rearrange("p a t -> p (a t)")

            def lru_differences(r):
                for b in range(2):
                    dve.wait_ge(sem["ru_u2"], count("ru_u2", r, b))
                    dve.tensor_tensor(u_2[b], u_2[b], u_1[b], ALU.subtract).then_inc(sem["ru_d"], 1)

            def lru_states(r):
                for b in range(2):
                    dve.wait_ge(sem["ru_e"], count("ru_e", r, b))
                    dve.tensor_tensor(u_2[b], u_2[b], u_i[b], ALU.mult).then_inc(sem["ru_b"], 1)
                    dve.wait_ge(sem["ru_b"], count("ru_b", r, b))
                    dve.tensor_tensor_scan(out=u_th[b], data0=u_r[b], data1=u_2[b], initial=0.0, op0=ALU.mult,
                                           op1=ALU.add).then_inc(sem["ru_h"], 1)
                    dve.wait_ge(sem["ru_h"], count("ru_h", r, b))
                    dve.wait_ge(sem["o_gate"], count("o_gate", r, 1 + b))
                    dve.tensor_tensor(row(4 + b, r, 2), u_th[b], og[:, 1 + b, :], ALU.mult).then_inc(sem["ru_y"], 1)

            def odd_round(i, last=False):
                if not is_first(i):
                    dve.wait_ge(sem["ru_th"], count("ru_th", i - 1, 1))
                dve.tensor_copy(cur_o, od[:, :, bass.ds(i * 2, 2)]).then_inc(sem["cur_o"], 1)
                dve.wait_ge(sem["cur_o"], count("cur_o", i))
                for k in range(4):
                    convolve(i, 0, k)
                if not is_first(i):
                    lru_differences(i - 1)
                tile_done(i, 2, U_ODD)
                dve.tensor_copy(mk, bank[0][:, :]).then_inc(sem["ofree0"], 1)
                if not is_first(i):
                    lru_states(i - 1)
                    dve.wait_ge(sem["ru_a"], count("ru_a", i - 1, 1))
                    dve.wait_ge(sem["ru_y"], count("ru_y", i - 1, 1))
                dve.tensor_copy(cneg, cur_o[:, CNEG, :]).then_inc(sem["cneg_set"], 1)
                attend(i, 0)
                attend(i, 1)
                for n in range(2 * CH):
                    normalise(i, n)
                    if n + 2 < 2 * CH:
                        attend(i, n + 2)
                    if 2 <= n < 6:
                        convolve(i, 1, n - 2)
                    if n == 3:
                        gate_tile(i, 0, 5)
                    if n == 5:
                        gate_tile(i, 1, 6)
                gate_tile(i, 2, 7)
                for b in range(2):
                    dve.wait_ge(sem["ru_i"], count("ru_i", i, b))
                    dve.tensor_tensor(u_i[b], u_i[b], xc[:, b, :], ALU.mult).then_inc(sem["ru_ix"], 1)
                for b in range(2):
                    dve.wait_ge(sem["ru_th"], count("ru_th", i, b))
                    dve.tensor_scalar(u_2[b], u_th[b], float(2.0 ** -103), float(2.0 ** 41), ALU.max, ALU.mult).then_inc(sem["ru_clamp"], 1)
                if last:
                    output_low(4 + KC, 2 * KC, ODD_OUTPUTS, 0)
                gate(i, 0)
                dve.wait_ge(sem["mo_pv"], count("mo_pv", i, 7))
                dve.wait_ge(sem["o_gate"], count("o_gate", i, 0))
                dve.tensor_tensor(row(0, i), bank[5][:, :], og[:, 0, :], ALU.mult).then_inc(sem["mo_y"], 1)
                gate(i, 1)
                gate(i, 2)
            odd_round(0)
            with dve.Fori(1, OD_ROUNDS - 1) as i:
                odd_round(i)
            odd_round(OD_ROUNDS - 1, last=True)
            for c in range(1, 3):
                output_low(4 + KC, 2 * KC, ODD_OUTPUTS, c)
            lru_differences(OD_ROUNDS - 1)
            lru_states(OD_ROUNDS - 1)
            for c in range(3, 4 + KC):
                output_low(4 + KC, 2 * KC, ODD_OUTPUTS, c)
            add_outputs(2, U_GAT1 - KC)
            gates(3, U_GAT1 + 8)
            normed(4, 4, prj)


def kernel(**inputs):
    import concourse.bacc as bacc
    from concourse.bass_utils import run_bass_kernel_spmd as run

    a = {n: np.asarray(v) for n, v in inputs.items()}

    def units(w):
        k, n = w.shape
        return w.reshape(k // P, P, n // P, P).transpose(0, 2, 1, 3)

    def pack(blocks):
        b = np.stack(blocks)
        return b.reshape(-1, 4, P, P).transpose(0, 2, 1, 3).reshape(-1, P, 4 * P)

    def column_tiles(w, tiles):
        u = units(w)
        return pack([u[k, n] for n in tiles for k in range(KC)])

    w_in = a["ev_w_in"][0]
    za, zr, gates = 0, 24, 49
    order = [zr + 24]
    for i in range(EV_ROUNDS + 1):
        if i:
            order.append(gates + 8 + i - 1)
        if i < EV_ROUNDS:
            order += [za + i, za + 8 + i, gates + i, za + 16 + i, zr + i, zr + 8 + i, zr + 16 + i]
    od_order = []
    for i in range(OD_ROUNDS):
        od_order += [12 + 2 * i, i, 4 + i, 8 + i, 13 + 2 * i, 20 + i, 24 + 2 * i, 25 + 2 * i]

    def rows(w, order=None):
        u = units(w)
        order = list(range(u.shape[0])) if order is None else list(order)
        tiles = range(u.shape[1])
        return pack([u[k, n] for k in order[:-4] for n in tiles] + [u[k, n] for n in tiles for k in order[-4:]])

    def by_output(w):
        u = units(w)
        return pack([u[k, n] for n in range(u.shape[1]) for k in range(u.shape[0])])

    wall = np.concatenate([
        column_tiles(w_in, order), by_output(a["ple_proj"][0]), rows(a["ev_w_out"][0]), rows(a["ple_gate"][0]),
        by_output(a["ple_proj"][1]),
        column_tiles(a["od_w_in"][0], od_order), rows(a["od_w_out"][0], ODD_OUTPUTS),
        rows(a["ple_gate"][1]),
    ])
    assert wall.shape[0] == N_UNITS

    def cols(v):
        return v.reshape(-1, P).T

    mu = a["rw_mu"][0]
    par_e = np.zeros((P, N_EV + 1, 8), np.float32)
    for n, v in enumerate((mu[0:1024], mu[1024:2048], mu[2048:3072], a["rw_w0"][0], a["rw_a0"][0], a["rw_k_k"][0],
                           a["rw_k_a"][0], a["rw_r_k"][0], a["rw_ln_g"][0], a["rw_ln_b"][0], a["hg_lb_logits"][0],
                           a["hg_norm"][0])):
        par_e[:, n, :] = cols(v)
    par_e[:, N_EV, 0] = mu[3072:]
    par_o = np.zeros((P, N_OD, 8), np.float32)
    for n, v in enumerate((*a["lru_conv_w"][0], a["lru_conv_b"][0], a["lru_ba"][0], a["lru_bx"][0], a["lru_lambda"][0])):
        par_o[:, n, :] = cols(v)
    gains = np.stack([cols(v) for v in (a["ev_norm"][0], a["ple_norm"][0], a["od_norm"][0], a["ple_norm"][1],
                                        a["final_norm"])], axis=1)
    w2a2 = np.concatenate([a["rw_w2"][0], a["rw_a2"][0]]).reshape(P, 8, P).transpose(1, 0, 2)
    lru_w = np.stack([a["lru_wa"][0], a["lru_wx"][0]], axis=1).reshape(OD_ROUNDS, 4, P, P).transpose(0, 2, 1, 3)

    t = np.arange(P)
    m8 = np.zeros((P, N_MASK), np.float32)
    for lvl in range(LEVELS):
        m = 1 << lvl
        blocks = t.reshape(-1, 2, m)
        even, odd = blocks[:, 0].ravel(), blocks[:, 1].ravel()
        pairs = (t[:, None] // (2 * m) == odd[None] // (2 * m)) & (t[:, None] % (2 * m) < m)
        m8[:, lvl * 256:(lvl + 1) * 256] = np.tile(pairs, (1, 4))
        if lvl < 6:
            pairs = (t[:, None] // (2 * m) == even[None] // (2 * m)) & (t[:, None] % (2 * m) >= m)
            m8[:, 2816 + lvl * P:2816 + (lvl + 1) * P] = np.tile(pairs, (1, 2))
    m8[:, 1792:2304] = np.tile(np.eye(P), (1, 4))
    before, upto = t[:, None] < t[None], t[:, None] <= t[None]
    m8[:, 2304:2816] = np.concatenate([before, upto, before, upto], axis=1)
    fc = np.zeros((P, 4, P), np.float32)
    fc[:, 0] = np.eye(P)
    fc[:, 1] = 1.0
    fc[:, 2] = t[:, None] // 64 == t[None] // 64
    fc[:, 3] = np.where(t[:, None] < t[None], -1e30, 0.0)

    arrays = {
        "xT": a["x"][0].T.reshape(KC, P, T).transpose(1, 0, 2),
        "pT": a["p"][:, 0].transpose(0, 2, 1).reshape(2, 2, P, T).transpose(0, 2, 1, 3),
        "wall": wall, "par_e": par_e, "par_o": par_o, "gains": gains, "w2a2": w2a2, "lru_w": lru_w,
        "mask_f32": m8, "const_f32": fc,
    }
    arrays = {n: np.ascontiguousarray(v) for n, v in arrays.items()}
    nc = bacc.Bacc("TRN2", target_bir_lowering=False, num_devices=1)
    d = {n: nc.dram_tensor(n, v.shape, mybir.dt.from_np(v.dtype), kind="ExternalInput").ap() for n, v in arrays.items()}
    out = nc.dram_tensor("out", (P, KC, T), F32, kind="ExternalOutput").ap()
    trunk(nc, d["xT"], d["pT"], d["wall"], d["par_e"], d["par_o"], d["gains"], d["w2a2"], d["lru_w"],
          (d["mask_f32"], d["const_f32"]), out)
    r = run(nc, [arrays], core_ids=[0])
    return r.results[0]["out"].transpose(1, 0, 2).reshape(D, T).T.reshape(1, T, D)
```
